# Optimizing a Trainium2 kernel written in Bass

```python
import math
import jax, jax.numpy as jnp
from jax import lax
import numpy as np

D_MODEL = 2048
BATCH = 1
SEQ = 256
DEPTH = 1

HEAD_DIM = 64
MIX_WIDTH = D_MODEL
SWA_WIDTH = 3 * MIX_WIDTH // 8
SWA_HEADS = SWA_WIDTH // HEAD_DIM
SWA_KV_HEADS = SWA_HEADS // 3
SWA_GROUP = SWA_HEADS // SWA_KV_HEADS
WINDOW = 128
SWA_BLOCK = 128
REL_BUCKETS = 32
REL_MAX_DIST = 128
GLA_WIDTH = 3 * MIX_WIDTH // 8
GLA_HEADS = 4
GLA_DV = GLA_WIDTH // GLA_HEADS
GLA_DK = GLA_DV // 2
GLA_LOWRANK = 16
GLA_CHUNK = 64
GATE_NORMALIZER = 16.0
GATE_LOG_MIN = -1.0
SB_WIDTH = MIX_WIDTH - SWA_WIDTH - GLA_WIDTH
SB_HEADS = SB_WIDTH // HEAD_DIM
SB_BLOCK = 128
D_FF = 4 * D_MODEL
RMS_EPS = 1e-6
NEG_INF = -1e30

PROJ_SIZES = (
    SWA_WIDTH, SWA_KV_HEADS * HEAD_DIM, SWA_KV_HEADS * HEAD_DIM,
    GLA_HEADS * GLA_DK, GLA_HEADS * GLA_DK, GLA_WIDTH, GLA_WIDTH, GLA_LOWRANK,
    SB_WIDTH, SB_WIDTH, SB_WIDTH,
)
PROJ_WIDTH = sum(PROJ_SIZES)


def rmsnorm(x, gain, eps=RMS_EPS):
    xf = x.astype(jnp.float32)
    y = xf * lax.rsqrt(jnp.mean(xf * xf, axis=-1, keepdims=True) + eps)
    return (y * gain.astype(jnp.float32)).astype(x.dtype)

def t5_causal_bucket(dist):
    max_exact = REL_BUCKETS // 2
    is_small = dist < max_exact
    ratio = jnp.log(jnp.maximum(dist, 1).astype(jnp.float32) / max_exact) / math.log(REL_MAX_DIST / max_exact)
    large = max_exact + (ratio * (REL_BUCKETS - max_exact)).astype(jnp.int32)
    large = jnp.minimum(large, REL_BUCKETS - 1)
    return jnp.where(is_small, dist, large)

def swa_sink_attention(q, k, v, sinks, rel_bias):
    B, S = q.shape[:2]
    nb = S // SWA_BLOCK
    qb = q.reshape(B, nb, SWA_BLOCK, SWA_KV_HEADS, SWA_GROUP, HEAD_DIM)
    kb = k.reshape(B, nb, SWA_BLOCK, SWA_KV_HEADS, HEAD_DIM)
    vb = v.reshape(B, nb, SWA_BLOCK, SWA_KV_HEADS, HEAD_DIM)
    pad = ((0, 0), (1, 0), (0, 0), (0, 0), (0, 0))
    kw = jnp.concatenate([jnp.pad(kb, pad)[:, :-1], kb], axis=2)
    vw = jnp.concatenate([jnp.pad(vb, pad)[:, :-1], vb], axis=2)
    logits = jnp.einsum('bnqhgd,bnkhd->bnhgqk', qb, kw).astype(jnp.float32) * (HEAD_DIM ** -0.5)
    qpos = jnp.arange(SWA_BLOCK) + SWA_BLOCK
    kpos = jnp.arange(2 * SWA_BLOCK)
    dist = qpos[:, None] - kpos[None, :]
    in_window = (dist >= 0) & (dist < WINDOW)
    key_abs = jnp.arange(nb)[:, None] * SWA_BLOCK - SWA_BLOCK + kpos[None, :]
    mask = in_window[None, :, :] & (key_abs >= 0)[:, None, :]
    bias = rel_bias.astype(jnp.float32)[t5_causal_bucket(jnp.maximum(dist, 0))]
    bias = bias.transpose(2, 0, 1).reshape(SWA_KV_HEADS, SWA_GROUP, SWA_BLOCK, 2 * SWA_BLOCK)
    logits = jnp.where(mask[None, :, None, None], logits + bias[None, None], NEG_INF)
    sink_col = jnp.broadcast_to(
        sinks.astype(jnp.float32).reshape(1, 1, SWA_KV_HEADS, SWA_GROUP, 1, 1),
        logits.shape[:-1] + (1,))
    probs = jax.nn.softmax(jnp.concatenate([logits, sink_col], axis=-1), axis=-1)[..., :-1]
    out = jnp.einsum('bnhgqk,bnkhd->bnqhgd', probs.astype(v.dtype), vw)
    return out.reshape(B, S, SWA_HEADS * HEAD_DIM)

def gla_chunked(q, k, v, log_gate):
    B, S, H, dk = q.shape
    dv = v.shape[-1]
    n = S // GLA_CHUNK
    f32 = jnp.float32
    q = (q.astype(f32) * dk ** -0.5).reshape(B, n, GLA_CHUNK, H, dk)
    k = k.astype(f32).reshape(B, n, GLA_CHUNK, H, dk)
    v = v.astype(f32).reshape(B, n, GLA_CHUNK, H, dv)
    b = jnp.cumsum(log_gate.reshape(B, n, GLA_CHUNK, H, dk), axis=2)
    b_last = b[:, :, -1:]
    q_dec = q * jnp.exp(b)
    k_inv = k * jnp.exp(-b)
    k_end = k * jnp.exp(b_last - b)
    causal = jnp.tril(jnp.ones((GLA_CHUNK, GLA_CHUNK), dtype=bool))
    scores = jnp.where(causal, jnp.einsum('bnthk,bnshk->bnhts', q_dec, k_inv), 0.0)
    o_intra = jnp.einsum('bnhts,bnshv->bnthv', scores, v)
    d_state = jnp.einsum('bnshk,bnshv->bnhkv', k_end, v)
    decay = jnp.exp(b_last[:, :, 0])

    def step(state, inp):
        dec, ds = inp
        return dec[..., None] * state + ds, state

    init = jnp.zeros((B, H, dk, dv), f32)
    _, s_prev = lax.scan(step, init, (decay.swapaxes(0, 1), d_state.swapaxes(0, 1)))
    s_prev = s_prev.swapaxes(0, 1)
    o_inter = jnp.einsum('bnthk,bnhkv->bnthv', q_dec, s_prev)
    return (o_intra + o_inter).reshape(B, S, H, dv)

def stick_breaking_attention(q, k, v):
    B, S, H, D = q.shape
    nb = S // SB_BLOCK
    qb = q.reshape(B, nb, SB_BLOCK, H, D).swapaxes(0, 1)
    kpos = jnp.arange(S)
    scale = D ** -0.5

    def block(args):
        q_blk, i = args
        z = jnp.einsum('bqhd,bshd->bhqs', q_blk, k).astype(jnp.float32) * scale
        qpos = i * SB_BLOCK + jnp.arange(SB_BLOCK)
        strict = kpos[None, :] < qpos[:, None]
        log_beta = jax.nn.log_sigmoid(z)
        log_1m_beta = jnp.where(strict, jax.nn.log_sigmoid(-z), 0.0)
        between = lax.cumsum(log_1m_beta, axis=3, reverse=True) - log_1m_beta
        w = jnp.where(strict, jnp.exp(log_beta + between), 0.0)
        return jnp.einsum('bhqs,bshd->bqhd', w.astype(v.dtype), v)

    out = lax.map(block, (qb, jnp.arange(nb)))
    return out.swapaxes(0, 1).reshape(B, S, H * D)

def token_mixing(h, w_in, sinks, rel_bias, gla_gate_w, gla_gate_b, gla_norm,
                 swa_out_norm, sb_out_norm, w_out):
    B, S, _ = h.shape
    proj = h @ w_in
    split_at = np.cumsum(PROJ_SIZES)[:-1].tolist()
    aq, ak, av, bq, bk, bv, br, blr, cq, ck, cv = jnp.split(proj, split_at, axis=-1)
    out_a = swa_sink_attention(
        aq.reshape(B, S, SWA_HEADS, HEAD_DIM),
        ak.reshape(B, S, SWA_KV_HEADS, HEAD_DIM),
        av.reshape(B, S, SWA_KV_HEADS, HEAD_DIM), sinks, rel_bias)
    out_a = rmsnorm(out_a, swa_out_norm)
    gate_pre = (blr @ gla_gate_w + gla_gate_b).astype(jnp.float32)
    log_gate = jnp.maximum(jax.nn.log_sigmoid(gate_pre) / GATE_NORMALIZER, GATE_LOG_MIN)
    o_b = gla_chunked(
        bq.reshape(B, S, GLA_HEADS, GLA_DK),
        bk.reshape(B, S, GLA_HEADS, GLA_DK),
        bv.reshape(B, S, GLA_HEADS, GLA_DV),
        log_gate.reshape(B, S, GLA_HEADS, GLA_DK))
    o_b = rmsnorm(o_b, gla_norm).reshape(B, S, GLA_WIDTH).astype(h.dtype)
    out_b = o_b * jax.nn.silu(br)
    out_c = stick_breaking_attention(
        cq.reshape(B, S, SB_HEADS, HEAD_DIM),
        ck.reshape(B, S, SB_HEADS, HEAD_DIM),
        cv.reshape(B, S, SB_HEADS, HEAD_DIM))
    out_c = rmsnorm(out_c, sb_out_norm)
    mixed = jnp.concatenate([out_a, out_b, out_c], axis=-1)
    return mixed @ w_out

def squared_relu_mlp(h, w1, w2):
    return jnp.square(jax.nn.relu(h @ w1)) @ w2

def first_inputs(seed: int = 0) -> dict:
    key = jax.random.key(seed)
    ks = jax.random.split(key, 15)
    f32 = jnp.float32

    def nrm(k, shape, scale):
        return jax.random.normal(k, shape, f32) * scale

    def gain(k, shape):
        return 1.0 + 0.05 * jax.random.normal(k, shape, f32)

    return {
        'x': nrm(ks[0], (BATCH, SEQ, D_MODEL), 1.0),
        'norm_mix': gain(ks[1], (DEPTH, D_MODEL)),
        'w_in': nrm(ks[2], (DEPTH, D_MODEL, PROJ_WIDTH), D_MODEL ** -0.5),
        'swa_sinks': nrm(ks[3], (DEPTH, SWA_HEADS), 0.5),
        'rel_bias': nrm(ks[4], (REL_BUCKETS, SWA_HEADS), 0.5),
        'gla_gate_w': nrm(ks[5], (DEPTH, GLA_LOWRANK, GLA_HEADS * GLA_DK), GLA_LOWRANK ** -0.5),
        'gla_gate_b': nrm(ks[6], (DEPTH, GLA_HEADS * GLA_DK), 0.1),
        'gla_norm': gain(ks[7], (DEPTH, GLA_DV)),
        'swa_out_norm': gain(ks[8], (DEPTH, SWA_WIDTH)),
        'sb_out_norm': gain(ks[9], (DEPTH, SB_WIDTH)),
        'w_out': nrm(ks[10], (DEPTH, MIX_WIDTH, D_MODEL), MIX_WIDTH ** -0.5),
        'norm_mlp': gain(ks[11], (DEPTH, D_MODEL)),
        'w_mlp_in': nrm(ks[12], (DEPTH, D_MODEL, D_FF), D_MODEL ** -0.5),
        'w_mlp_out': nrm(ks[13], (DEPTH, D_FF, D_MODEL), D_FF ** -0.5),
        'norm_final': gain(ks[14], (D_MODEL,)),
    }

def first_block(x, norm_mix, w_in, swa_sinks, rel_bias, gla_gate_w, gla_gate_b, gla_norm,
              swa_out_norm, sb_out_norm, w_out, norm_mlp, w_mlp_in, w_mlp_out, norm_final):
    for l in range(DEPTH):
        h = rmsnorm(x, norm_mix[l])
        x = x + token_mixing(h, w_in[l], swa_sinks[l], rel_bias, gla_gate_w[l], gla_gate_b[l],
                             gla_norm[l], swa_out_norm[l], sb_out_norm[l], w_out[l])
        h = rmsnorm(x, norm_mlp[l])
        x = x + squared_relu_mlp(h, w_mlp_in[l], w_mlp_out[l])
    return rmsnorm(x, norm_final)


CTX_LEN = 256
GRID_W = 64
N_MIXERS = 3
MIXER_NA = 0
MIXER_GMLP = 1
MIXER_CONV = 2
NA_HEADS = 16
HEAD_DIM_2 = D_MODEL // NA_HEADS
WIN_H = 8
WIN_W = 16
QROWS = 2
GM_WIDTH = 2 * D_MODEL
GM_GROUPS = 16
GM_GROUP_DIM = GM_WIDTH // GM_GROUPS
GM_CHUNK = 128
FFN_DIM = 5504
N_MOD = 6
EPS = 1e-6


def rms_norm(x, g):
    x32 = x.astype(jnp.float32)
    y = x32 * lax.rsqrt(jnp.mean(x32 * x32, axis=-1, keepdims=True) + EPS)
    return (y * g.astype(jnp.float32)).astype(x.dtype)

def adaln(cond, w, b):
    return jnp.split(jax.nn.silu(cond) @ w + b, N_MOD, axis=-1)

def modulate(x, shift, scale):
    return x * (1.0 + scale) + shift

def dwconv3(z, w, b=None):
    zp = jnp.pad(z, ((0, 0), (1, 1), (0, 0)))
    y = zp[:, :-2] * w[0] + zp[:, 1:-1] * w[1] + zp[:, 2:] * w[2]
    return y if b is None else y + b

def neighbourhood_attention(h, hc, w_qkv, q_g, k_g, rpb, w_o, ctx_out):
    bn, n, d = h.shape
    rows = n // GRID_W
    kh = min(WIN_H, rows)
    nb = min(kh + QROWS - 1, rows)
    n_blk = rows // QROWS
    qw = QROWS * GRID_W
    nk = nb * GRID_W
    scale = HEAD_DIM_2 ** -0.5

    def project(t):
        q, k, v = jnp.split(t @ w_qkv, 3, axis=-1)
        sh = (t.shape[0], t.shape[1], NA_HEADS, HEAD_DIM_2)
        return rms_norm(q.reshape(sh), q_g), rms_norm(k.reshape(sh), k_g), v.reshape(sh)

    q, k, v = project(h)
    qc, kc, vc = project(hc)
    kg = k.reshape(bn, rows, GRID_W, NA_HEADS, HEAD_DIM_2)
    vg = v.reshape(bn, rows, GRID_W, NA_HEADS, HEAD_DIM_2)

    q_row_off = jnp.repeat(jnp.arange(QROWS), GRID_W)
    q_col = jnp.tile(jnp.arange(GRID_W), QROWS)
    k_row_off = jnp.repeat(jnp.arange(nb), GRID_W)
    k_col = jnp.tile(jnp.arange(GRID_W), nb)
    c_start = jnp.clip(q_col - WIN_W // 2, 0, GRID_W - WIN_W)
    col_ok = (k_col[None, :] >= c_start[:, None]) & (k_col[None, :] < c_start[:, None] + WIN_W)
    dc_idx = jnp.clip(k_col[None, :] - q_col[:, None], -(WIN_W - 1), WIN_W - 1) + WIN_W - 1

    def block(args):
        blk, qb = args
        r0 = blk * QROWS
        q_row = r0 + q_row_off
        r_start = jnp.clip(q_row - kh // 2, 0, rows - kh)
        band0 = jnp.minimum(jnp.clip(r0 - kh // 2, 0, rows - kh), rows - nb)
        k_row = band0 + k_row_off
        kb = lax.dynamic_slice_in_dim(kg, band0, nb, axis=1).reshape(bn, nk, NA_HEADS, HEAD_DIM_2)
        vb = lax.dynamic_slice_in_dim(vg, band0, nb, axis=1).reshape(bn, nk, NA_HEADS, HEAD_DIM_2)
        ok = col_ok & (k_row[None, :] >= r_start[:, None]) & (k_row[None, :] < r_start[:, None] + kh)
        dr_idx = jnp.clip(k_row[None, :] - q_row[:, None], -(WIN_H - 1), WIN_H - 1) + WIN_H - 1
        bias = rpb[:, dr_idx, dc_idx].astype(jnp.float32)
        s_lat = jnp.einsum('bqhd,bkhd->bhqk', qb, kb).astype(jnp.float32) * scale + bias
        s_lat = jnp.where(ok, s_lat, -jnp.inf)
        s_ctx = jnp.einsum('bqhd,bchd->bhqc', qb, kc).astype(jnp.float32) * scale
        p = jax.nn.softmax(jnp.concatenate([s_lat, s_ctx], axis=-1), axis=-1).astype(vb.dtype)
        return (jnp.einsum('bhqk,bkhd->bqhd', p[..., :nk], vb)
                + jnp.einsum('bhqc,bchd->bqhd', p[..., nk:], vc))

    q_blocks = q.reshape(bn, n_blk, qw, NA_HEADS, HEAD_DIM_2).transpose(1, 0, 2, 3, 4)
    o = lax.map(block, (jnp.arange(n_blk), q_blocks))
    y = o.transpose(1, 0, 2, 3, 4).reshape(bn, n, d) @ w_o
    yc = None
    if ctx_out:
        s = jnp.einsum('bqhd,bkhd->bhqk', qc, kc).astype(jnp.float32) * scale
        p = jax.nn.softmax(s, axis=-1).astype(vc.dtype)
        yc = jnp.einsum('bhqk,bkhd->bqhd', p, vc).reshape(bn, hc.shape[1], d) @ w_o
    return y, yc

def chunk_gmlp(h, w_in, v_g, w_s, b_s, w_out):
    bn, n, _ = h.shape
    u, v = jnp.split(jax.nn.gelu(h @ w_in), 2, axis=-1)
    v = rms_norm(v, v_g)
    vch = v.reshape(bn, n // GM_CHUNK, GM_CHUNK, GM_GROUPS, GM_GROUP_DIM)
    sv = jnp.einsum('gij,bnjgd->bnigd', w_s, vch) + b_s.T[None, None, :, :, None]
    return (u * sv.reshape(bn, n, GM_WIDTH)) @ w_out

def short_conv(h, w_in, conv_w, w_out):
    b_gate, c_gate, xv = jnp.split(h @ w_in, 3, axis=-1)
    return (b_gate * dwconv3(c_gate * xv, conv_w)) @ w_out

def conv_ffn(h, w_up, conv_w, conv_b, w_down):
    gate, up = jnp.split(dwconv3(h @ w_up, conv_w, conv_b), 2, axis=-1)
    return (jax.nn.silu(gate) * up) @ w_down

def second_inputs(seed: int = 0) -> dict:
    key = jax.random.key(seed)
    keys = iter(jax.random.split(key, 40))

    def nrm(shape, s):
        return jax.random.normal(next(keys), shape, jnp.float32) * s

    d = D_MODEL
    n_na = len(range(MIXER_NA, DEPTH, N_MIXERS))
    n_gm = len(range(MIXER_GMLP, DEPTH, N_MIXERS))
    n_sc = len(range(MIXER_CONV, DEPTH, N_MIXERS))
    return {
        'x': nrm((BATCH, SEQ, d), 1.0),
        'c': nrm((BATCH, d), 1.0),
        'ctx': nrm((BATCH, CTX_LEN, d), 1.0),
        'c_ctx': nrm((d,), 1.0),
        'norm_mix_g': 1.0 + nrm((DEPTH, d), 0.1),
        'norm_ffn_g': 1.0 + nrm((DEPTH, d), 0.1),
        'w_ada': nrm((DEPTH, d, N_MOD * d), 0.5 * d ** -0.5),
        'b_ada': nrm((DEPTH, N_MOD * d), 0.02),
        'na_w_qkv': nrm((n_na, d, 3 * d), d ** -0.5),
        'na_q_g': 1.0 + nrm((n_na, HEAD_DIM_2), 0.1),
        'na_k_g': 1.0 + nrm((n_na, HEAD_DIM_2), 0.1),
        'na_rpb': nrm((n_na, NA_HEADS, 2 * WIN_H - 1, 2 * WIN_W - 1), 0.2),
        'na_w_o': nrm((n_na, d, d), d ** -0.5),
        'gm_w_in': nrm((n_gm, d, 2 * GM_WIDTH), d ** -0.5),
        'gm_v_g': 1.0 + nrm((n_gm, GM_WIDTH), 0.1),
        'gm_w_s': nrm((n_gm, GM_GROUPS, GM_CHUNK, GM_CHUNK), GM_CHUNK ** -0.5),
        'gm_b_s': 1.0 + nrm((n_gm, GM_GROUPS, GM_CHUNK), 0.1),
        'gm_w_out': nrm((n_gm, GM_WIDTH, d), GM_WIDTH ** -0.5),
        'sc_w_in': nrm((n_sc, d, 3 * d), d ** -0.5),
        'sc_conv_w': nrm((n_sc, 3, d), 3 ** -0.5),
        'sc_w_out': nrm((n_sc, d, d), d ** -0.5),
        'ffn_w_up': nrm((DEPTH, d, 2 * FFN_DIM), d ** -0.5),
        'ffn_conv_w': nrm((DEPTH, 3, 2 * FFN_DIM), 3 ** -0.5),
        'ffn_conv_b': nrm((DEPTH, 2 * FFN_DIM), 0.02),
        'ffn_w_down': nrm((DEPTH, FFN_DIM, d), FFN_DIM ** -0.5),
    }

def second_block(x, c, ctx, c_ctx, norm_mix_g, norm_ffn_g, w_ada, b_ada,
              na_w_qkv, na_q_g, na_k_g, na_rpb, na_w_o,
              gm_w_in, gm_v_g, gm_w_s, gm_b_s, gm_w_out,
              sc_w_in, sc_conv_w, sc_w_out,
              ffn_w_up, ffn_conv_w, ffn_conv_b, ffn_w_down):
    cond_lat = c[:, None, :]
    cond_ctx = c_ctx[None, None, :]
    for i in range(DEPTH):
        last = i == DEPTH - 1
        m, j = i % N_MIXERS, i // N_MIXERS
        sh1, sc1, g1, sh2, sc2, g2 = adaln(cond_lat, w_ada[i], b_ada[i])
        h = modulate(rms_norm(x, norm_mix_g[i]), sh1, sc1)
        hc = None
        if (not last) or m == MIXER_NA:
            csh1, csc1, cg1, csh2, csc2, cg2 = adaln(cond_ctx, w_ada[i], b_ada[i])
            hc = modulate(rms_norm(ctx, norm_mix_g[i]), csh1, csc1)
        if m == MIXER_NA:
            y, yc = neighbourhood_attention(h, hc, na_w_qkv[j], na_q_g[j], na_k_g[j],
                                            na_rpb[j], na_w_o[j], not last)
        elif m == MIXER_GMLP:
            y = chunk_gmlp(h, gm_w_in[j], gm_v_g[j], gm_w_s[j], gm_b_s[j], gm_w_out[j])
            yc = None if last else chunk_gmlp(hc, gm_w_in[j], gm_v_g[j], gm_w_s[j], gm_b_s[j], gm_w_out[j])
        else:
            y = short_conv(h, sc_w_in[j], sc_conv_w[j], sc_w_out[j])
            yc = None if last else short_conv(hc, sc_w_in[j], sc_conv_w[j], sc_w_out[j])
        x = x + g1 * y
        hf = modulate(rms_norm(x, norm_ffn_g[i]), sh2, sc2)
        x = x + g2 * conv_ffn(hf, ffn_w_up[i], ffn_conv_w[i], ffn_conv_b[i], ffn_w_down[i])
        if not last:
            ctx = ctx + cg1 * yc
            hcf = modulate(rms_norm(ctx, norm_ffn_g[i]), csh2, csc2)
            ctx = ctx + cg2 * conv_ffn(hcf, ffn_w_up[i], ffn_conv_w[i], ffn_conv_b[i], ffn_w_down[i])
    return x


def setup_inputs(seed=0):
    out = dict(first_inputs(seed))
    for name, value in second_inputs(seed + 1).items():
        if name != "x":
            out[name + "_2"] = value
    return out


def reference(
    x, norm_mix, w_in, swa_sinks, rel_bias, gla_gate_w, gla_gate_b, gla_norm, swa_out_norm,
    sb_out_norm, w_out, norm_mlp, w_mlp_in, w_mlp_out, norm_final, c_2, ctx_2, c_ctx_2,
    norm_mix_g_2, norm_ffn_g_2, w_ada_2, b_ada_2, na_w_qkv_2, na_q_g_2, na_k_g_2, na_rpb_2,
    na_w_o_2, gm_w_in_2, gm_v_g_2, gm_w_s_2, gm_b_s_2, gm_w_out_2, sc_w_in_2, sc_conv_w_2,
    sc_w_out_2, ffn_w_up_2, ffn_conv_w_2, ffn_conv_b_2, ffn_w_down_2,
):
    x = first_block(
        x, norm_mix, w_in, swa_sinks, rel_bias, gla_gate_w, gla_gate_b, gla_norm, swa_out_norm,
        sb_out_norm, w_out, norm_mlp, w_mlp_in, w_mlp_out, norm_final,
    )
    return second_block(
        x, c_2, ctx_2, c_ctx_2, norm_mix_g_2, norm_ffn_g_2, w_ada_2, b_ada_2, na_w_qkv_2,
        na_q_g_2, na_k_g_2, na_rpb_2, na_w_o_2, gm_w_in_2, gm_v_g_2, gm_w_s_2, gm_b_s_2,
        gm_w_out_2, sc_w_in_2, sc_conv_w_2, sc_w_out_2, ffn_w_up_2, ffn_conv_w_2, ffn_conv_b_2,
        ffn_w_down_2,
    )


_drawn_inputs = setup_inputs


def setup_inputs(seed=0):
    import zlib

    import numpy as np

    out = dict(_drawn_inputs(seed))
    spreads = {}
    factors = {'swa_sinks': 4.052,
     'gla_gate_b': 4.154,
     'gla_norm': 3.685,
     'sb_out_norm': 2.789,
     'norm_mix_g_2': 8.0,
     'b_ada_2': 3.089,
     'na_q_g_2': 8.0,
     'na_k_g_2': 8.0,
     'na_rpb_2': 8.0,
     'ffn_conv_b_2': 27.274,
     'norm_ffn_g_2': 5.202}
    for name, (base, spread) in spreads.items():
        noise = np.random.default_rng([zlib.crc32(name.encode()), seed]).standard_normal(out[name].shape)
        drawn = base * np.exp(spread * noise) if base else spread * noise
        out[name] = __import__('jax').numpy.asarray(drawn.astype(out[name].dtype))
    for name, factor in factors.items():
        out[name] = (out[name] * factor).astype(out[name].dtype)
    return out
```

```python
import math
from contextlib import ExitStack, contextmanager

import numpy as np

import concourse.bass as bass
from concourse import mybir

F32 = mybir.dt.float32
F32R = mybir.dt.float32r
ACT = mybir.ActivationFunctionType
ALU = mybir.AluOpType
AXX = mybir.AxisListType.X

P = 128
S = 256
RT = S // P
D = 2048
KC = D // P
HD = 64
SWA_W, SWA_H, SWA_KV, SWA_G = 768, 12, 4, 3
GLA_H, DK, DV, LR, CH = 4, 96, 192, 16, 64
SB_W, SB_H = 512, 8
FF = 4 * D
NH, NHD = 16, 128
GRID, WIN_W, ROWS = 64, 16, 4
FFN = 5504
FC = FFN // P
EPS = 1e-6
NEG = -1e30
ADA_W = 384

PANELS_IN = [
    ("Q0", 0, 384), ("Q1", 384, 384), ("KV", 768, 512), ("GQ", 1280, 384), ("GK", 1664, 384),
    ("BR0", 2816, 384), ("BR1", 3200, 400), ("BV0", 2048, 384), ("BV1", 2432, 384),
    ("CQ", 3600, 512), ("CK", 4112, 512), ("CV", 4624, 512),
]

RING = 4
U_IN = 0
U_OUT = U_IN + 8 * len(PANELS_IN)
U_MLP = U_OUT + 8 * 4
U_NA = U_MLP + 8 * 32
U_WO = U_NA + 12 * 8
U_FFN = U_WO + 8 * 4
U_LAST = U_FFN + 2 * 96
U_DOWN = U_LAST + 4 * 8 + 2 * 8
U_END = U_DOWN + 4 * 6

CONST = {}
_at = 0
for _name, _w in (("ident", 128), ("ones", 128), ("tri", 128), ("strict", 128), ("negstrict", 128),
                  ("swamask", 256), ("namask", 64), ("glamask", 128), ("reset", 256), ("bucket", 256)):
    CONST[_name] = (_at, _at + _w)
    _at += _w
NCONST = _at


def shape_constants():
    c = np.zeros((P, NCONST), np.float32)
    p, f = np.arange(P)[:, None], np.arange(P)[None, :]

    def put(name, v):
        a, b = CONST[name]
        c[:v.shape[0], a:b] = v

    put("ident", (p == f).astype(np.float32))
    put("ones", np.ones((P, P), np.float32))
    put("tri", (p >= f).astype(np.float32))
    put("strict", (p < f).astype(np.float32))
    put("negstrict", np.where(p < f, 0.0, NEG).astype(np.float32))
    put("swamask", np.concatenate([np.where(f > p, 0.0, NEG), np.where(f <= p, 0.0, NEG)], 1).astype(np.float32))
    qc, kc = np.arange(P)[:, None] % GRID, np.arange(GRID)[None, :]
    first = np.clip(qc - WIN_W // 2, 0, GRID - WIN_W)
    put("namask", np.where((kc >= first) & (kc < first + WIN_W), 0.0, NEG).astype(np.float32))
    put("glamask", ((p // CH == f // CH) & (p <= f)).astype(np.float32))
    put("reset", np.broadcast_to((np.arange(S) % CH != 0).astype(np.float32), (P, S)))
    dist = (-np.arange(S)) % P
    ratio = np.log(np.maximum(dist, 1).astype(np.float32) / np.float32(16)) / np.float32(math.log(128 / 16))
    large = np.minimum(16 + (ratio * np.float32(16)).astype(np.int32), 31)
    bucket = np.where(dist < 16, dist, large)
    put("bucket", (np.arange(32)[:, None] == bucket[None, :]).astype(np.float32))
    return c


COLS0 = [("norm_mix", 0, 16), ("norm_mlp", 16, 16), ("norm_mix_g_2", 32, 16), ("norm_ffn_g_2", 48, 16),
         ("c_2", 64, 16), ("c_ctx_2", 80, 16)]
R_MIXG, R_QG, R_KG = 96, 112, 113
C_PACK0, C_ADAB, C_GATEB, C_CONV = 0, 114, 210, 214
NCOLS = C_CONV + 4 * 2 * FC


NROWS_DMA = len(COLS0) + 2 + 8 + 8
AHEAD = 2


NA_SCALE = float(NHD) ** -0.5
NA_OWN = 36
TURN_AT = [0, KC, 2 * KC, 3 * KC, 4 * KC, 6 * KC]
OT_AT = 5 * KC


class Steps:

    def __init__(self, eng, sem):
        self.eng, self.sem, self.n, self.turns = eng, sem, 0, []

    def mark(self, ins):
        ins.then_inc(self.sem, 1)
        self.n += 1

    def wait(self):
        value = self.n
        for var, per in self.turns:
            value = var * per + value
        self.eng.wait_ge(self.sem, value)

    def done(self, ins):
        self.mark(ins)
        self.wait()

    @contextmanager
    def loop(self, start, end, per):
        enter = self.n
        self.n = enter - start * per
        at = self.n
        with self.eng.Fori(start, end) as var:
            self.turns.append((var, per))
            yield var
            self.turns.pop()
        assert self.n - at == per, f"{self.n - at} steps in a turn"
        self.n = enter + (end - start) * per


def program(nc, t, out):
    ctx = ExitStack()
    with ctx:
        def sb(name, shape, dt=F32):
            return ctx.enter_context(nc.sbuf_tensor(name, shape, dt))

        def sem(name):
            return ctx.enter_context(nc.semaphore(name))

        raw = sb("raw", [P, RING, 1024])
        whi = sb("whi", [P, RING, 1024], F32R)
        wlo = sb("wlo", [P, RING, 1024], F32R)
        ahi = sb("ahi", [P, KC, 2 * S], F32R)
        alo = sb("alo", [P, KC, 2 * S], F32R)
        x = sb("x", [P, RT, D])
        cst = sb("cst", [P, NCONST])
        cols = sb("cols", [P, NCOLS])
        mods = sb("mods", [P, 96])
        modc = sb("modc", [P, 48])
        cond = sb("cond", [P, 32])
        stat = sb("stat", [P, 168])
        arena = sb("arena", [P, 17152])
        ps = ctx.enter_context(nc.psum_tensor("ps", [P, 8, 512], F32))
        G = [ps[:, 0:2, :], ps[:, 2:4, :]]
        Gf = [g.rearrange("p a b -> p (a b)") for g in G]
        X = [ps[:, 4 + b, :] for b in range(4)]
        X01 = ps[:, 4:6, :].rearrange("p a b -> p (a b)")
        X23 = ps[:, 6:8, :].rearrange("p a b -> p (a b)")

        def C(name):
            return cst[:, CONST[name][0]:CONST[name][1]]

        def area(first, *shape):
            n = int(np.prod(shape))
            v = arena[:, first:first + n]
            if len(shape) == 1:
                return v
            names = "abcd"[:len(shape)]
            return v.rearrange(f"p ({' '.join(names)}) -> p {' '.join(names)}",
                               **{names[i]: shape[i] for i in range(len(shape) - 1)})

        ident, ones = C("ident"), C("ones")
        sq_ = area(0, 6, S)
        skd = area(1536, 4, S)
        sv = area(2560, RT, S)
        bm = area(3072, 12, S)
        cq, ck = area(0, 4, S), area(1024, 4, S)
        cv = area(2048, RT, SB_W)
        sb_z, sb_l, sb_p, sb_w = (area(3072 + 768 * i, 2, 384) for i in range(4))
        gq, gk = area(6144, 4, S), area(7168, 4, S)
        bv, br = area(8192, RT, 768), area(9728, RT, 768)
        lrT = area(11264, S)
        swt = area(11520, 2, 2, S)
        swp = area(12544, 2, 512)
        g1, g2, g3 = (area(11520 + 1024 * i, 4, S) for i in range(3))
        kend = area(14592, RT, 4 * DK)
        state = area(15360, 4 * DV)
        scT = area(16128, RT, 4, P)
        xs = area(0, RT, D)
        colrow = area(11520, 7, P)
        fT = area(16128, S)
        gw = area(15360, 384)
        relb = area(16384, 12)
        ada1 = area(4096, 4, 4, ADA_W)
        accL, accC = area(10240, ADA_W), area(10624, ADA_W)
        ebias = area(11008, 16, 6, GRID)
        nfin = area(11008, D)
        ctxr = area(13056, RT, D)
        tabp = area(11008, P)
        relu = area(0, 1024)
        sqr = area(1024, 1024)
        oT = area(0, NH, S)
        kT = area(4096, 2, 2 * S)
        vv = area(5120, 4, S)
        qT = area(6144, 2, S)
        eh = area(6656, 2, 6 * GRID)
        pr = area(7424, 2, 512)
        pT = area(8448, 2, 512)
        nsq = area(9472, 1024)
        nrs = area(10496, 1024)
        ada2 = area(11520, 2, 4, ADA_W)
        acc2 = area(14592, ADA_W)
        gb = area(14976, D)
        gdiag = area(4096, 512)
        turned_f = area(8448, 2, S)
        tmp = area(4096, 1024)
        held = area(5120, 1024)
        cvt = area(6144, 1024)

        negsink, sink = stat[:, 0:12], stat[:, 12:24]
        smax, snm, sden, ses = (stat[:, 24 + 24 * i:48 + 24 * i] for i in range(4))
        ssum, rstd = stat[:, 120:132], stat[:, 132:144]
        mss, mrs = stat[:, 144:156], stat[:, 156:168]
        acc3 = sb("acc3", [P, ADA_W])
        dec = sb("dec", [P, 16])
        nst = sb("nst", [P, 48])
        dg = sb("dg", [P, 2, P])
        coefs = sb("coefs", [P, 48])

        bias_dram = nc.dram_tensor("swa_bias_scratch", [12, P, S], F32, kind="Internal").ap()
        tab_dram = nc.dram_tensor("na_table_scratch", [112, GRID, P], F32, kind="Internal").ap()
        eb_dram = nc.dram_tensor("na_bias_scratch", [P, 16 * 384], F32, kind="Internal").ap()

        raw_full = [sem(f"raw_full{i}") for i in range(RING)]
        hi_done, lo_done = sem("hi_done"), sem("lo_done")
        unit_used = sem("unit_used")
        drained = [sem("drained0"), sem("drained1")]
        act_step, dve_step, pool_step = sem("act_step"), sem("dve_step"), sem("pool_step")
        x_in, cst_in, small_in, rows_in = sem("x_in"), sem("cst_in"), sem("small_in"), sem("rows_in")
        colT, cols_ok = sem("colT"), sem("cols_ok")
        ss_a, rstd_ok, xs_ok, turned, a_hi, a_lo = (sem(n) for n in
                                                    ("ss_a", "rstd_ok", "xs_ok", "turned", "a_hi", "a_lo"))
        ft_mm, ft_ok, ft_out, bm_in, bm_ok = (sem(n) for n in ("ft_mm", "ft_ok", "ft_out", "bm_in", "bm_ok"))
        in_ready = sem("in_ready")
        lr_ok = [sem(f"lr_ok{i}") for i in range(RING)]
        w_s, w_t, w_nm, w_p, w_tr, w_pt, w_o, w_out_ok = (sem("swa_" + n) for n in
            ("scores", "logits", "max", "exp", "turned", "pt", "pv", "out"))
        gla = {n: sem("gla_" + n) for n in ("gate", "l", "b", "eb", "q", "ki", "d", "ke", "turn", "kend", "sc",
                                            "scm", "intra", "ic", "ds", "st", "inter", "add")}
        sbs = {n: sem("sb_" + n) for n in ("z", "zs", "l", "p", "c", "arg", "w", "o", "out")}
        mix_a, mix_v = sem("mix_a"), sem("mix_v")
        x_again = sem("x_again")
        hid_a, hid_v = sem("hid_a"), sem("hid_v")
        ada_in = [sem(f"ada_in{i}") for i in range(4)]
        ada_done, ada_used, ada_mm, ada_col = sem("ada_done"), sem("ada_used"), sem("ada_mm"), sem("ada_col")
        tab_ok, tab_out, e_in, e_ok, e_out, nf_in, ctx_in = (sem(n) for n in
            ("tab_ok", "tab_out", "e_in", "e_ok", "e_out", "nf_in", "ctx_in"))
        cond_ok, coef_ok = sem("cond_ok"), sem("coef_ok")
        n_eh, n_s, n_t, n_nm, n_p, n_dg, n_tr, n_pt, n_o, n_oc = (sem("na_" + n) for n in
            ("bias", "scores", "logits", "max", "exp", "diag", "turned", "pt", "pv", "out"))
        n_sq, n_nsum, n_rs, n_norm, n_v = (sem("na_" + n) for n in ("sq", "nsum", "rs", "norm", "v"))
        gb_mm, gb_ok, gb_rd = sem("gb_mm"), sem("gb_ok"), sem("gb_rd")
        tmp_ok = sem("tmp_ok")
        x_done, stored = sem("x_done"), sem("stored")
        f_a, f_v = sem("f_a"), sem("f_v")

        D0_IN, D1_IN = 10, 6
        D_OUT = (D0_IN + 2, D1_IN + 2)
        D_MLP = (D_OUT[0] + 16, D_OUT[1] + 16)
        D_NA = (D_MLP[0], D_MLP[1] + 8)
        D_WO = (D_NA[0] + 2, D_NA[1] + 2)
        D_F1 = (D_WO[0] + 12, D_WO[1] + 12)

        block = ctx.enter_context(nc.Block())

        PLAN = {}
        for s in range(12):
            PLAN.setdefault(26 + 3 * s, []).append(("swa_a", s))
            PLAN.setdefault(27 + 3 * s, []).append(("swa_b", s))
            PLAN.setdefault(28 + 3 * s, []).append(("swa_c", s))
        for n, m in enumerate((66, 74, 77, 79, 81, 83, 86, 88, 90)):
            PLAN.setdefault(m, []).append(("gla", n))

        @block.sync
        def _(sp):
            def load(u0, j, dst, src):
                if not (isinstance(u0, int) and u0 + j < RING):
                    sp.wait_ge(lo_done, u0 + (j - RING + 1))
                sp.dma_start(dst, src).then_inc(raw_full[j % RING], 16)

            def wide(u0, j, w, src, kk=2):
                dst = raw[:, j % RING, :].rearrange("p (k n) -> p k n", n=512)[:, 0:kk, 0:w]
                load(u0, j, dst, src)

            x_rows = t["x"].rearrange("b (r p) d -> p (b r) d", p=P)
            sp.dma_start(x[:, :, :], x_rows).then_inc(x_in, 16)
            sp.dma_start(cst[:, :], t["consts"]).then_inc(cst_in, 16)
            w_in = t["w_in"][0].rearrange("(k p) n -> p k n", p=P)
            for n, (name, c0, w) in enumerate(PANELS_IN):
                for j in range(8):
                    u = 8 * n + j
                    if name == "BR1":
                        if u >= RING:
                            sp.wait_ge(lo_done, u - RING + 1)
                        dst = raw[:, j % RING, :].rearrange("p (k n) -> p k n", n=512)
                        sp.dma_start(dst[:, :, 0:LR], w_in[:, 2 * j:2 * j + 2, 3584:3600]).then_inc(lr_ok[j % RING], 16)
                        sp.dma_start(dst[:, :, LR:400], w_in[:, 2 * j:2 * j + 2, 3200:3584])\
                          .then_inc(raw_full[j % RING], 16)
                    else:
                        wide(8 * n, j, w, w_in[:, 2 * j:2 * j + 2, c0:c0 + w])

            w_o = t["w_out"][0].rearrange("(k p) n -> p k n", p=P)
            with sp.Fori(0, 4) as n:
                for j in range(8):
                    wide(n * 8 + U_OUT, j, 512, w_o[:, 2 * j:2 * j + 2, bass.ds(n * 512, 512)])
            w1 = t["w_mlp_in"][0].rearrange("(k p) n -> p k n", p=P)
            w2 = t["w_mlp_out"][0].rearrange("(k p) n -> p k n", p=P)
            with sp.Fori(0, 4) as g:
                with sp.Fori(0, 4) as n:
                    for j in range(8):
                        wide(g * 64 + n * 8 + U_MLP, j, 512, w1[:, 2 * j:2 * j + 2, bass.ds(g * 2048 + n * 512, 512)])
                with sp.Fori(0, 4) as n:
                    for j in range(8):
                        wide(g * 64 + n * 8 + (U_MLP + 32), j, 512,
                             w2[:, bass.ds(g * 16 + 2 * j, 2), bass.ds(n * 512, 512)])
            wq = t["na_w_qkv_2"][0].rearrange("(k p) n -> p k n", p=P)
            with sp.Fori(1, 9) as i:
                for j in range(12):
                    first = (D, 0, 2 * D)[j // 4]
                    load(i * 12 + (U_NA - 12), j, raw[:, j % RING, :].rearrange("p (k n) -> p k n", n=256),
                         wq[:, 4 * (j % 4):4 * (j % 4) + 4, bass.ds(i * 256 + (first - 256), 256)])
            wo = t["na_w_o_2"][0].rearrange("(k p) n -> p k n", p=P)
            with sp.Fori(0, 4) as n:
                for j in range(8):
                    wide(n * 8 + U_WO, j, 512, wo[:, 2 * j:2 * j + 2, bass.ds(n * 512, 512)])
            fu = t["ffn_w_up_2"][0].rearrange("(k p) n -> p k n", p=P)
            fd = t["ffn_w_down_2"][0].rearrange("(k p) n -> p k n", p=P)
            with sp.Fori(0, 2) as g:
                with sp.Fori(0, 4) as n:
                    for j in range(16):
                        wide(g * 96 + n * 16 + U_FFN, j, 512,
                             fu[:, 2 * (j % 8):2 * (j % 8) + 2, bass.ds(g * 2048 + n * 512 + (j // 8) * FFN, 512)])
                with sp.Fori(0, 4) as n:
                    for j in range(8):
                        wide(g * 96 + n * 8 + (U_FFN + 64), j, 512,
                             fd[:, bass.ds(g * 16 + 2 * j, 2), bass.ds(n * 512, 512)])
            with sp.Fori(0, 2) as n:
                for j in range(16):
                    wide(n * 16 + U_LAST, j, 512,
                         fu[:, 2 * (j % 8):2 * (j % 8) + 2, bass.ds(n * 512 + (4096 + (j // 8) * FFN), 512)])
            for j in range(16):
                c0 = 5120 + (j // 8) * FFN
                wide(U_LAST + 32, j, 384, fu[:, 2 * (j % 8):2 * (j % 8) + 2, c0:c0 + 384])
            with sp.Fori(0, 2) as n:
                for j in range(12):
                    kk = 1 if j % 6 == 5 else 2
                    k0 = 32 + 2 * (j % 6)
                    wide(n * 12 + U_DOWN, j, 512, fd[:, k0:k0 + kk, bass.ds(n * 1024 + (j // 6) * 512, 512)], kk)
            sp.wait_ge(x_done, 5)
            sp.dma_start(out.rearrange("b (r p) d -> p (b r) d", p=P), x[:, :, :]).then_inc(stored, 16)
            sp.wait_ge(stored, 16)

        @block.gpsimd
        def _(pool):
            own = Steps(pool, pool_step)
            own.done(pool.memset(colrow, 0.0))
            n = 0
            for name, r0, k in COLS0:
                v = t[name]
                v = v[0] if len(v.shape) == 2 else v
                pool.dma_start(colrow[r0:r0 + k, 0, :], v.rearrange("(k n) -> k n", n=P)).then_inc(rows_in, 16)
                n += 1
            sw, so = t["swa_out_norm"][0], t["sb_out_norm"][0]
            pool.dma_start(colrow[R_MIXG:R_MIXG + 6, 0, :], sw.rearrange("(k n) -> k n", n=P)).then_inc(rows_in, 16)
            pool.dma_start(colrow[R_MIXG + 12:R_MIXG + 16, 0, :], so.rearrange("(k n) -> k n", n=P)).then_inc(rows_in, 16)
            n += 2
            gn = t["gla_norm"]
            for h in range(2):
                r = R_MIXG + 6 + 3 * h
                for row, a, b, s0 in ((r, 0, 128, 0), (r + 1, 0, 64, 128), (r + 1, 64, 128, 0), (r + 2, 0, 128, 64)):
                    pool.dma_start(colrow[row:row + 1, 0, a:b], gn[0:1, s0:s0 + b - a]).then_inc(rows_in, 16)
                    n += 1
            pool.dma_start(colrow[R_QG:R_QG + 1, 0, :], t["na_q_g_2"]).then_inc(rows_in, 16)
            pool.dma_start(colrow[R_KG:R_KG + 1, 0, :], t["na_k_g_2"]).then_inc(rows_in, 16)
            pool.dma_start(colrow[0:96, 1, :], t["b_ada_2"][0].rearrange("(k n) -> k n", n=P)).then_inc(rows_in, 16)
            pool.dma_start(colrow[0:4, 2, 0:DK], t["gla_gate_b"][0].rearrange("(k n) -> k n", n=DK)).then_inc(rows_in, 16)
            pool.dma_start(colrow[0:2 * FC, 3, :], t["ffn_conv_b_2"][0].rearrange("(k n) -> k n", n=P)).then_inc(rows_in, 16)
            for i in range(3):
                pool.dma_start(colrow[0:2 * FC, 4 + i, :], t["ffn_conv_w_2"][0, i].rearrange("(k n) -> k n", n=P))\
                    .then_inc(rows_in, 16)
            n += 8
            assert n == NROWS_DMA
            pool.dma_start(relb[0:32, :], t["rel_bias"]).then_inc(small_in, 16)
            pool.dma_start(sink, bass.AP(t["swa_sinks"].tensor, 0, [[0, P], [1, 12]])).then_inc(small_in, 16)
            pool.dma_start(gw[0:LR, :], t["gla_gate_w"][0]).then_inc(small_in, 16)
            pool.wait_ge(ft_ok, 1)
            pool.dma_start(bias_dram, fT[0:12, :].unsqueeze(1).to_broadcast([12, P, S])).then_inc(ft_out, 16)
            pool.wait_ge(ft_out, 16)
            pool.wait_ge(turned, 8)
            shifted = bass.AP(bias_dram.tensor, P, [[S - 1, P], [P * S, 12], [1, P]])
            pool.dma_start(bm[:, :, P:S], shifted).then_inc(bm_in, 16)
            pool.wait_ge(bm_in, 16)
            own.done(pool.tensor_copy(bm[:, :, 0:P], bm[:, :, P:S]))
            m = C("swamask").unsqueeze(1).to_broadcast([P, 12, S])
            pool.wait_ge(cst_in, 16)
            pool.tensor_tensor(bm[:, :, :], bm[:, :, :], m, ALU.add).then_inc(bm_ok, 1)
            pool.wait_ge(turned, 8 + 8)
            pool.dma_start(x[:, :, :], t["x"].rearrange("b (r p) d -> p (b r) d", p=P)).then_inc(x_again, 16)
            wa = t["w_ada_2"][0].rearrange("(k p) n -> p k n", p=P)

            def ada_load(s, q, wait=True):
                if wait:
                    pool.wait_ge(ada_done, s * 4 + (q - 3))
                pool.dma_start(ada1[:, q, :, :], wa[:, 4 * q:4 * q + 4, bass.ds(s * ADA_W, ADA_W)])\
                    .then_inc(ada_in[q], 16)
            for q in range(4):
                ada_load(0, q, False)
            own.done(pool.memset(tabp[0:112, :], 0.0))
            for h in range(NH):
                pool.dma_start(tabp[7 * h:7 * h + 7, 48:79], t["na_rpb_2"][0, h, 4:11, :]).then_inc(tab_ok, 16)
            pool.wait_ge(tab_ok, 16 * NH)
            pool.dma_start(tab_dram, tabp[0:112, :].unsqueeze(1).to_broadcast([112, GRID, P])).then_inc(tab_out, 16)
            pool.wait_ge(tab_out, 16)
            for h in range(NH):
                for half in range(2):
                    first = (7 * h + 1 - half) * GRID * P + GRID - 1
                    src = bass.AP(tab_dram.tensor, first, [[P - 1, GRID], [GRID * P, 6], [1, GRID]])
                    pool.dma_start(ebias[GRID * half:GRID * half + GRID, h, :, :], src).then_inc(e_in, 16)
            pool.wait_ge(e_in, 32 * NH)
            for h in range(NH):
                own.mark(pool.tensor_tensor(ebias[:, h, :, :], ebias[:, h, :, :],
                                            C("namask").unsqueeze(1).to_broadcast([P, 6, GRID]), ALU.add))
            own.wait()
            pool.dma_start(eb_dram, ebias.rearrange("p a b c -> p (a b c)")).then_inc(e_out, 16)
            pool.wait_ge(e_out, 16)
            pool.dma_start(nfin, bass.AP(t["norm_final"].tensor, 0, [[0, P], [1, D]])).then_inc(nf_in, 16)
            pool.dma_start(ctxr, t["ctx_2"].rearrange("b (r p) d -> p (b r) d", p=P)).then_inc(ctx_in, 16)
            with pool.Fori(1, 16) as s:
                for q in range(4):
                    ada_load(s, q)
            pool.wait_ge(turned, 8 * 5)

            def attention_loads(i):
                for q in range(8):
                    s, c = q // 4, q % 4
                    pool.wait_ge(ada_done, i * 8 + (64 + q - 1))
                    pool.dma_start(ada2[:, q % 2, :, :],
                                   wa[:, 4 * c:4 * c + 4, bass.ds(i * 768 + (6144 + s * ADA_W), ADA_W)])\
                        .then_inc(ada_in[q % 2], 16)
                    if q == 3:
                        pool.wait_ge(n_t, i * 4 + AHEAD)
                        pool.dma_start(eh, eb_dram.rearrange("p (h c) -> p h c", c=384)[:, bass.ds(i * 2, 2), :])\
                            .then_inc(n_eh, 16)
            with pool.Fori(0, 8) as i:
                attention_loads(i)

        @block.scalar
        def _(act):
            own = Steps(act, act_step)
            act.preload_act_table_set("natural_log_exp_and_others")
            act.sem_inc(n_pt, AHEAD)
            act.sem_inc(n_rs, AHEAD)

            def split(u0, j, w=1024, extra=None):
                s = j % RING
                act.wait_ge(raw_full[s], u0 * 4 + 16 * (j // RING + 1))
                if extra:
                    act.wait_ge(*extra)
                if not (isinstance(u0, int) and u0 + j < RING):
                    act.wait_ge(unit_used, u0 + (j - RING + 1))
                a, b = (v[:, s, :] for v in (whi, raw))
                if w < 1024:
                    a, b = (v.rearrange("p (k n) -> p k n", n=512)[:, 0:2, 0:w] for v in (a, b))
                act.activation(a, b, ACT.Copy).then_inc(hi_done, 1)

            def rms_rows(n, rows, junk):
                own.done(act.activation(junk, rows, ACT.Square, accum_out=ssum[:, 2 * n:2 * n + 1]))
                act.wait_ge(ss_a, n + 1)
                own.done(act.activation(rstd[:, 2 * n:2 * n + 2], ssum[:, 2 * n:2 * n + 2], ACT.Ln, scale=1.0 / D, bias=EPS))
                act.activation(rstd[:, 2 * n:2 * n + 2], rstd[:, 2 * n:2 * n + 2], ACT.Exp, scale=-0.5)\
                    .then_inc(rstd_ok, 1)
                act.wait_ge(rstd_ok, n + 1)

            def turn(e, off, gain, shift=None):
                for k in range(KC):
                    act.wait_ge(turned, 8 * e + k // 2 + 1)
                    z = X[(k // 2) % 4][:, (k % 2) * S:(k % 2) * S + S]
                    b = shift(k) if shift else 0.0
                    act.activation(ahi[:, k, off:off + S], z, ACT.Identity, scale=gain(k), bias=b).then_inc(a_hi, 1)

            act.wait_ge(x_in, 16)
            rms_rows(0, x[:, 0, :], xs[:, 0, :])
            act.activation(xs[:, 0, :], x[:, 0, :], ACT.Copy, scale=rstd[:, 0:1]).then_inc(xs_ok, 1)
            act.wait_ge(cols_ok, 2)
            for m in range(3):
                split(0, m, 384)
            turn(0, 0, lambda k: cols[:, k:k + 1])

            cc = cols[:, 64:96]
            own.done(act.activation(cond[:, :], cc, ACT.Abs))
            own.done(act.activation(cond[:, :], cond[:, :], ACT.Exp, scale=-1.0))
            act.activation(cond[:, :], cond[:, :], ACT.Ln, bias=1.0).then_inc(cond_ok, 1)
            act.wait_ge(cond_ok, 2)
            act.activation(cond[:, :], cond[:, :], ACT.Exp).then_inc(cond_ok, 1)

            def evac_in(n):
                name = PANELS_IN[n][0]
                act.wait_ge(unit_used, 8 * n + 8)
                g, gf = G[n % 2], Gf[n % 2]
                done = drained[n % 2]
                if name in ("Q0", "Q1"):
                    act.activation(sq_[:, 3 * n:3 * n + 3, :], gf[:, 0:768].rearrange("p (c t) -> p c t", t=S),
                                   ACT.Copy).then_inc(done, 1)
                elif name == "KV":
                    kk = skd.rearrange("p (c a) t -> p c a t", a=2)
                    for a in range(2):
                        act.activation(kk[0:HD, :, a, :], g[HD * a:HD * a + HD, 0, :].rearrange("p (c t) -> p c t", t=S),
                                       ACT.Copy).then_inc(done, 1)
                    act.activation(sv[:, :, :], g[:, 1, :].rearrange("p (c t) -> p c t", t=S), ACT.Copy).then_inc(done, 1)
                elif name in ("GQ", "GK"):
                    act.activation((gq if name == "GQ" else gk)[0:DK], gf[0:DK, :].rearrange("p (c t) -> p c t", t=S),
                                   ACT.Copy).then_inc(done, 1)
                elif name == "BR1":
                    act.activation(lrT[0:LR, :].rearrange("p (r t) -> p r t", r=RT), g[0:LR, :, 384:512], ACT.Copy)\
                        .then_inc(in_ready, 1)
                    act.activation(br[:, :, 384:768], g[:, :, 0:384], ACT.Copy).then_inc(done, 1)
                elif name in ("BR0", "BV0", "BV1"):
                    dst = {"BR0": br[:, :, 0:384], "BV0": bv[:, :, 0:384], "BV1": bv[:, :, 384:768]}[name]
                    act.activation(dst, g[:, :, 0:384], ACT.Copy).then_inc(done, 1)
                elif name in ("CQ", "CK"):
                    act.wait_ge(w_out_ok, 12)
                    act.activation(cq if name == "CQ" else ck, gf.rearrange("p (c t) -> p c t", t=S),
                                   ACT.Copy).then_inc(done, 1)
                else:
                    act.activation(cv, g[:, :, :], ACT.Copy).then_inc(done, 1)

            def swa(part, s):
                n, c = divmod(s, 6)
                w, lo = (P, P) if n == 0 else (S, 0)
                if part == "swa_a":
                    act.wait_ge(w_nm, s + 1)
                    for a in range(2):
                        v = swt[:, s % 2, a, 0:w]
                        i = 12 * n + 2 * c + a
                        act.activation(v, v, ACT.Exp, bias=snm[:, i:i + 1], accum_out=sden[:, i:i + 1]).then_inc(w_p, 1)
                    i = 12 * n + 2 * c
                    act.activation(ses[:, i:i + 2], ses[:, i:i + 2], ACT.Exp).then_inc(w_p, 1)
                elif part == "swa_b":
                    act.wait_ge(w_tr, s + 1)
                    if s >= 2:
                        act.wait_ge(w_o, s - 1)
                    k = 2 * w
                    act.activation(swp[:, s % 2, 0:k], X[2][:, 0:k], ACT.Copy).then_inc(w_pt, 1)

            def gla_a(n):
                if n == 0:
                    act.wait_ge(gla["gate"], 1)
                    for h in range(4):
                        own.mark(act.activation(g1[0:DK, h, :], X01[0:DK, S * h:S * h + S], ACT.Abs,
                                                bias=cols[0:DK, C_GATEB + h:C_GATEB + h + 1]))
                    own.wait()
                    own.done(act.activation(g1[0:DK], g1[0:DK], ACT.Exp, scale=-1.0))
                    act.activation(g1[0:DK], g1[0:DK], ACT.Ln, bias=1.0).then_inc(gla["l"], 1)
                    act.wait_ge(gla["b"], 1)
                    act.activation(g2[0:DK], g1[0:DK], ACT.Exp).then_inc(gla["eb"], 1)
                    act.activation(g3[0:DK], g1[0:DK], ACT.Exp, scale=-1.0).then_inc(gla["eb"], 1)
                    last = g1[0:DK].rearrange("p h (c t) -> p h c t", t=CH)[:, :, :, CH - 1]
                    act.activation(dec[0:DK, :].rearrange("p (h c) -> p h c", c=4), last, ACT.Exp).then_inc(gla["eb"], 1)
                    act.wait_ge(gla["d"], 1)
                    act.activation(g2[0:DK], g2[0:DK], ACT.Exp).then_inc(gla["ke"], 1)
                if n == 1:
                    act.wait_ge(gla["turn"], 2)
                    for r in range(RT):
                        act.activation(kend[:, r, :], X[2 + r][:, 0:4 * DK], ACT.Copy).then_inc(gla["kend"], 1)
                if n in (2, 3):
                    r = n - 2
                    act.wait_ge(gla["intra"], n - 1)
                    m = x[:, r, SWA_W:SWA_W + 768].rearrange("p (a b) -> p a b", a=2)
                    act.activation(m, ps[:, 4:6, 0:384], ACT.Copy).then_inc(gla["ic"], 1)

            for m in range(8 * len(PANELS_IN)):
                n, j = divmod(m + 3, 8)
                if n < len(PANELS_IN):
                    name, _, w = PANELS_IN[n]
                    split(8 * n, j, w, (lr_ok[j % RING], 16 * (j // RING + 1)) if name == "BR1" else None)
                else:
                    split(8 * n, j)
                if m % 8 == 0 and m:
                    evac_in(m // 8 - 1)
                for part, s in PLAN.get(m, []):
                    swa(part, s) if part != "gla" else gla_a(s)
            split(U_OUT, 3)
            evac_in(len(PANELS_IN) - 1)

            for c in range(4):
                act.wait_ge(sbs["z"], c + 1)
                v = sb_l[:, :, :]
                own.done(act.activation(v, ps[:, 4:6, 0:384], ACT.Abs, scale=0.125))
                own.done(act.activation(v, v, ACT.Exp, scale=-1.0))
                act.activation(v, v, ACT.Ln, bias=1.0).then_inc(sbs["l"], 1)
                act.wait_ge(sbs["arg"], c + 1)
                act.activation(sb_w[:, :, :], sb_w[:, :, :], ACT.Exp).then_inc(sbs["w"], 1)
                act.wait_ge(sbs["o"], c + 1)
                for r in range(RT):
                    act.activation(x[:, r, 1536 + P * c:1536 + P * c + P], X[2 + r][:, 384:512], ACT.Copy)\
                        .then_inc(sbs["out"], 1)

            act.wait_ge(mix_v, 1)
            own.done(act.activation(mrs[:, 0:2], mss[:, 0:2], ACT.Ln, scale=1.0 / SWA_W, bias=EPS))
            own.done(act.activation(mrs[:, 2:10], mss[:, 2:10], ACT.Ln, scale=1.0 / DV, bias=EPS))
            own.done(act.activation(mrs[:, 10:12], mss[:, 10:12], ACT.Ln, scale=1.0 / SB_W, bias=EPS))
            act.activation(mrs[:, :], mrs[:, :], ACT.Exp, scale=-0.5).then_inc(mix_a, 1)
            sg = area(11520, RT, 768)
            own.done(act.activation(sg, br, ACT.Abs))
            own.done(act.activation(sg, sg, ACT.Exp, scale=-1.0))
            act.activation(sg, sg, ACT.Ln, bias=1.0).then_inc(mix_a, 1)
            act.wait_ge(mix_v, 2)
            act.activation(sg, sg, ACT.Exp).then_inc(mix_a, 1)
            turn(1, S, lambda k: cols[:, R_MIXG + k:R_MIXG + k + 1])

            with act.Fori(0, 4) as n:
                for j in range(4, 12):
                    split(n * 8 + U_OUT, j)

            act.wait_ge(x_done, 1)
            rms_rows(1, x[:, 0, :], xs[:, 0, :])
            act.activation(xs[:, 0, :], x[:, 0, :], ACT.Copy, scale=rstd[:, 2:3]).then_inc(xs_ok, 1)
            turn(2, 0, lambda k: cols[:, 16 + k:17 + k])
            with own.loop(0, 4, 4) as g:
                with own.loop(0, 2, 2) as i:
                    for j in range(4, 20):
                        split(g * 64 + i * 16 + U_MLP, j)
                        if j % 8 == 3:
                            q = j // 8 - 1
                            act.wait_ge(unit_used, g * 64 + i * 16 + (U_MLP + 8 * q + 8))
                            act.activation(relu, Gf[q], ACT.Relu).then_inc(drained[q], 1)
                            act.wait_ge(drained[q], g * 4 + i + (D_OUT[q] + 1))
                            act.wait_ge(hid_v, g * 4 + i * 2 + (q + AHEAD))
                            own.done(act.activation(sqr, relu, ACT.Square))
                            act.activation(ahi[:, bass.ds(i * 8 + 4 * q, 4), S:2 * S],
                                           sqr.rearrange("p (c t) -> p c t", t=S), ACT.Copy).then_inc(hid_a, 1)
                with act.Fori(0, 2) as i:
                    for j in range(4, 20):
                        split(g * 64 + i * 16 + (U_MLP + 32), j)

            act.wait_ge(x_done, 2)
            rms_rows(2, x[:, 0, :], xs[:, 0, :])
            act.wait_ge(x_done, 3)
            rms_rows(3, x[:, 0, :], xs[:, 0, :])
            act.activation(xs[:, 0, :], x[:, 0, :], ACT.Copy, scale=rstd[:, 6:7]).then_inc(xs_ok, 1)
            act.wait_ge(ctx_in, 16)
            rms_rows(4, ctxr[:, 0, :], area(4096, D))
            act.activation(ctxr[:, 0, :], ctxr[:, 0, :], ACT.Copy, scale=rstd[:, 8:9]).then_inc(xs_ok, 1)
            act.wait_ge(coef_ok, 2)
            turn(3, 0, lambda k: coefs[:, k:k + 1], lambda k: mods[:, k:k + 1])
            turn(4, S, lambda k: coefs[:, 16 + k:17 + k], lambda k: modc[:, k:k + 1])

            def attend_a(i, m):
                if m < 4:
                    a = i * 4 + (m - 4)
                    act.wait_ge(n_nm, a + 1)
                    act.activation(pr[:, m % 2, :], pr[:, m % 2, :], ACT.Exp, bias=nst[:, 4 + m:5 + m],
                                   accum_out=nst[:, 8 + m:9 + m]).then_inc(n_p, 1)
                if 1 <= m <= 4:
                    T = m - 1
                    a = i * 4 + (T - 4)
                    act.wait_ge(n_tr, a + (1 + AHEAD))
                    act.wait_ge(n_o, a + (AHEAD - 1))
                    act.activation(pT[:, T % 2, :], X[2], ACT.Copy).then_inc(n_pt, 1)

            def inv_rms(i, r):
                v = nrs[:, 512 * (r % 2):512 * (r % 2) + 512]
                act.wait_ge(n_nsum, i * 3 + (r + 1))
                act.wait_ge(n_norm, i * 3 + ((1 if r == 2 else 0) + AHEAD))
                act.activation(v, X[2], ACT.Ln, scale=1.0 / NHD, bias=EPS).then_inc(n_rs, 1)
                act.wait_ge(n_rs, i * 6 + (2 * r + 1 + AHEAD))
                act.activation(v, v, ACT.Exp, scale=-0.5).then_inc(n_rs, 1)

            def na_turn(i, first):
                u0 = i * 12 + U_NA
                for m in range(12):
                    if not (first and m == 0):
                        split(u0, m + 3)
                    if m == 0 and not first:
                        act.wait_ge(unit_used, u0)
                        act.activation(vv, Gf[1].rearrange("p (c t) -> p c t", t=S), ACT.Copy).then_inc(drained[1], 1)
                    if not first:
                        attend_a(i, m)
                    if m == 4:
                        act.wait_ge(unit_used, u0 + 4)
                        act.activation(nsq, Gf[0], ACT.Square).then_inc(n_sq, 1)
                    if m == 6:
                        inv_rms(i, 0)
                    if m == 7:
                        inv_rms(i, 1)
                    if m == 8:
                        act.wait_ge(unit_used, u0 + 8)
                        act.activation(nsq[:, 0:512], X[0], ACT.Square).then_inc(n_sq, 1)
                    if m == 10:
                        inv_rms(i, 2)

            na_turn(0, True)
            with act.Fori(1, 8) as i:
                na_turn(i, False)
            split(U_WO, 3)
            act.wait_ge(unit_used, U_WO)
            act.activation(vv, Gf[1].rearrange("p (c t) -> p c t", t=S), ACT.Copy).then_inc(drained[1], 1)
            for m in range(6):
                attend_a(8, m)
            act.wait_ge(n_oc, NH + AHEAD)
            for k in range(KC):
                act.activation(ahi[:, k, S:2 * S], oT[:, k, :], ACT.Copy).then_inc(a_hi, 1)
            with act.Fori(0, 4) as n:
                for j in range(4, 12):
                    split(n * 8 + U_WO, j)

            act.wait_ge(x_done, 4)
            rms_rows(5, x[:, 0, :], xs[:, 0, :])
            act.activation(xs[:, 0, :], x[:, 0, :], ACT.Copy, scale=rstd[:, 10:11]).then_inc(xs_ok, 1)
            act.wait_ge(coef_ok, 3)
            turn(5, 0, lambda k: coefs[:, 32 + k:33 + k], lambda k: mods[:, 48 + k:49 + k])
            act.preload_act_table_set("silu_and_others")

            def conv_a(pair, q, nc_, used, n_local):
                act.wait_ge(unit_used, used)
                dst = (held, cvt)[q]
                act.wait_ge(f_v, pair * 4 + (AHEAD - 1 + 2 * q))
                for c in range(nc_):
                    at = C_CONV + q * FC + c
                    ins = act.activation(dst[:, S * c:S * c + S], Gf[q][:, S * c:S * c + S], ACT.Identity,
                                         scale=cols[:, bass.ds(pair * 4 + (at + 4 * FC), 1)],
                                         bias=cols[:, bass.ds(pair * 4 + at, 1)])
                ins.then_inc(f_a, 1)
                act.wait_ge(f_v, pair * 4 + (AHEAD + 1 + 2 * q))
                if q == 0:
                    v = held[:, 0:S * nc_]
                    act.activation(v, v, ACT.Silu).then_inc(f_a, 1)
                else:
                    act.activation(ahi[:, bass.ds(n_local * 4, nc_), S:2 * S],
                                   cvt[:, 0:S * nc_].rearrange("p (c t) -> p c t", t=S), ACT.Copy).then_inc(f_a, 1)

            def conv_pair(pair, u0, n_local, nc_):
                for j in range(4, 20):
                    split(u0, j)
                    if j == 11:
                        conv_a(pair, 0, nc_, u0 + 8, n_local)
                    if j == 19:
                        conv_a(pair, 1, nc_, u0 + 16, n_local)

            with act.Fori(0, 2) as g:
                with act.Fori(0, 4) as n:
                    conv_pair(g * 4 + n, g * 96 + n * 16 + U_FFN, n, 4)
                with act.Fori(0, 4) as n:
                    for j in range(4, 12):
                        split(g * 96 + n * 8 + (U_FFN + 64), j)
            with act.Fori(0, 2) as n:
                conv_pair(n + 8, n * 16 + U_LAST, n, 4)
            conv_pair(10, U_LAST + 32, 2, 3)
            for j in range(4, 24):
                split(U_DOWN, j)

        @block.vector
        def _(dve):
            own = Steps(dve, dve_step)
            for s_ in (n_t, n_oc, n_norm, f_v, hid_v):
                dve.sem_inc(s_, AHEAD)

            def f(ap):
                return ap.bitcast(F32)

            def split(u0, j, w=1024):
                s = j % RING
                dve.wait_ge(hi_done, u0 + (j + 1))
                a, b, c = wlo[:, s, :], raw[:, s, :], f(whi[:, s, :])
                if w < 1024:
                    a, b, c = (v.rearrange("p (k n) -> p k n", n=512)[:, 0:2, 0:w] for v in (a, b, c))
                dve.tensor_tensor(a, b, c, ALU.subtract).then_inc(lo_done, 1)

            def ss_rows(n, rows, junk):
                dve.tensor_tensor_reduce(junk, rows, rows, 1.0, 0.0, ALU.mult, ALU.add,
                                         ssum[:, 2 * n + 1:2 * n + 2]).then_inc(ss_a, 1)

            def scale_rows(n, dst, rows):
                dve.wait_ge(rstd_ok, n + 1)
                dve.tensor_scalar(dst, rows, rstd[:, 2 * n + 1:2 * n + 2], None, ALU.mult).then_inc(xs_ok, 1)

            def turn(e, off, gain, shift=None):
                for k in range(KC):
                    dve.wait_ge(a_hi, TURN_AT[e] + 2 * (k // 2) + 2)
                    z = X[(k // 2) % 4][:, (k % 2) * S:(k % 2) * S + S]
                    hi = f(ahi[:, k, off:off + S])
                    if shift:
                        v = turned_f[:, k % 2, :]
                        own.done(dve.tensor_scalar(v, z, gain(k), shift(k), ALU.mult, ALU.add))
                        dve.tensor_tensor(alo[:, k, off:off + S], v, hi, ALU.subtract).then_inc(a_lo, 1)
                    else:
                        dve.scalar_tensor_tensor(out=alo[:, k, off:off + S], in0=z, scalar=gain(k), in1=hi,
                                                 op0=ALU.mult, op1=ALU.subtract).then_inc(a_lo, 1)

            dve.wait_ge(x_in, 16)
            ss_rows(0, x[:, 1, :], xs[:, 1, :])
            scale_rows(0, xs[:, 1, :], x[:, 1, :])
            dve.wait_ge(colT, 1)
            dve.tensor_copy(cols[:, 0:C_CONV], X01[:, 0:C_CONV]).then_inc(cols_ok, 1)
            dve.tensor_copy(cols[:, C_CONV:NCOLS], X01[:, 512:512 + NCOLS - C_CONV]).then_inc(cols_ok, 1)
            dve.wait_ge(ft_mm, 1)
            dve.tensor_copy(fT[0:12, :], X[2][0:12, 0:S]).then_inc(ft_ok, 1)
            for m in range(3):
                split(0, m, 384)
            dve.wait_ge(cols_ok, 2)
            turn(0, 0, lambda k: cols[:, k:k + 1])
            cc = cols[:, 64:96]
            dve.wait_ge(cond_ok, 1)
            dve.scalar_tensor_tensor(out=cond[:, :], in0=cc, scalar=0.0, in1=cond[:, :],
                                     op0=ALU.min, op1=ALU.subtract).then_inc(cond_ok, 1)
            dve.wait_ge(cond_ok, 3)
            own.done(dve.tensor_tensor(cond[:, :], cond[:, :], cc, ALU.mult))
            dve.wait_ge(small_in, 48)
            own.done(dve.tensor_scalar(negsink, sink, -1.0, None, ALU.mult))

            def evac_in(n):
                if PANELS_IN[n][0] == "KV":
                    dve.wait_ge(unit_used, 8 * n + 8)
                    dve.wait_ge(drained[0], 4)
                    kk = skd.rearrange("p (c a) t -> p c a t", a=2)
                    for a in range(2):
                        dve.tensor_copy(kk[HD:P, :, a, :],
                                        G[0][HD * a:HD * a + HD, 0, :].rearrange("p (c t) -> p c t", t=S))\
                            .then_inc(drained[0], 1)

            def swa(part, s):
                n, c = divmod(s, 6)
                w, lo = (P, P) if n == 0 else (S, 0)
                i = 12 * n + 2 * c
                if part == "swa_a":
                    dve.wait_ge(w_s, s + 1)
                    if s == 0:
                        dve.wait_ge(bm_ok, 1)
                    if s >= 2:
                        dve.wait_ge(w_tr, s - 1)
                    for a in range(2):
                        ins = dve.scalar_tensor_tensor(out=swt[:, s % 2, a, 0:w], in0=X[a][:, 0:w], scalar=0.125,
                                                       in1=bm[:, 2 * c + a, lo:S], op0=ALU.mult, op1=ALU.add)
                    ins.then_inc(w_t, 1)
                    dve.wait_ge(w_t, s + 1)
                    own.done(dve.tensor_reduce(smax[:, i:i + 2], swt[:, s % 2, :, 0:w], AXX, ALU.max))
                    own.done(dve.scalar_tensor_tensor(out=snm[:, i:i + 2], in0=smax[:, i:i + 2], scalar=-1.0,
                                                      in1=negsink[:, 2 * c:2 * c + 2], op0=ALU.mult, op1=ALU.min))
                    dve.tensor_tensor(ses[:, i:i + 2], snm[:, i:i + 2], sink[:, 2 * c:2 * c + 2], ALU.add)\
                        .then_inc(w_nm, 1)
                elif part == "swa_b":
                    dve.wait_ge(w_p, 3 * s + 3)
                    own.done(dve.tensor_tensor(sden[:, i:i + 2], sden[:, i:i + 2], ses[:, i:i + 2], ALU.add))
                    own.done(dve.reciprocal(sden[:, i:i + 2], sden[:, i:i + 2]))
                else:
                    dve.wait_ge(w_o, s + 1)
                    for a in range(2):
                        h = 2 * c + a
                        ins = dve.tensor_scalar(x[:, n, HD * h:HD * h + HD], X[3][:, HD * a:HD * a + HD],
                                                sden[:, i + a:i + a + 1], None, ALU.mult)
                    ins.then_inc(w_out_ok, 1)

            def gla_v(n):
                gd = gla
                if n == 0:
                    dve.wait_ge(gd["gate"], 1)
                    dve.wait_ge(gd["l"], 1)
                    for h in range(4):
                        own.mark(dve.tensor_scalar(g2[0:DK, h, :], X01[0:DK, S * h:S * h + S],
                                                   cols[0:DK, C_GATEB + h:C_GATEB + h + 1], 0.0, ALU.add, ALU.min))
                    own.wait()
                    own.done(dve.tensor_tensor(g2[0:DK], g2[0:DK], g1[0:DK], ALU.subtract))
                    own.done(dve.tensor_scalar(g2[0:DK], g2[0:DK], 1.0 / 16.0, -1.0, ALU.mult, ALU.max))
                    for h in range(4):
                        ins = dve.tensor_tensor_scan(g1[0:DK, h, :], C("reset")[0:DK, :], g2[0:DK, h, :], 0.0,
                                                     ALU.mult, ALU.add)
                    ins.then_inc(gd["b"], 1)
                    dve.wait_ge(gd["b"], 1)
                    dve.wait_ge(gd["eb"], 3)
                    own.done(dve.scalar_tensor_tensor(out=gq[0:DK], in0=gq[0:DK], scalar=float(DK) ** -0.5,
                                                      in1=g2[0:DK], op0=ALU.mult, op1=ALU.mult))
                    own.done(dve.tensor_tensor(g3[0:DK], g3[0:DK], gk[0:DK], ALU.mult))
                    b4 = g1[0:DK].rearrange("p h (c t) -> p (h c) t", t=CH)
                    o4 = g2[0:DK].rearrange("p h (c t) -> p (h c) t", t=CH)
                    last = b4[:, :, CH - 1:CH].to_broadcast([DK, 16, CH])
                    dve.tensor_tensor(o4, last, b4, ALU.subtract).then_inc(gd["d"], 1)
                    dve.wait_ge(gd["ke"], 1)
                    dve.tensor_tensor(g2[0:DK], g2[0:DK], gk[0:DK], ALU.mult).then_inc(gd["ki"], 1)
                if n == 1:
                    for r in range(RT):
                        dve.wait_ge(gd["sc"], r + 1)
                        dve.tensor_tensor(scT[:, r], X[r].rearrange("p (h t) -> p h t", t=P),
                                          C("glamask").unsqueeze(1).to_broadcast([P, 4, P]), ALU.mult)\
                            .then_inc(gd["scm"], 1)
                if n in (4, 5, 6):
                    c = n - 4
                    dve.wait_ge(gd["ds"], c + 1)
                    for h in range(4):
                        src = ps[0:DK, 6 + h // 2, DV * (h % 2):DV * (h % 2) + DV]
                        dst = state[0:DK, DV * h:DV * h + DV]
                        if c == 0:
                            ins = dve.tensor_copy(dst, src)
                        else:
                            ins = dve.scalar_tensor_tensor(out=dst, in0=dst, scalar=dec[0:DK, 4 * h + c:4 * h + c + 1],
                                                           in1=src, op0=ALU.mult, op1=ALU.add)
                    ins.then_inc(gd["st"], 1)
                    dve.wait_ge(gd["st"], c + 1)
                if n in (5, 6, 7):
                    c = n - 4
                    dve.wait_ge(gd["inter"], c)
                    dve.wait_ge(gd["ic"], 2)
                    p0 = CH * (c % 2)
                    m = x[p0:p0 + CH, c // 2, SWA_W:SWA_W + 768].rearrange("p (a b) -> p a b", a=2)
                    dve.tensor_tensor(m, m, ps[p0:p0 + CH, 4:6, 0:384], ALU.add).then_inc(gd["add"], 1)

            for m in range(8 * len(PANELS_IN)):
                n, j = divmod(m + 3, 8)
                split(8 * n, j, PANELS_IN[n][2] if n < len(PANELS_IN) else 1024)
                if m % 8 == 0 and m:
                    evac_in(m // 8 - 1)
                for part, s in PLAN.get(m, []):
                    swa(part, s) if part != "gla" else gla_v(s)
            split(U_OUT, 3)

            for c in range(4):
                dve.wait_ge(sbs["l"], c + 1)
                zz = ps[:, 4:6, 0:384]
                own.done(dve.tensor_scalar(sb_z[:, :, :], zz, 0.125, None, ALU.mult))
                own.done(dve.scalar_tensor_tensor(out=sb_p[:, :, :], in0=sb_z[:, :, :], scalar=0.0, in1=sb_l[:, :, :],
                                                  op0=ALU.max, op1=ALU.add))
                st = C("strict").unsqueeze(1).to_broadcast([P, 2, P])
                own.mark(dve.tensor_tensor(sb_p[:, :, 0:P], sb_p[:, :, 0:P], st, ALU.mult))
                dve.tensor_tensor(sb_p[:, :, S:384], sb_p[:, :, S:384], st, ALU.mult).then_inc(sbs["p"], 1)
                dve.wait_ge(sbs["c"], c + 1)
                own.done(dve.tensor_tensor(sb_w[:, :, :], sb_z[:, :, :], ps[:, 6:8, 0:384], ALU.subtract))
                ng = C("negstrict").unsqueeze(1).to_broadcast([P, 2, P])
                own.mark(dve.tensor_tensor(sb_w[:, :, 0:P], sb_w[:, :, 0:P], ng, ALU.add))
                dve.tensor_tensor(sb_w[:, :, S:384], sb_w[:, :, S:384], ng, ALU.add).then_inc(sbs["arg"], 1)

            jk = (area(13056, 768), area(13824, 768))
            sg = area(11520, RT, 768)
            dve.wait_ge(sbs["out"], 8)
            for r in range(RT):
                own.done(dve.tensor_tensor_reduce(jk[0], x[:, r, 0:768], x[:, r, 0:768], 1.0, 0.0, ALU.mult, ALU.add,
                                                  mss[:, r:r + 1]))
                own.done(dve.tensor_tensor_reduce(jk[0][:, 0:512], x[:, r, 1536:D], x[:, r, 1536:D], 1.0, 0.0,
                                                  ALU.mult, ALU.add, mss[:, 10 + r:11 + r]))
                own.done(dve.tensor_tensor(jk[1], x[:, r, 768:1536], x[:, r, 768:1536], ALU.mult))
                ins = dve.tensor_reduce(mss[:, 2 + 4 * r:6 + 4 * r], jk[1].rearrange("p (h v) -> p h v", h=4), AXX, ALU.add)
            ins.then_inc(mix_v, 1)
            dve.wait_ge(mix_v, 1)
            dve.wait_ge(mix_a, 2)
            dve.scalar_tensor_tensor(out=sg, in0=br, scalar=0.0, in1=sg, op0=ALU.min, op1=ALU.subtract)\
                .then_inc(mix_v, 1)
            for r in range(RT):
                own.mark(dve.tensor_scalar(x[:, r, 0:768], x[:, r, 0:768], mrs[:, r:r + 1], None, ALU.mult))
                own.mark(dve.tensor_scalar(x[:, r, 1536:D], x[:, r, 1536:D], mrs[:, 10 + r:11 + r], None, ALU.mult))
                for h in range(4):
                    v = x[:, r, 768 + DV * h:768 + DV * h + DV]
                    own.mark(dve.scalar_tensor_tensor(out=v, in0=v, scalar=mrs[:, 2 + 4 * r + h:3 + 4 * r + h],
                                                      in1=br[:, r, DV * h:DV * h + DV], op0=ALU.mult, op1=ALU.mult))
            own.wait()
            dve.wait_ge(mix_a, 3)
            dve.tensor_tensor(x[:, :, 768:1536], x[:, :, 768:1536], sg, ALU.mult).then_inc(mix_v, 1)
            turn(1, S, lambda k: cols[:, R_MIXG + k:R_MIXG + k + 1])

            def add_panel(n, q, used, done):
                dve.wait_ge(unit_used, used)
                v = x[:, :, bass.ds(n * 512, 512)]
                dve.tensor_tensor(v, v, G[q], ALU.add).then_inc(done, 1)

            dve.wait_ge(x_again, 16)
            with dve.Fori(0, 2) as i:
                for j in range(4, 20):
                    split(i * 16 + U_OUT, j)
                    if j % 8 == 3:
                        q = j // 8 - 1
                        add_panel(i * 2 + q, q, i * 16 + (U_OUT + 8 * q + 8), drained[q])
            for q in range(2):
                dve.wait_ge(drained[q], D_OUT[q])
            dve.sem_inc(x_done, 1)

            ss_rows(1, x[:, 1, :], xs[:, 1, :])
            scale_rows(1, xs[:, 1, :], x[:, 1, :])
            turn(2, 0, lambda k: cols[:, 16 + k:17 + k])

            def ada_term(s, k, piece, acc, c, first):
                sc = cond[:, c + k:c + k + 1]
                if first:
                    return dve.tensor_scalar(acc, piece, sc, None, ALU.mult)
                return dve.scalar_tensor_tensor(out=acc, in0=piece, scalar=sc, in1=acc, op0=ALU.mult, op1=ALU.add)

            def ada_slot(s, ks):
                for k in ks:
                    q = k // 4
                    if k % 4 == 0:
                        dve.wait_ge(ada_in[q], s * 16 + 16)
                    own.done(ada_term(s, k, ada1[:, q, k % 4, :], accL, 0, k == 0))
                    ins = ada_term(s, k, ada1[:, q, k % 4, :], accC, 16, k == 0)
                    if k % 4 == 3:
                        ins.then_inc(ada_done, 1)
                        dve.wait_ge(ada_done, s * 4 + (q + 1))
                    else:
                        own.done(ins)

            def mlp_pair(g, i, up):
                u0 = g * 64 + i * 16 + (U_MLP if up else U_MLP + 32)
                s = g * 4 + i + (0 if up else 2)
                for j in range(4, 20):
                    split(u0, j)
                    slot = j - 3
                    ada_slot(s, [0, 1] if slot == 1 else [slot] if slot < 16 else [])
                    if j % 8 == 3:
                        q = j // 8 - 1
                        if up:
                            dve.wait_ge(hid_a, g * 4 + i * 2 + (q + 1))
                            dve.tensor_tensor(alo[:, bass.ds(i * 8 + 4 * q, 4), S:2 * S],
                                              sqr.rearrange("p (c t) -> p c t", t=S),
                                              f(ahi[:, bass.ds(i * 8 + 4 * q, 4), S:2 * S]), ALU.subtract).then_inc(hid_v, 1)
                        else:
                            add_panel(i * 2 + q, q, u0 + (8 * q + 8), drained[q])
                dve.wait_ge(ada_mm, s + 1)
                own.mark(dve.tensor_copy(mods[:, bass.ds(s * 3, 3)], X[0][:, 0:3]))
                dve.tensor_copy(modc[:, bass.ds(s * 3, 3)], X[0][:, 4:7]).then_inc(ada_col, 1)

            with own.loop(0, 4, 4 * 29) as g:
                with own.loop(0, 2, 29) as i:
                    mlp_pair(g, i, True)
                with own.loop(0, 2, 29) as i:
                    mlp_pair(g, i, False)
            for q in range(2):
                dve.wait_ge(drained[q], D_MLP[q])
            dve.sem_inc(x_done, 1)

            ss_rows(2, x[:, 1, :], xs[:, 1, :])
            dve.wait_ge(rstd_ok, 3)
            dve.wait_ge(nf_in, 16)
            for r in range(RT):
                own.mark(dve.scalar_tensor_tensor(out=x[:, r, :], in0=x[:, r, :], scalar=rstd[:, 4 + r:5 + r], in1=nfin,
                                                  op0=ALU.mult, op1=ALU.mult))
            own.wait()
            dve.sem_inc(x_done, 1)
            ss_rows(3, x[:, 1, :], xs[:, 1, :])
            dve.wait_ge(ada_col, 16)
            own.mark(dve.tensor_tensor(mods[:, 0:48], mods[:, 0:48], cols[:, C_ADAB:C_ADAB + 48], ALU.add))
            own.done(dve.tensor_tensor(modc[:, 0:48], modc[:, 0:48], cols[:, C_ADAB:C_ADAB + 48], ALU.add))
            for v, o in ((mods, 0), (modc, 16)):
                dve.scalar_tensor_tensor(out=coefs[:, o:o + 16], in0=v[:, 16:32], scalar=1.0, in1=cols[:, 32:48],
                                         op0=ALU.add, op1=ALU.mult).then_inc(coef_ok, 1)
            scale_rows(3, xs[:, 1, :], x[:, 1, :])
            dve.wait_ge(ctx_in, 16)
            ss_rows(4, ctxr[:, 1, :], area(6144, D))
            scale_rows(4, ctxr[:, 1, :], ctxr[:, 1, :])
            dve.wait_ge(coef_ok, 2)
            turn(3, 0, lambda k: coefs[:, k:k + 1], lambda k: mods[:, k:k + 1])
            turn(4, S, lambda k: coefs[:, 16 + k:17 + k], lambda k: modc[:, k:k + 1])

            def spread(n, at):
                for b in range(4):
                    v = gdiag
                    if b:
                        dve.wait_ge(gb_mm, 4 * n + b)
                    for c in range(4):
                        own.mark(dve.tensor_scalar(v[:, P * c:P * c + P], ident, mods[:, at + 4 * b + c:at + 4 * b + c + 1],
                                                   None, ALU.mult))
                    own.wait()
                    dve.sem_inc(gb_ok, 1)
                    dve.wait_ge(gb_mm, 4 * n + b + 1)
                    dve.tensor_copy(gb[:, 512 * b:512 * b + 512], X[0]).then_inc(gb_rd, 1)
                    dve.wait_ge(gb_rd, 4 * n + b + 1)

            spread(0, 32)

            KG, QG = cols[:, R_KG:R_KG + 1], cols[:, R_QG:R_QG + 1]

            def attend_v(i, m):
                if m < 4:
                    a = i * 4 + (m - 4)
                    hh, qb = m // 2, m % 2
                    if m == 0:
                        dve.wait_ge(n_eh, i * 16)
                    dve.wait_ge(n_s, a + 1)
                    dve.wait_ge(n_tr, a + (AHEAD - 1))
                    v = pr[:, m % 2, :]
                    e0 = GRID * (2 - 2 * qb)
                    own.mark(dve.scalar_tensor_tensor(out=v[:, 0:S], in0=X[1][:, 0:S], scalar=NA_SCALE,
                                                      in1=eh[:, hh, e0:e0 + S], op0=ALU.mult, op1=ALU.add))
                    dve.tensor_scalar(v[:, S:2 * S], X[1][:, S:2 * S], NA_SCALE, None, ALU.mult).then_inc(n_t, 1)
                    dve.wait_ge(n_t, a + (1 + AHEAD))
                    own.done(dve.tensor_reduce(nst[:, m:m + 1], v, AXX, ALU.max))
                    dve.tensor_scalar(nst[:, 4 + m:5 + m], nst[:, m:m + 1], -1.0, None, ALU.mult).then_inc(n_nm, 1)
                    dve.wait_ge(n_p, a + 1)
                    own.done(dve.reciprocal(nst[:, 12 + m:13 + m], nst[:, 8 + m:9 + m]))
                    dve.tensor_scalar(dg[:, m % 2, :], ident, nst[:, 12 + m:13 + m], None, ALU.mult).then_inc(n_dg, 1)
                if m in (3, 5):
                    hh = (m - 3) // 2
                    dve.wait_ge(n_o, i * 4 + (m - 5 + AHEAD))
                    dve.tensor_copy(oT[:, bass.ds(i * 2 + (hh - 2), 1), :], X[3][:, 0:S].unsqueeze(1)).then_inc(n_oc, 1)

            def norm(i, r):
                dve.wait_ge(n_rs, i * 6 + (2 * r + 2 + AHEAD))
                if r < 2:
                    dve.scalar_tensor_tensor(out=kT[:, r, :], in0=Gf[0][:, 512 * r:512 * r + 512], scalar=KG,
                                             in1=nrs[:, 512 * r:512 * r + 512], op0=ALU.mult, op1=ALU.mult)\
                        .then_inc(n_norm, 1)
                else:
                    dve.scalar_tensor_tensor(out=qT.rearrange("p a b -> p (a b)"), in0=X[0], scalar=QG,
                                             in1=nrs[:, 0:512], op0=ALU.mult, op1=ALU.mult).then_inc(n_norm, 1)

            def ada_tail(i, slot):
                ks = ([3 * slot + c for c in range(3)] if slot < 4 else [8 + slot] if slot < 8 else
                      [16 + 4 * (slot - 8) + c for c in range(4)])
                for kk in ks:
                    s, k = divmod(kk, 16)
                    q = kk // 4
                    if k % 4 == 0:
                        dve.wait_ge(ada_in[q % 2], i * 64 + (16 * 16 + 16 * (q // 2) + 16))
                    ins = ada_term(s, k, ada2[:, q % 2, k % 4, :], (acc2, acc3[:, :])[s], 0, k == 0)
                    if k % 4 == 3:
                        ins.then_inc(ada_done, 1)
                        dve.wait_ge(ada_done, i * 8 + (64 + q + 1))
                    else:
                        own.done(ins)

            def ada_out(i, s):
                dve.wait_ge(ada_mm, i * 2 + (16 + s + 1))
                dve.tensor_copy(mods[:, bass.ds(i * 6 + (48 + 3 * s), 3)], X[1][:, 4 * s:4 * s + 3]).then_inc(ada_col, 1)

            def na_turn(i, first):
                u0 = i * 12 + U_NA
                for m in range(12):
                    if m == 0 and not first:
                        ada_out(i - 1, 1)
                    if not (first and m == 0):
                        split(u0, m + 3)
                    if not first:
                        attend_v(i, m)
                    ada_tail(i, m)
                    if m in (6, 7):
                        norm(i, m - 6)
                    if m == 10:
                        norm(i, 2)
                        ada_out(i, 0)

            na_turn(0, True)
            with own.loop(1, 8, NA_OWN) as i:
                na_turn(i, False)
            ada_out(7, 1)
            split(U_WO, 3)
            for m in range(6):
                attend_v(8, m)
            for k in range(KC):
                dve.wait_ge(a_hi, OT_AT + k + 1)
                dve.tensor_tensor(alo[:, k, S:2 * S], oT[:, k, :], f(ahi[:, k, S:2 * S]), ALU.subtract).then_inc(a_lo, 1)
            dve.wait_ge(ada_col, 32)
            own.done(dve.tensor_tensor(mods[:, 48:96], mods[:, 48:96], cols[:, C_ADAB + 48:C_ADAB + 96], ALU.add))
            dve.scalar_tensor_tensor(out=coefs[:, 32:48], in0=mods[:, 64:80], scalar=1.0, in1=cols[:, 48:64],
                                     op0=ALU.add, op1=ALU.mult).then_inc(coef_ok, 1)

            def add_gated(n, q, used, done, count):
                dve.wait_ge(unit_used, used)
                gg = gb[:, bass.ds(n * 512, 512)].unsqueeze(1).to_broadcast([P, RT, 512])
                v = x[:, :, bass.ds(n * 512, 512)]
                tt = tmp.rearrange("p (r n) -> p r n", r=RT)
                dve.tensor_tensor(tt, G[q], gg, ALU.mult).then_inc(done, 1)
                dve.wait_ge(done, count)
                own.done(dve.tensor_tensor(v, v, tt, ALU.add))

            with own.loop(0, 2, 2) as i:
                for j in range(4, 20):
                    split(i * 16 + U_WO, j)
                    if j % 8 == 3:
                        q = j // 8 - 1
                        add_gated(i * 2 + q, q, i * 16 + (U_WO + 8 * q + 8), drained[q], i + (D_NA[q] + 1))
            dve.sem_inc(x_done, 1)

            ss_rows(5, x[:, 1, :], xs[:, 1, :])
            scale_rows(5, xs[:, 1, :], x[:, 1, :])
            dve.wait_ge(coef_ok, 3)
            turn(5, 0, lambda k: coefs[:, 32 + k:33 + k], lambda k: mods[:, 48 + k:49 + k])
            spread(1, 80)

            def conv_v(pair, q, nc_, n_local, done):
                dst = (held, cvt)[q]
                dve.wait_ge(f_a, pair * 4 + (1 + 2 * q))
                for tap in (0, 2):
                    for c in range(nc_):
                        z = Gf[q][:, S * c:S * c + S]
                        v = dst[:, S * c:S * c + S]
                        w = cols[:, bass.ds(pair * 4 + (C_CONV + 2 * FC * (1 + tap) + q * FC + c), 1)]
                        a, b = (v[:, 1:S], z[:, 0:S - 1]) if tap == 0 else (v[:, 0:S - 1], z[:, 1:S])
                        ins = dve.scalar_tensor_tensor(out=a, in0=b, scalar=w, in1=a, op0=ALU.mult, op1=ALU.add)
                    if tap == 0:
                        own.done(ins)
                ins.then_inc(f_v, 1)
                dve.wait_ge(f_v, pair * 4 + (AHEAD + 1 + q))
                dve.sem_inc(done, 1)
                if q == 1:
                    w = S * nc_
                    dve.wait_ge(f_a, pair * 4 + 3)
                    dve.tensor_tensor(cvt[:, 0:w], cvt[:, 0:w], held[:, 0:w], ALU.mult).then_inc(f_v, 1)
                    dve.wait_ge(f_a, pair * 4 + 4)
                    dve.tensor_tensor(alo[:, bass.ds(n_local * 4, nc_), S:2 * S],
                                      cvt[:, 0:w].rearrange("p (c t) -> p c t", t=S),
                                      f(ahi[:, bass.ds(n_local * 4, nc_), S:2 * S]), ALU.subtract).then_inc(f_v, 1)

            def conv_pair(pair, u0, n_local, nc_):
                for j in range(4, 20):
                    split(u0, j)
                    if j == 11:
                        conv_v(pair, 0, nc_, n_local, drained[0])
                    if j == 19:
                        conv_v(pair, 1, nc_, n_local, drained[1])

            with own.loop(0, 2, 12) as g:
                with own.loop(0, 4, 2) as n:
                    conv_pair(g * 4 + n, g * 96 + n * 16 + U_FFN, n, 4)
                with own.loop(0, 2, 2) as n:
                    for j in range(4, 20):
                        split(g * 96 + n * 16 + (U_FFN + 64), j)
                        if j % 8 == 3:
                            q = j // 8 - 1
                            add_gated(n * 2 + q, q, g * 96 + n * 16 + (U_FFN + 64 + 8 * q + 8), drained[q],
                                      g * 6 + n + (D_WO[q] + 4 + 1))
            with own.loop(0, 2, 2) as n:
                conv_pair(n + 8, n * 16 + U_LAST, n, 4)
            conv_pair(10, U_LAST + 32, 2, 3)
            for j in range(4, 24):
                split(U_DOWN, j)
                if j % 6 == 3:
                    n = j // 6 - 1
                    add_gated(n, n % 2, U_DOWN + 6 * n + 6, drained[n % 2], D_F1[n % 2] + 3 + n // 2 + 1)
            add_gated(3, 1, U_DOWN + 24, drained[1], D_F1[1] + 3 + 2)
            dve.sem_inc(x_done, 1)

        @block.tensor
        def _(pe):
            pe.sem_inc(n_tr, AHEAD)
            pe.sem_inc(n_o, AHEAD)

            def kn(v, j):
                return v[:, j % RING, :].rearrange("p (k n) -> p k n", n=512)

            def terms(w_hi, w_lo, a_hi_, a_lo_, weights_left):
                for w, a in ((w_hi, a_hi_), (w_hi, a_lo_), (w_lo, a_hi_)):
                    yield (w, a) if weights_left else (a, w)

            def columns(o, j, kk, c0, k, t0, tn, start, last):
                n = o.shape[0]
                wh, wl = kn(whi, j)[:, kk, c0:c0 + n], kn(wlo, j)[:, kk, c0:c0 + n]
                for i, (a, b) in enumerate(terms(wh, wl, ahi[:, k, t0:t0 + tn], alo[:, k, t0:t0 + tn], True)):
                    ins = pe.matmul(o, a, b, start=start and i == 0, stop=last and i == 2, skip_group_check=True)
                return ins

            def rows(o, j, kk, c0, k, t0, start, last):
                n = o.shape[1]
                wh, wl = kn(whi, j)[:, kk, c0:c0 + n], kn(wlo, j)[:, kk, c0:c0 + n]
                for i, (a, b) in enumerate(terms(wh, wl, ahi[:, k, t0:t0 + P], alo[:, k, t0:t0 + P], False)):
                    ins = pe.matmul(o, a, b, start=start and i == 0, stop=last and i == 2, skip_group_check=True)
                return ins

            def unit_columns(u0, j, q, nc_, k0, t0, kc=KC, kper=2, width=P):
                pe.wait_ge(lo_done, u0 + (j + 1))
                for kk in range(kper):
                    k = k0 + kk
                    for c in range(nc_):
                        o = Gf[q][0:width, S * c:S * c + S]
                        ins = columns(o, j, kk, width * c, k, t0, S, k == 0 and c % 2 == 0, k == kc - 1)
                ins.then_inc(unit_used, 1)

            def unit_rows(u0, j, q, k0, t0, kc=KC, kper=2, w=512):
                pe.wait_ge(lo_done, u0 + (j + 1))
                for kk in range(kper):
                    k = k0 + kk
                    for r in range(RT):
                        ins = rows(G[q][:, r, 0:w], j, kk, 0, k, t0 + P * r, k == 0, k == kc - 1)
                ins.then_inc(unit_used, 1)

            def turn_rows(e, src, ready):
                for w in ready:
                    pe.wait_ge(*w)
                for kp in range(8):
                    if kp >= 4:
                        pe.wait_ge(a_lo, TURN_AT[e] + 2 * (kp - 4) + 2)
                    for c in range(2):
                        for r in range(RT):
                            k = 2 * kp + c
                            o = X[kp % 4][:, c * S + P * r:c * S + P * r + P]
                            ins = pe.transpose(o, src[:, r, P * k:P * k + P], ident)
                    ins.then_inc(turned, 1)

            pe.wait_ge(cst_in, 16)
            pe.wait_ge(rows_in, 16 * NROWS_DMA)
            pe.wait_ge(pool_step, 1)
            pe.transpose(X01[:, 0:114], colrow[0:114, 0, :], ident[0:114, 0:114])
            pe.transpose(X01[:, C_ADAB:C_ADAB + 96], colrow[0:96, 1, :], ident[0:96, 0:96])
            pe.transpose(X01[:, C_GATEB:C_GATEB + 4], colrow[0:4, 2, :], ident[0:4, 0:4])
            for i in range(4):
                ins = pe.transpose(X01[:, 512 + 2 * FC * i:512 + 2 * FC * (i + 1)], colrow[0:2 * FC, 3 + i, :],
                                   ident[0:2 * FC, 0:2 * FC])
            ins.then_inc(colT, 1)
            pe.wait_ge(small_in, 48)
            pe.matmul(X[2][0:12, 0:S], relb[0:32, :], C("bucket")[0:32, :], start=True, stop=True).then_inc(ft_mm, 1)
            turn_rows(0, xs, [(xs_ok, 2), (cols_ok, 2), (ft_ok, 1)])

            def swa(part, s):
                n, c = divmod(s, 6)
                w = P if n == 0 else S
                if part == "swa_a":
                    if s == 0:
                        pe.wait_ge(drained[0], 6)
                        pe.wait_ge(drained[1], 1)
                        pe.wait_ge(a_lo, KC)
                    else:
                        pe.wait_ge(w_t, s)
                    for a in range(2):
                        p0 = HD * a
                        ins = pe.matmul(X[a][:, 0:w], sq_[p0:p0 + HD, c, P * n:P * n + P],
                                        skd[p0:p0 + HD, (2 * c + a) // 3, 0:w], start=True, stop=True)
                    ins.then_inc(w_s, 1)
                elif part == "swa_b":
                    pe.wait_ge(w_p, 3 * s + 3)
                    if s:
                        pe.wait_ge(w_pt, s)
                    for a in range(2):
                        for b in range(w // P):
                            ins = pe.transpose(X[2][:, a * w + P * b:a * w + P * b + P],
                                               swt[:, s % 2, a, P * b:P * b + P], ident)
                    ins.then_inc(w_tr, 1)
                else:
                    pe.wait_ge(w_pt, s + 1)
                    if s:
                        pe.wait_ge(w_out_ok, s)
                    for a in range(2):
                        kv = (2 * c + a) // 3
                        for b in range(w // P):
                            ins = pe.matmul(X[3][:, HD * a:HD * a + HD], swp[:, s % 2, a * w + P * b:a * w + P * b + P],
                                            sv[:, b, HD * kv:HD * kv + HD], start=(b == 0), stop=(b == w // P - 1))
                    ins.then_inc(w_o, 1)

            def gla_p(n):
                gd = gla
                if n == 0:
                    pe.wait_ge(in_ready, 1)
                    pe.wait_ge(w_t, 12)
                    for h in range(4):
                        ins = pe.matmul(X01[0:DK, S * h:S * h + S], gw[0:LR, DK * h:DK * h + DK], lrT[0:LR, :],
                                        start=(h % 2 == 0), stop=True, skip_group_check=True)
                    ins.then_inc(gd["gate"], 1)
                if n == 1:
                    pe.wait_ge(gd["ki"], 1)
                    pe.wait_ge(w_out_ok, 12)
                    for r in range(RT):
                        for h in range(4):
                            ins = pe.transpose(X[2 + r][:, DK * h:DK * h + DK], g2[0:DK, h, P * r:P * r + P], ident[0:DK, 0:DK])
                        ins.then_inc(gd["turn"], 1)
                    for r in range(RT):
                        for h in range(4):
                            ins = pe.matmul(X[r][:, P * h:P * h + P], g3[0:DK, h, P * r:P * r + P],
                                            gq[0:DK, h, P * r:P * r + P], start=True, stop=True)
                        ins.then_inc(gd["sc"], 1)
                if n in (2, 3):
                    r = n - 2
                    if r == 0:
                        pe.wait_ge(drained[0], 9)
                        pe.wait_ge(drained[1], 4)
                        pe.wait_ge(gd["scm"], 2)
                    else:
                        pe.wait_ge(gd["ic"], 1)
                    for h in range(4):
                        ins = pe.matmul(ps[:, 4 + h // 2, DV * (h % 2):DV * (h % 2) + DV], scT[:, r, h, :],
                                        bv[:, r, DV * h:DV * h + DV], start=True, stop=True)
                    ins.then_inc(gd["intra"], 1)
                if n in (5, 6, 7):
                    c = n - 4
                    p0 = CH * (c % 2)
                    pe.wait_ge(gd["st"], c)
                    if c == 1:
                        pe.wait_ge(gd["ic"], 2)
                    else:
                        pe.wait_ge(gd["add"], c - 1)
                    for h in range(4):
                        ins = pe.matmul(ps[p0:p0 + CH, 4 + h // 2, DV * (h % 2):DV * (h % 2) + DV],
                                        gq[0:DK, h, CH * c:CH * c + CH], state[0:DK, DV * h:DV * h + DV],
                                        start=True, stop=True)
                    ins.then_inc(gd["inter"], 1)
                if n in (4, 5, 6):
                    c = n - 4
                    p0 = CH * (c % 2)
                    pe.wait_ge(gd["kend"], 2)
                    for h in range(4):
                        ins = pe.matmul(ps[0:DK, 6 + h // 2, DV * (h % 2):DV * (h % 2) + DV],
                                        kend[p0:p0 + CH, c // 2, DK * h:DK * h + DK], bv[p0:p0 + CH, c // 2, DV * h:DV * h + DV],
                                        start=True, stop=True)
                    ins.then_inc(gd["ds"], 1)

            before = {0: 0, 1: 0}
            for m in range(8 * len(PANELS_IN)):
                n, j = divmod(m, 8)
                name, _, w = PANELS_IN[n]
                q = n % 2
                u0 = 8 * n
                if j == 0:
                    if n >= 2:
                        pe.wait_ge(drained[q], before[q])
                    before[q] += 5 if name == "KV" else 1
                if n == 0:
                    pe.wait_ge(a_lo, 2 * j + 2)
                if name in ("Q0", "Q1"):
                    unit_columns(u0, j, q, 3, 2 * j, 0)
                elif name == "KV":
                    pe.wait_ge(lo_done, u0 + j + 1)
                    for kk in range(2):
                        k = 2 * j + kk
                        for c in range(2):
                            columns(Gf[q][:, S * c:S * c + S], j, kk, P * c, k, 0, S, k == 0 and c == 0, k == KC - 1)
                        for r in range(RT):
                            ins = rows(G[q][:, 1, S * r:S * r + S], j, kk, S, k, P * r, k == 0 and r == 0, k == KC - 1)
                    ins.then_inc(unit_used, 1)
                elif name in ("GQ", "GK"):
                    unit_columns(u0, j, q, 4, 2 * j, 0, width=DK)
                elif name == "BR1":
                    pe.wait_ge(lo_done, u0 + j + 1)
                    for kk in range(2):
                        k = 2 * j + kk
                        for r in range(RT):
                            rows(G[q][:, r, 0:384], j, kk, LR, k, P * r, k == 0, k == KC - 1)
                            ins = columns(G[q][:, r, 384:512], j, kk, 0, k, P * r, P, False, k == KC - 1)
                    ins.then_inc(unit_used, 1)
                elif name in ("CQ", "CK"):
                    unit_columns(u0, j, q, 4, 2 * j, 0)
                else:
                    unit_rows(u0, j, q, 2 * j, 0, w=w)
                for part, s in PLAN.get(m, []):
                    swa(part, s) if part != "gla" else gla_p(s)

            for c in range(4):
                if c == 0:
                    pe.wait_ge(drained[0], D0_IN)
                    pe.wait_ge(drained[1], D1_IN)
                    pe.wait_ge(gla["add"], 3)
                else:
                    pe.wait_ge(sbs["p"], c)
                for a in range(2):
                    p0 = HD * a
                    pe.matmul(X[a][:, 0:S], ck[p0:p0 + HD, c, 0:P], cq[p0:p0 + HD, c, :], start=True, stop=True)
                    ins = pe.matmul(X[a][:, S:384], ck[p0:p0 + HD, c, P:S], cq[p0:p0 + HD, c, P:S], start=True, stop=True)
                ins.then_inc(sbs["z"], 1)
                pe.wait_ge(sbs["p"], c + 1)
                if c:
                    pe.wait_ge(sbs["out"], 2 * c)
                for a in range(2):
                    pe.matmul(X[2 + a][:, 0:384], C("tri"), sb_p[:, a, :], start=True, stop=False, skip_group_check=True)
                    ins = pe.matmul(X[2 + a][:, P:S], ones, sb_p[:, a, S:384], start=False, stop=True, skip_group_check=True)
                ins.then_inc(sbs["c"], 1)
                pe.wait_ge(sbs["w"], c + 1)
                for a in range(2):
                    h = 2 * c + a
                    vcol = slice(HD * h, HD * h + HD)
                    pe.matmul(X[2][:, 384 + HD * a:448 + HD * a], sb_w[:, a, 0:P], cv[:, 0, vcol], start=True, stop=True)
                    o = X[3][:, 384 + HD * a:448 + HD * a]
                    pe.matmul(o, sb_w[:, a, P:S], cv[:, 0, vcol], start=True, stop=False)
                    ins = pe.matmul(o, sb_w[:, a, S:384], cv[:, 1, vcol], start=False, stop=True)
                ins.then_inc(sbs["o"], 1)

            turn_rows(1, x, [(mix_v, 3), (sbs["out"], 8)])
            pe.wait_ge(a_lo, TURN_AT[2])
            with pe.Fori(0, 2) as i:
                for q in range(2):
                    pe.wait_ge(drained[q], i + ((D0_IN, D1_IN)[q]))
                    for j in range(8):
                        unit_rows(i * 16 + U_OUT, 8 * q + j, q, 2 * j, S)

            turn_rows(2, xs, [(xs_ok, 4)])
            pe.wait_ge(a_lo, TURN_AT[3])

            def ada_sums(s, lat, cx, o, ready):
                pe.wait_ge(*ready)
                for c in range(3):
                    ins = pe.matmul(o[:, c:c + 1], lat[:, P * c:P * c + P], ones[:, 0:1], start=True, stop=True)
                if cx is not None:
                    for c in range(3):
                        ins = pe.matmul(o[:, 4 + c:5 + c], cx[:, P * c:P * c + P], ones[:, 0:1], start=True, stop=True)
                ins.then_inc(ada_mm, 1)

            with pe.Fori(0, 4) as g:
                with pe.Fori(0, 2) as i:
                    for q in range(2):
                        pe.wait_ge(drained[q], g * 4 + i + D_OUT[q])
                        for j in range(8):
                            unit_columns(g * 64 + i * 16 + U_MLP, 8 * q + j, q, 4, 2 * j, 0)
                    ada_sums(None, accL, accC, X[0], (ada_done, g * 16 + i * 4 + 4))
                with pe.Fori(0, 2) as i:
                    for q in range(2):
                        pe.wait_ge(drained[q], g * 4 + i + (D_OUT[q] + 2))
                        for j in range(8):
                            if q == 0 and j == 0:
                                pe.wait_ge(hid_v, g * 4 + (3 + AHEAD))
                            if q == 0 and j == 6:
                                pe.wait_ge(hid_v, g * 4 + (4 + AHEAD))
                            unit_rows(g * 64 + i * 16 + (U_MLP + 32), 8 * q + j, q, 2 * j, S)
                    ada_sums(None, accL, accC, X[0], (ada_done, g * 16 + i * 4 + 12))

            turn_rows(3, xs, [(xs_ok, 8), (ada_col, 16)])
            turn_rows(4, ctxr, [(xs_ok, 8), (a_lo, TURN_AT[4])])

            def spread(n, free):
                for b in range(4):
                    pe.wait_ge(gb_ok, 4 * n + b + 1)
                    if b == 0:
                        pe.wait_ge(*free)
                    pe.matmul(X[0], ones, gdiag, start=True, stop=True).then_inc(gb_mm, 1)

            spread(0, (a_lo, OT_AT))

            def attend_p(i, m):
                if m < 4:
                    a = i * 4 + (m - 4)
                    hh, qb = m // 2, m % 2
                    if m == 0:
                        pe.wait_ge(n_norm, i * 3 + AHEAD)
                    pe.wait_ge(n_t, a + AHEAD)
                    if m == 0:
                        pe.wait_ge(ada_col, i * 2 + 16)
                    pe.matmul(X[1], qT[:, hh, P * qb:P * qb + P], kT[:, hh, :], start=True, stop=True).then_inc(n_s, 1)
                if 1 <= m <= 4:
                    T = m - 1
                    a = i * 4 + (T - 4)
                    pe.wait_ge(n_dg, a + 1)
                    pe.wait_ge(n_pt, a + AHEAD)
                    if m == 1:
                        pe.wait_ge(n_rs, i * 6 + AHEAD)
                    for k in range(4):
                        ins = pe.matmul(X[2][:, P * k:P * k + P], pr[:, T % 2, P * k:P * k + P], dg[:, T % 2, :],
                                        start=True, stop=True)
                    ins.then_inc(n_tr, 1)
                if 2 <= m <= 5:
                    T = m - 2
                    hh, qb = T // 2, T % 2
                    a = i * 4 + (T - 4)
                    pe.wait_ge(n_pt, a + (1 + AHEAD))
                    if T == 0:
                        pe.wait_ge(drained[1], i + D_MLP[1])
                    if qb == 0:
                        pe.wait_ge(n_oc, i * 2 + (hh - 2 + AHEAD))
                    for k in range(4):
                        ins = pe.matmul(X[3][:, P * qb:P * qb + P], vv[:, k, NHD * hh:NHD * hh + NHD], pT[:, T % 2, P * k:P * k + P],
                                        start=(k == 0), stop=(k == 3))
                    ins.then_inc(n_o, 1)

            def norm_sums(i, r):
                pe.wait_ge(n_sq, i * 2 + (1 if r < 2 else 2))
                pe.wait_ge(n_pt, i * 4 + AHEAD)
                pe.wait_ge(n_rs, i * 6 + (2 * r + AHEAD))
                pe.matmul(X[2], ones, nsq[:, 512 * (r % 2):512 * (r % 2) + 512], start=True, stop=True).then_inc(n_nsum, 1)

            def na_turn(i, first):
                u0 = i * 12 + U_NA
                for m in range(12):
                    part = m // 4
                    j = m % 4
                    wh, wl = (v[:, m % RING, :].rearrange("p (k n) -> p k n", n=256) for v in (whi, wlo))
                    if m == 0 and first:
                        pe.wait_ge(drained[0], D_MLP[0])
                    elif m == 0:
                        pe.wait_ge(n_norm, i * 3 + (AHEAD - 1))
                    if m == 4:
                        pe.wait_ge(n_norm, i * 3 + AHEAD) if not first else pe.wait_ge(gb_rd, 4)
                    if m == 8:
                        pe.wait_ge(drained[1], i + D_MLP[1])
                    pe.wait_ge(lo_done, u0 + (m + 1))
                    for kk in range(4):
                        k = 4 * j + kk
                        st, sp_ = k == 0, k == KC - 1
                        if part == 0:
                            for c in range(2):
                                cs = slice(P * c, P * c + P)
                                for y, (a, b) in enumerate(terms(wh[:, kk, cs], wl[:, kk, cs], ahi[:, k, :], alo[:, k, :], True)):
                                    ins = pe.matmul(G[0][:, c, :], a, b, start=st and y == 0, stop=sp_ and y == 2)
                        elif part == 1:
                            for c in range(2):
                                cs = slice(P * c, P * c + P)
                                for y, (a, b) in enumerate(terms(wh[:, kk, cs], wl[:, kk, cs], ahi[:, k, 0:S], alo[:, k, 0:S], True)):
                                    ins = pe.matmul(X[0][:, S * c:S * c + S], a, b, start=st and y == 0 and c == 0,
                                                    stop=sp_ and y == 2, skip_group_check=True)
                        else:
                            for r in range(4):
                                rs = slice(P * r, P * r + P)
                                for y, (a, b) in enumerate(terms(wh[:, kk, :], wl[:, kk, :], ahi[:, k, rs], alo[:, k, rs], False)):
                                    ins = pe.matmul(Gf[1][:, S * r:S * r + S], a, b, start=st and y == 0 and r % 2 == 0,
                                                    stop=sp_ and y == 2, skip_group_check=True)
                    ins.then_inc(unit_used, 1)
                    if not first:
                        attend_p(i, m)
                    if m in (6, 7):
                        norm_sums(i, m - 6)
                    if m == 9:
                        ada_sums(None, acc2, None, X[1], (ada_done, i * 8 + (64 + 4)))
                    if m == 10:
                        norm_sums(i, 2)
                    if m == 11:
                        ada_sums(None, acc3, None, X[1][:, 4:8], (ada_done, i * 8 + (64 + 8)))

            na_turn(0, True)
            with pe.Fori(1, 8) as i:
                na_turn(i, False)
            for m in range(6):
                attend_p(8, m)

            with pe.Fori(0, 2) as i:
                for q in range(2):
                    pe.wait_ge(drained[q], i + D_NA[q])
                    for j in range(8):
                        if q == 0:
                            pe.wait_ge(a_lo, OT_AT + 2 * j + 2)
                        unit_rows(i * 16 + U_WO, 8 * q + j, q, 2 * j, S)

            turn_rows(5, xs, [(xs_ok, 10)])
            spread(1, (a_lo, 7 * KC))
            pe.wait_ge(a_lo, 7 * KC)

            def pair_units(u0, nc_, count):
                for q in range(2):
                    pe.wait_ge(drained[q], count(q))
                    for j in range(8):
                        unit_columns(u0, 8 * q + j, q, nc_, 2 * j, 0)

            with pe.Fori(0, 2) as g:
                with pe.Fori(0, 4) as n:
                    pair_units(g * 96 + n * 16 + U_FFN, 4, lambda q: g * 6 + n + D_WO[q])
                with pe.Fori(0, 2) as n:
                    for q in range(2):
                        pe.wait_ge(drained[q], g * 6 + n + (D_WO[q] + 4))
                        for j in range(8):
                            if q == 0 and j == 0:
                                pe.wait_ge(f_v, g * 16 + (12 + AHEAD))
                            if q == 0 and j == 6:
                                pe.wait_ge(f_v, g * 16 + (16 + AHEAD))
                            unit_rows(g * 96 + n * 16 + (U_FFN + 64), 8 * q + j, q, 2 * j, S)
            with pe.Fori(0, 2) as n:
                pair_units(n * 16 + U_LAST, 4, lambda q: n + D_F1[q])
            pair_units(U_LAST + 32, 3, lambda q: 2 + D_F1[q])
            for n in range(4):
                pe.wait_ge(drained[n % 2], D_F1[n % 2] + 3 + n // 2)
                for j in range(6):
                    if n == 0 and j == 0:
                        pe.wait_ge(f_v, 40 + AHEAD)
                    if n == 0 and j == 4:
                        pe.wait_ge(f_v, 44 + AHEAD)
                    unit_rows(U_DOWN, 6 * n + j, n % 2, 2 * j, S, kc=11, kper=1 if j == 5 else 2)


_INS = ["x", "norm_mix", "w_in", "swa_sinks", "rel_bias", "gla_gate_w", "gla_gate_b", "gla_norm", "swa_out_norm",
        "sb_out_norm", "w_out", "norm_mlp", "w_mlp_in", "w_mlp_out", "norm_final", "c_2", "ctx_2", "c_ctx_2",
        "norm_mix_g_2", "norm_ffn_g_2", "w_ada_2", "b_ada_2", "na_w_qkv_2", "na_q_g_2", "na_k_g_2", "na_rpb_2",
        "na_w_o_2", "ffn_w_up_2", "ffn_conv_w_2", "ffn_conv_b_2", "ffn_w_down_2"]


def kernel(**inputs):
    import concourse.bacc as bacc
    from concourse.bass_utils import run_bass_kernel_spmd

    nc = bacc.Bacc("TRN2", target_bir_lowering=False, num_devices=1)
    arrays, tensors = {}, {}
    for name in _INS + ["consts"]:
        a = shape_constants() if name == "consts" else np.ascontiguousarray(inputs[name])
        arrays[f"in_{name}"] = a
        tensors[name] = nc.dram_tensor(f"in_{name}", a.shape, mybir.dt.from_np(a.dtype), kind="ExternalInput").ap()
    out = nc.dram_tensor("out_x", (1, S, D), F32, kind="ExternalOutput").ap()
    program(nc, tensors, out)
    return run_bass_kernel_spmd(nc, [arrays], core_ids=[0]).results[0]["out_x"]
```

```python
import math
from contextlib import ExitStack, contextmanager

import numpy as np

import concourse.bass as bass
from concourse import mybir

F32 = mybir.dt.float32
F32R = mybir.dt.float32r
ACT = mybir.ActivationFunctionType
ALU = mybir.AluOpType
AXX = mybir.AxisListType.X

P = 128
S = 256
RT = S // P
D = 2048
KC = D // P
HD = 64
SWA_W = 768
DK, DV, LR, CH = 96, 192, 16, 64
SB_W = 512
NH, NHD = 16, 128
GRID, WIN_W = 64, 16
FFN = 5504
FC = FFN // P
EPS = 1e-6
NEG = -1e30
ADA_W = 384

PANELS_IN = [
    ("Q0", 0, 384), ("Q1", 384, 384), ("KV", 768, 512), ("CQ", 3600, 512), ("CK", 4112, 512), ("CV", 4624, 512),
    ("GQ", 1280, 384), ("GK", 1664, 384), ("BV0", 2048, 400), ("BV1", 2432, 384), ("BR0", 2816, 384),
    ("BR1", 3200, 384),
]
ORDER_OUT, EARLY = [0, 1, 2, 6, 7, 3, 4, 5], 6

RING = 4
U_IN = 0
U_OUT = U_IN + 8 * len(PANELS_IN)
U_MLP = U_OUT + 8 * 4
U_NA = U_MLP + 8 * 32
U_WO = U_NA + 12 * 8
U_FFN = U_WO + 8 * 4
U_LAST = U_FFN + 2 * 96
U_DOWN = U_LAST + 4 * 8 + 2 * 8

CONST = {}
_at = 0
for _name, _w in (("ident", 128), ("ones", 128), ("tri", 128), ("strict", 128), ("negstrict", 128),
                  ("swamask", 256), ("namask", 64), ("glamask", 128), ("reset", 256), ("bucket", 256)):
    CONST[_name] = (_at, _at + _w)
    _at += _w
NCONST = _at


def shape_constants():
    c = np.zeros((P, NCONST), np.float32)
    p, f = np.arange(P)[:, None], np.arange(P)[None, :]

    def put(name, v):
        a, b = CONST[name]
        c[:v.shape[0], a:b] = v

    put("ident", (p == f).astype(np.float32))
    put("ones", np.ones((P, P), np.float32))
    put("tri", (p >= f).astype(np.float32))
    put("strict", (p < f).astype(np.float32))
    put("negstrict", np.where(p < f, 0.0, NEG).astype(np.float32))
    put("swamask", np.concatenate([np.where(f > p, 0.0, NEG), np.where(f <= p, 0.0, NEG)], 1).astype(np.float32))
    qc, kc = np.arange(P)[:, None] % GRID, np.arange(GRID)[None, :]
    first = np.clip(qc - WIN_W // 2, 0, GRID - WIN_W)
    put("namask", np.where((kc >= first) & (kc < first + WIN_W), 0.0, NEG).astype(np.float32))
    put("glamask", ((p // CH == f // CH) & (p <= f)).astype(np.float32))
    put("reset", np.broadcast_to((np.arange(S) % CH != 0).astype(np.float32), (P, S)))
    dist = (-np.arange(S)) % P
    ratio = np.log(np.maximum(dist, 1).astype(np.float32) / np.float32(16)) / np.float32(math.log(128 / 16))
    large = np.minimum(16 + (ratio * np.float32(16)).astype(np.int32), 31)
    bucket = np.where(dist < 16, dist, large)
    put("bucket", (np.arange(32)[:, None] == bucket[None, :]).astype(np.float32))
    return c


COLS0 = [("norm_mix", 0, 16), ("norm_mlp", 16, 16), ("norm_mix_g_2", 32, 16), ("norm_ffn_g_2", 48, 16),
         ("c_2", 64, 16), ("c_ctx_2", 80, 16)]
R_MIXG, R_QG, R_KG = 96, 112, 113
C_ADAB, C_GATEB, C_CONV = 114, 210, 214
NCOLS = C_CONV + 4 * 2 * FC


NROWS_DMA = len(COLS0) + 2 + 8 + 8
AHEAD = 2


NA_SCALE = float(NHD) ** -0.5
NA_OWN = 36
TURN_AT = [0, KC, 2 * KC, 3 * KC, 4 * KC, 6 * KC]
OT_AT = 5 * KC


class Steps:

    def __init__(self, eng, sem):
        self.eng, self.sem, self.n, self.turns = eng, sem, 0, []

    def mark(self, ins):
        ins.then_inc(self.sem, 1)
        self.n += 1

    def wait(self):
        value = self.n
        for var, per in self.turns:
            value = var * per + value
        self.eng.wait_ge(self.sem, value)

    def done(self, ins):
        self.mark(ins)
        self.wait()

    @contextmanager
    def loop(self, start, end, per):
        enter = self.n
        self.n = enter - start * per
        at = self.n
        with self.eng.Fori(start, end) as var:
            self.turns.append((var, per))
            yield var
            self.turns.pop()
        assert self.n - at == per, f"{self.n - at} steps in a turn"
        self.n = enter + (end - start) * per


def program(nc, t, out):
    ctx = ExitStack()
    with ctx:
        def sb(name, shape, dt=F32):
            return ctx.enter_context(nc.sbuf_tensor(name, shape, dt))

        def sem(name):
            return ctx.enter_context(nc.semaphore(name))

        raw = sb("raw", [P, RING, 1024])
        whi = sb("whi", [P, RING, 1024], F32R)
        wlo = sb("wlo", [P, RING, 1024], F32R)
        ahi = sb("ahi", [P, KC, 2 * S], F32R)
        alo = sb("alo", [P, KC, 2 * S], F32R)
        x = sb("x", [P, RT, D])
        cst = sb("cst", [P, NCONST])
        cols = sb("cols", [P, NCOLS])
        mods = sb("mods", [P, 96])
        modc = sb("modc", [P, 48])
        cond = sb("cond", [P, 32])
        stat = sb("stat", [P, 168])
        arena = sb("arena", [P, 17152])
        ps = ctx.enter_context(nc.psum_tensor("ps", [P, 8, 512], F32))
        G = [ps[:, 0:2, :], ps[:, 2:4, :]]
        Gf = [g.rearrange("p a b -> p (a b)") for g in G]
        X = [ps[:, 4 + b, :] for b in range(4)]
        X01 = ps[:, 4:6, :].rearrange("p a b -> p (a b)")

        def C(name):
            return cst[:, CONST[name][0]:CONST[name][1]]

        def area(first, *shape):
            n = int(np.prod(shape))
            v = arena[:, first:first + n]
            if len(shape) == 1:
                return v
            names = "abcd"[:len(shape)]
            return v.rearrange(f"p ({' '.join(names)}) -> p {' '.join(names)}",
                               **{names[i]: shape[i] for i in range(len(shape) - 1)})

        ident, ones = C("ident"), C("ones")
        sq_ = area(0, 6, S)
        skd = area(1536, 4, S)
        sv = area(2560, RT, S)
        bm = area(3072, 12, S)
        cq, ck, cv = (area(8192 + 1024 * i, 4, S) for i in range(3))
        sb_z, sb_l, sb_sp, sb_w = (area(3072 + 768 * i, 2, 384) for i in range(4))
        gq, gk = area(6144, 4, S), area(7168, 4, S)
        bv, br = area(8192, RT, 768), area(9728, RT, 768)
        lrT = area(11264, S)
        swt = area(11520, 2, 2, S)
        swp = area(12544, 2, 512)
        g1, g2, g3 = (area(11520 + 1024 * i, 4, S) for i in range(3))
        kend = area(14592, RT, 4 * DK)
        state = area(15360, 4 * DV)
        scT = area(16128, RT, 4, P)
        sg = area(11520, RT, 768)
        xs = area(0, RT, D)
        colrow = area(11520, 7, P)
        fT = area(16128, S)
        gw = area(15360, 384)
        relb = area(16384, 12)
        ada1 = area(4096, 4, 4, ADA_W)
        accL, accC = area(10240, ADA_W), area(10624, ADA_W)
        ebias = area(11008, 16, 6, GRID)
        nfin = area(11008, D)
        ctxr = area(13056, RT, D)
        relu = area(0, 1024)
        sqr = area(1024, 1024)
        oT = area(0, NH, S)
        kT = area(4096, 2, 2 * S)
        vv = area(5120, 4, S)
        qT = area(6144, 2, S)
        eh = area(6656, 2, 6 * GRID)
        pr = area(7424, 2, 512)
        pT = area(8448, 2, 512)
        nsq = area(9472, 1024)
        nrs = area(10496, 1024)
        ada2 = area(11520, 2, 4, ADA_W)
        acc2 = area(14592, ADA_W)
        gb = area(14976, D)
        gdiag = area(4096, D)
        gdiag2, gb2 = area(9472, D), area(11520, D)
        turned_f = area(8448, 2, 2, S)
        tmp = area(4096, 1024)
        held = area(5120, 1024)
        cvt = area(6144, 1024)

        negsink, sink = stat[:, 0:12], stat[:, 12:24]
        smax, snm, sden, ses = (stat[:, 24 + 24 * i:48 + 24 * i] for i in range(4))
        ssum, rstd = stat[:, 120:132], stat[:, 132:144]
        mss, mrs = stat[:, 144:156], stat[:, 156:168]
        acc3 = sb("acc3", [P, ADA_W])
        tabp = acc3[:, 0:P]
        dec = sb("dec", [P, 16])
        nst = sb("nst", [P, 48])
        coefs = sb("coefs", [P, 48])

        bias_dram = nc.dram_tensor("swa_bias_scratch", [12, P, S], F32, kind="Internal").ap()
        tab_dram = nc.dram_tensor("na_table_scratch", [112, GRID, P], F32, kind="Internal").ap()
        eb_dram = nc.dram_tensor("na_bias_scratch", [P, 16 * 384], F32, kind="Internal").ap()

        raw_full = [sem(f"raw_full{i}") for i in range(RING)]
        hi_done, lo_done = sem("hi_done"), sem("lo_done")
        unit_used = sem("unit_used")
        drained = [sem("drained0"), sem("drained1")]
        act_step, dve_step, pool_step = sem("act_step"), sem("dve_step"), sem("pool_step")
        x_in, cst_in, small_in, rows_in = sem("x_in"), sem("cst_in"), sem("small_in"), sem("rows_in")
        colT, cols_ok = sem("colT"), sem("cols_ok")
        a_f = sem("a_f")
        ss_a, rstd_ok, xs_ok, turned, a_hi, a_lo = (sem(n) for n in
                                                    ("ss_a", "rstd_ok", "xs_ok", "turned", "a_hi", "a_lo"))
        ft_mm, ft_ok, ft_out, bm_in, bm_ok = (sem(n) for n in ("ft_mm", "ft_ok", "ft_out", "bm_in", "bm_ok"))
        in_ready = sem("in_ready")
        lr_ok = [sem(f"lr_ok{i}") for i in range(RING)]
        w_s, w_t, w_nm, w_p, w_tr, w_pt, w_o, w_out_ok = (sem("swa_" + n) for n in
            ("scores", "logits", "max", "exp", "turned", "pt", "pv", "out"))
        gla = {n: sem("gla_" + n) for n in ("gate", "l", "b", "eb", "ki", "d", "ke", "turn", "kend", "sc",
                                            "scm", "intra", "ic", "ds", "st", "inter", "add")}
        sbs = {n: sem("sb_" + n) for n in ("z", "l", "p", "c", "arg", "w", "o", "out")}
        mix_a, mix_v = sem("mix_a"), sem("mix_v")
        x_again = sem("x_again")
        hid_a, hid_v = sem("hid_a"), sem("hid_v")
        ada_in = [sem(f"ada_in{i}") for i in range(4)]
        ada_done, ada_mm, ada_col, ada_c = sem("ada_done"), sem("ada_mm"), sem("ada_col"), sem("ada_c")
        tab_ok, tab_out, e_in, e_out, nf_in, ctx_in = (sem(n) for n in
            ("tab_ok", "tab_out", "e_in", "e_out", "nf_in", "ctx_in"))
        ctx_rs, ctx_ok = sem("ctx_rs"), sem("ctx_ok")
        cond_ok, coef_ok = sem("cond_ok"), sem("coef_ok")
        n_eh, n_s, n_t, n_nm, n_p, n_pn, n_tr, n_pt, n_o, n_oc = (sem("na_" + n) for n in
            ("bias", "scores", "logits", "max", "exp", "probs", "turned", "pt", "pv", "out"))
        n_sq, n_nsum, n_rs, n_norm = (sem("na_" + n) for n in ("sq", "nsum", "rs", "norm"))
        gb_mm, gb_ok, gb_rd = sem("gb_mm"), sem("gb_ok"), sem("gb_rd")
        x_done, stored = sem("x_done"), sem("stored")
        f_a, f_v, f_h = sem("f_a"), sem("f_v"), sem("f_h")

        D0_IN, D1_IN = 10, 6
        D_OUT = (D0_IN + 2, D1_IN + 2)
        D_MLP = (D_OUT[0] + 16, D_OUT[1] + 16)
        D_NA = (D_MLP[0], D_MLP[1] + 8)
        D_WO = (D_NA[0] + 2, D_NA[1] + 2)
        D_F1 = (D_WO[0] + 12, D_WO[1] + 12)

        block = ctx.enter_context(nc.Block())

        PLAN = {}

        def plan(m, part, n):
            PLAN.setdefault(m, []).append((part, n))

        for s in range(12):
            for i, part in enumerate(("swa_a", "swa_b", "swa_c")):
                plan(26 + 2 * s + i, part, s)
        for c in range(4):
            for i, part in ((0, "sb_a"), (2, "sb_b"), (3, "sb_c")):
                plan(51 + 3 * c + i, part, c)
        plan(52, "norm_a", 0)
        plan(55, "norm_b", 0)
        plan(64, "norm_a", 1)
        plan(66, "norm_b", 1)
        for n, m in ((0, 73), (8, 75), (1, 78), (2, 81), (3, 82), (4, 83), (5, 84), (6, 85), (7, 86)):
            plan(m, "gla", n)
        plan(88, "norm_a", 2)
        plan(91, "gate", 0)
        plan(92, "turn", 0)

        @block.sync
        def _(sp):
            def load(u0, j, dst, src):
                if not (isinstance(u0, int) and u0 + j < RING):
                    sp.wait_ge(lo_done, u0 + (j - RING + 1))
                sp.dma_start(dst, src).then_inc(raw_full[j % RING], 16)

            def wide(u0, j, w, src, kk=2):
                dst = raw[:, j % RING, :].rearrange("p (k n) -> p k n", n=512)[:, 0:kk, 0:w]
                load(u0, j, dst, src)

            x_rows = t["x"].rearrange("b (r p) d -> p (b r) d", p=P)
            sp.dma_start(x[:, :, :], x_rows).then_inc(x_in, 16)
            sp.dma_start(cst[:, :], t["consts"]).then_inc(cst_in, 16)
            w_in = t["w_in"][0].rearrange("(k p) n -> p k n", p=P)
            for n, (name, c0, w) in enumerate(PANELS_IN):
                for j in range(8):
                    u = 8 * n + j
                    if name == "BV0":
                        if u >= RING:
                            sp.wait_ge(lo_done, u - RING + 1)
                        dst = raw[:, j % RING, :].rearrange("p (k n) -> p k n", n=512)
                        sp.dma_start(dst[:, :, 0:LR], w_in[:, 2 * j:2 * j + 2, 3584:3600]).then_inc(lr_ok[j % RING], 16)
                        sp.dma_start(dst[:, :, LR:400], w_in[:, 2 * j:2 * j + 2, 2048:2432])\
                          .then_inc(raw_full[j % RING], 16)
                    else:
                        wide(8 * n, j, w, w_in[:, 2 * j:2 * j + 2, c0:c0 + w])

            w_o = t["w_out"][0].rearrange("(k p) n -> p k n", p=P)

            def out_unit(n, j):
                k = 2 * ORDER_OUT[j]
                cs = slice(512 * n, 512 * n + 512) if isinstance(n, int) else bass.ds(n * 512, 512)
                wide(n * 8 + U_OUT, j, 512, w_o[:, k:k + 2, cs])

            for n in range(2):
                for j in range(8):
                    out_unit(n, j)
                    if n == 0 and j == 7:
                        sp.wait_ge(tab_out, 16)
                        sp.wait_ge(mix_v, 7)
                    for i in range(4 * (8 * n + j - 7), 4 * (8 * n + j - 6)) if 7 <= 8 * n + j < 15 else ():
                        h, half = i // 2, i % 2
                        first = (7 * h + 1 - half) * GRID * P + GRID - 1
                        src = bass.AP(tab_dram.tensor, first, [[P - 1, GRID], [GRID * P, 6], [1, GRID]])
                        sp.dma_start(ebias[GRID * half:GRID * half + GRID, h, :, :], src).then_inc(e_in, 16)
            with sp.Fori(2, 4) as n:
                for j in range(8):
                    out_unit(n, j)
            w1 = t["w_mlp_in"][0].rearrange("(k p) n -> p k n", p=P)
            w2 = t["w_mlp_out"][0].rearrange("(k p) n -> p k n", p=P)
            with sp.Fori(0, 4) as g:
                with sp.Fori(0, 4) as n:
                    for j in range(8):
                        wide(g * 64 + n * 8 + U_MLP, j, 512, w1[:, 2 * j:2 * j + 2, bass.ds(g * 2048 + n * 512, 512)])
                with sp.Fori(0, 4) as n:
                    for j in range(8):
                        wide(g * 64 + n * 8 + (U_MLP + 32), j, 512,
                             w2[:, bass.ds(g * 16 + 2 * j, 2), bass.ds(n * 512, 512)])
            wq = t["na_w_qkv_2"][0].rearrange("(k p) n -> p k n", p=P)
            with sp.Fori(1, 9) as i:
                for j in range(12):
                    first = (D, 0, 2 * D)[j // 4]
                    load(i * 12 + (U_NA - 12), j, raw[:, j % RING, :].rearrange("p (k n) -> p k n", n=256),
                         wq[:, 4 * (j % 4):4 * (j % 4) + 4, bass.ds(i * 256 + (first - 256), 256)])
            wo = t["na_w_o_2"][0].rearrange("(k p) n -> p k n", p=P)
            with sp.Fori(0, 4) as n:
                for j in range(8):
                    wide(n * 8 + U_WO, j, 512, wo[:, 2 * j:2 * j + 2, bass.ds(n * 512, 512)])
            fu = t["ffn_w_up_2"][0].rearrange("(k p) n -> p k n", p=P)
            fd = t["ffn_w_down_2"][0].rearrange("(k p) n -> p k n", p=P)
            with sp.Fori(0, 2) as g:
                with sp.Fori(0, 4) as n:
                    for j in range(16):
                        wide(g * 96 + n * 16 + U_FFN, j, 512,
                             fu[:, 2 * (j % 8):2 * (j % 8) + 2, bass.ds(g * 2048 + n * 512 + (j // 8) * FFN, 512)])
                with sp.Fori(0, 4) as n:
                    for j in range(8):
                        wide(g * 96 + n * 8 + (U_FFN + 64), j, 512,
                             fd[:, bass.ds(g * 16 + 2 * j, 2), bass.ds(n * 512, 512)])
            with sp.Fori(0, 2) as n:
                for j in range(16):
                    wide(n * 16 + U_LAST, j, 512,
                         fu[:, 2 * (j % 8):2 * (j % 8) + 2, bass.ds(n * 512 + (4096 + (j // 8) * FFN), 512)])
            for j in range(16):
                c0 = 5120 + (j // 8) * FFN
                wide(U_LAST + 32, j, 384, fu[:, 2 * (j % 8):2 * (j % 8) + 2, c0:c0 + 384])
            with sp.Fori(0, 2) as n:
                for j in range(12):
                    kk = 1 if j % 6 == 5 else 2
                    k0 = 32 + 2 * (j % 6)
                    wide(n * 12 + U_DOWN, j, 512, fd[:, k0:k0 + kk, bass.ds(n * 1024 + (j // 6) * 512, 512)], kk)
            for n in range(4):
                sp.wait_ge(x_done, 5 + n)
                sp.dma_start(out.rearrange("b (r p) d -> p (b r) d", p=P)[:, :, 512 * n:512 * n + 512],
                             x[:, :, 512 * n:512 * n + 512]).then_inc(stored, 16)
            sp.wait_ge(stored, 64)

        @block.gpsimd
        def _(pool):
            own = Steps(pool, pool_step)
            pool.sem_inc(f_h, AHEAD)
            own.mark(pool.memset(colrow, 0.0))
            pool.dma_start(relb[0:32, :], t["rel_bias"]).then_inc(small_in, 16)
            pool.dma_start(sink, bass.AP(t["swa_sinks"].tensor, 0, [[0, P], [1, 12]])).then_inc(small_in, 16)
            pool.dma_start(gw[0:LR, :], t["gla_gate_w"][0]).then_inc(small_in, 16)
            pool.wait_ge(ft_ok, 1)
            pool.dma_start(bias_dram, fT[0:12, :].unsqueeze(1).to_broadcast([12, P, S])).then_inc(ft_out, 16)
            pool.wait_ge(ft_out, 16)
            pool.wait_ge(turned, 8)
            shifted = bass.AP(bias_dram.tensor, P, [[S - 1, P], [P * S, 12], [1, P]])
            pool.dma_start(bm[:, :, P:S], shifted).then_inc(bm_in, 16)
            pool.wait_ge(bm_in, 16)
            own.done(pool.tensor_copy(bm[:, :, 0:P], bm[:, :, P:S]))
            m = C("swamask").unsqueeze(1).to_broadcast([P, 12, S])
            pool.wait_ge(cst_in, 16)
            pool.tensor_tensor(bm[:, :, :], bm[:, :, :], m, ALU.add).then_inc(bm_ok, 1)
            own.done(pool.memset(tabp[0:112, :], 0.0))
            for h in range(NH):
                pool.dma_start(tabp[7 * h:7 * h + 7, 48:79], t["na_rpb_2"][0, h, 4:11, :]).then_inc(tab_ok, 16)
            pool.wait_ge(tab_ok, 16 * NH)
            pool.dma_start(tab_dram, tabp[0:112, :].unsqueeze(1).to_broadcast([112, GRID, P])).then_inc(tab_out, 16)
            for n in (0, 3, 1, 2):
                pool.wait_ge(turned, 8 + (EARLY if n in (0, 3) else 8))
                cs = slice(512 * n, 512 * n + 512)
                pool.dma_start(x[:, :, cs], t["x"].rearrange("b (r p) d -> p (b r) d", p=P)[:, :, cs]).then_inc(x_again, 16)
            wa = t["w_ada_2"][0].rearrange("(k p) n -> p k n", p=P)

            def ada_load(s, q, wait=True):
                if wait:
                    pool.wait_ge(ada_done, s * 4 + (q - 3))
                pool.dma_start(ada1[:, q, :, :], wa[:, 4 * q:4 * q + 4, bass.ds(s * ADA_W, ADA_W)])\
                    .then_inc(ada_in[q], 16)
            for q in range(4):
                ada_load(0, q, False)
            pool.wait_ge(e_in, 32 * NH)
            for h in range(NH):
                own.mark(pool.tensor_tensor(ebias[:, h, :, :], ebias[:, h, :, :],
                                            C("namask").unsqueeze(1).to_broadcast([P, 6, GRID]), ALU.add))
            own.wait()
            pool.dma_start(eb_dram, ebias.rearrange("p a b c -> p (a b c)")).then_inc(e_out, 16)
            pool.wait_ge(e_out, 16)
            pool.dma_start(nfin, bass.AP(t["norm_final"].tensor, 0, [[0, P], [1, D]])).then_inc(nf_in, 16)
            pool.dma_start(ctxr, t["ctx_2"].rearrange("b (r p) d -> p (b r) d", p=P)).then_inc(ctx_in, 16)
            def ada_context(s, more):
                for k in range(16):
                    q, piece = k // 4, ada1[:, k // 4, k % 4, :]
                    if k % 4 == 0:
                        pool.wait_ge(ada_in[q], s * 16 + 16)
                    sc = cond[:, 16 + k:17 + k].to_broadcast([P, ADA_W])
                    own.done(pool.tensor_tensor(acc3[:, :] if k else accC, piece, sc, ALU.mult))
                    if k:
                        own.done(pool.tensor_tensor(accC, accC, acc3[:, :], ALU.add))
                    if k % 4 == 3 and more:
                        ada_load(s + 1, q)
                pool.sem_inc(ada_c, 1)
                pool.wait_ge(ada_mm, s + 1)

            pool.wait_ge(cond_ok, 4)
            with own.loop(0, 15, 31) as s:
                ada_context(s, True)
            ada_context(15, False)

            def turn(e, off):
                n = (3, 4, 5).index(e)
                for at in range(8):
                    pool.wait_ge(a_hi, TURN_AT[e] + 2 * at + 2)
                    pool.wait_ge(a_f, KC * n + 2 * at + 2)
                    k = slice(2 * at, 2 * at + 2)
                    pool.tensor_tensor(alo[:, k, off:off + S], turned_f[:, at % 2],
                                       ahi[:, k, off:off + S].bitcast(F32), ALU.subtract).then_inc(a_lo, 2)

            turn(3, 0)
            turn(4, S)
            pool.wait_ge(turned, 8 * 5)

            def attention_loads(i):
                for q in range(8):
                    s, c = q // 4, q % 4
                    pool.wait_ge(ada_done, i * 8 + (64 + q - 1))
                    pool.dma_start(ada2[:, q % 2, :, :],
                                   wa[:, 4 * c:4 * c + 4, bass.ds(i * 768 + (6144 + s * ADA_W), ADA_W)])\
                        .then_inc(ada_in[q % 2], 16)
                    if q == 3:
                        pool.wait_ge(n_t, i * 4 + AHEAD)
                        pool.dma_start(eh, eb_dram.rearrange("p (h c) -> p h c", c=384)[:, bass.ds(i * 2, 2), :])\
                            .then_inc(n_eh, 16)
            with pool.Fori(0, 8) as i:
                attention_loads(i)

            turn(5, 0)
            def hidden(pair, n_local, nc_, down):
                pool.wait_ge(f_a, pair * 3 + 2)
                pool.wait_ge(f_v, pair * 2 + 2)
                pool.wait_ge(unit_used, down)
                p_, h_ = cvt[:, 0:S * nc_], held[:, 0:S * nc_]
                dst = (slice(None), bass.ds(n_local * 4, nc_), slice(S, 2 * S))
                rows_ = p_.rearrange("p (c t) -> p c t", t=S)
                pool.tensor_tensor(p_, p_, h_, ALU.mult).then_inc(f_h, 1)
                pool.wait_ge(f_h, pair * 3 + (AHEAD + 1))
                pool.tensor_copy(ahi[dst], rows_).then_inc(f_h, 1)
                pool.wait_ge(f_h, pair * 3 + (AHEAD + 2))
                pool.tensor_tensor(alo[dst], rows_, ahi[dst].bitcast(F32), ALU.subtract).then_inc(f_h, 1)

            with pool.Fori(0, 2) as g:
                with pool.Fori(0, 4) as n:
                    hidden(g * 4 + n, n, 4, g * 96 + U_FFN)
            with pool.Fori(0, 2) as n:
                hidden(n + 8, n, 4, U_LAST)
            hidden(10, 2, 3, U_LAST)

        @block.scalar
        def _(act):
            own = Steps(act, act_step)
            act.wait_ge(pool_step, 1)
            n = 0
            for name, r0, k in COLS0:
                v = t[name]
                v = v[0] if len(v.shape) == 2 else v
                act.dma_start(colrow[r0:r0 + k, 0, :], v.rearrange("(k n) -> k n", n=P)).then_inc(rows_in, 16)
                n += 1
            sw, so = t["swa_out_norm"][0], t["sb_out_norm"][0]
            act.dma_start(colrow[R_MIXG:R_MIXG + 6, 0, :], sw.rearrange("(k n) -> k n", n=P)).then_inc(rows_in, 16)
            act.dma_start(colrow[R_MIXG + 12:R_MIXG + 16, 0, :], so.rearrange("(k n) -> k n", n=P)).then_inc(rows_in, 16)
            n += 2
            gn = t["gla_norm"]
            for h in range(2):
                r = R_MIXG + 6 + 3 * h
                for row, a, b, s0 in ((r, 0, 128, 0), (r + 1, 0, 64, 128), (r + 1, 64, 128, 0), (r + 2, 0, 128, 64)):
                    act.dma_start(colrow[row:row + 1, 0, a:b], gn[0:1, s0:s0 + b - a]).then_inc(rows_in, 16)
                    n += 1
            act.dma_start(colrow[R_QG:R_QG + 1, 0, :], t["na_q_g_2"]).then_inc(rows_in, 16)
            act.dma_start(colrow[R_KG:R_KG + 1, 0, :], t["na_k_g_2"]).then_inc(rows_in, 16)
            act.dma_start(colrow[0:96, 1, :], t["b_ada_2"][0].rearrange("(k n) -> k n", n=P)).then_inc(rows_in, 16)
            act.dma_start(colrow[0:4, 2, 0:DK], t["gla_gate_b"][0].rearrange("(k n) -> k n", n=DK)).then_inc(rows_in, 16)
            act.dma_start(colrow[0:2 * FC, 3, :], t["ffn_conv_b_2"][0].rearrange("(k n) -> k n", n=P)).then_inc(rows_in, 16)
            for i in range(3):
                act.dma_start(colrow[0:2 * FC, 4 + i, :], t["ffn_conv_w_2"][0, i].rearrange("(k n) -> k n", n=P))\
                    .then_inc(rows_in, 16)
            n += 8
            assert n == NROWS_DMA
            act.preload_act_table_set("natural_log_exp_and_others")
            act.sem_inc(n_pt, AHEAD)
            act.sem_inc(n_rs, AHEAD)

            def split(u0, j, w=1024, extra=None):
                s = j % RING
                act.wait_ge(raw_full[s], u0 * 4 + 16 * (j // RING + 1))
                if extra:
                    act.wait_ge(*extra)
                if not (isinstance(u0, int) and u0 + j < RING):
                    act.wait_ge(unit_used, u0 + (j - RING + 1))
                a, b = (v[:, s, :] for v in (whi, raw))
                if w < 1024:
                    a, b = (v.rearrange("p (k n) -> p k n", n=512)[:, 0:2, 0:w] for v in (a, b))
                act.activation(a, b, ACT.Copy).then_inc(hi_done, 1)

            def rms_rows(n, rows, junk):
                own.done(act.activation(junk, rows, ACT.Square, accum_out=ssum[:, 2 * n:2 * n + 1]))
                act.wait_ge(ss_a, n + 1)
                own.done(act.activation(rstd[:, 2 * n:2 * n + 2], ssum[:, 2 * n:2 * n + 2], ACT.Ln, scale=1.0 / D, bias=EPS))
                act.activation(rstd[:, 2 * n:2 * n + 2], rstd[:, 2 * n:2 * n + 2], ACT.Exp, scale=-0.5)\
                    .then_inc(rstd_ok, 1)
                act.wait_ge(rstd_ok, n + 1)

            def turn(e, off, gain, shift=None, order=range(8), at_=range(8)):
                for at in at_:
                    act.wait_ge(turned, 8 * e + at + 1)
                    for c in range(2):
                        k = 2 * order[at] + c
                        z = X[at % 4][:, c * S:c * S + S]
                        b = shift(k) if shift else 0.0
                        act.activation(ahi[:, k, off:off + S], z, ACT.Identity, scale=gain(k), bias=b).then_inc(a_hi, 1)

            act.wait_ge(x_in, 16)
            rms_rows(0, x[:, 0, :], xs[:, 0, :])
            act.activation(xs[:, 0, :], x[:, 0, :], ACT.Copy, scale=rstd[:, 0:1]).then_inc(xs_ok, 1)
            act.wait_ge(cols_ok, 2)
            for m in range(3):
                split(0, m, 384)
            turn(0, 0, lambda k: cols[:, k:k + 1])

            cc = cols[:, 64:96]
            own.done(act.activation(cond[:, :], cc, ACT.Abs))
            own.done(act.activation(cond[:, :], cond[:, :], ACT.Exp, scale=-1.0))
            act.activation(cond[:, :], cond[:, :], ACT.Ln, bias=1.0).then_inc(cond_ok, 1)
            act.wait_ge(cond_ok, 2)
            act.activation(cond[:, :], cond[:, :], ACT.Exp).then_inc(cond_ok, 1)

            def evac_in(n):
                name = PANELS_IN[n][0]
                act.wait_ge(unit_used, 8 * n + 8)
                g, gf = G[n % 2], Gf[n % 2]
                done = drained[n % 2]
                if name in ("Q0", "Q1"):
                    act.activation(sq_[:, 3 * n:3 * n + 3, :], gf[:, 0:768].rearrange("p (c t) -> p c t", t=S),
                                   ACT.Copy).then_inc(done, 1)
                elif name == "KV":
                    kk = skd.rearrange("p (c a) t -> p c a t", a=2)
                    for a in range(2):
                        act.activation(kk[0:HD, :, a, :], g[HD * a:HD * a + HD, 0, :].rearrange("p (c t) -> p c t", t=S),
                                       ACT.Copy).then_inc(done, 1)
                    act.activation(sv[:, :, :], g[:, 1, :].rearrange("p (c t) -> p c t", t=S), ACT.Copy).then_inc(done, 1)
                elif name in ("GQ", "GK"):
                    act.activation((gq if name == "GQ" else gk)[0:DK], gf[0:DK, :].rearrange("p (c t) -> p c t", t=S),
                                   ACT.Copy).then_inc(done, 1)
                elif name in ("BR0", "BR1", "BV0", "BV1"):
                    if name == "BV0":
                        act.activation(lrT[0:LR, :].rearrange("p (r t) -> p r t", r=RT), g[0:LR, :, 384:512], ACT.Copy)\
                            .then_inc(in_ready, 1)
                    c0 = 384 * int(name[2])
                    dst = (br if name[1] == "R" else bv)[:, :, c0:c0 + 384]
                    act.activation(dst, g[:, :, 0:384], ACT.Copy).then_inc(done, 1)
                else:
                    dst = {"CQ": cq, "CK": ck, "CV": cv}[name]
                    act.activation(dst, gf.rearrange("p (c t) -> p c t", t=S), ACT.Copy).then_inc(done, 1)

            def swa(part, s):
                n, c = divmod(s, 6)
                w, lo = (P, P) if n == 0 else (S, 0)
                if part == "swa_a":
                    act.wait_ge(w_nm, s + 1)
                    for a in range(2):
                        v = swt[:, s % 2, a, 0:w]
                        i = 12 * n + 2 * c + a
                        act.activation(v, v, ACT.Exp, bias=snm[:, i:i + 1], accum_out=sden[:, i:i + 1]).then_inc(w_p, 1)
                    i = 12 * n + 2 * c
                    act.activation(ses[:, i:i + 2], ses[:, i:i + 2], ACT.Exp).then_inc(w_p, 1)
                elif part == "swa_b":
                    act.wait_ge(w_tr, s + 1)
                    if s >= 2:
                        act.wait_ge(w_o, s - 1)
                    k = 2 * w
                    act.activation(swp[:, s % 2, 0:k], X[2][:, 0:k], ACT.Copy).then_inc(w_pt, 1)

            def gla_a(n):
                if n == 0:
                    act.wait_ge(gla["gate"], 1)
                    for h in range(4):
                        own.mark(act.activation(g1[0:DK, h, :], X01[0:DK, S * h:S * h + S], ACT.Abs,
                                                bias=cols[0:DK, C_GATEB + h:C_GATEB + h + 1]))
                    own.wait()
                    own.done(act.activation(g1[0:DK], g1[0:DK], ACT.Exp, scale=-1.0))
                    act.activation(g1[0:DK], g1[0:DK], ACT.Ln, bias=1.0).then_inc(gla["l"], 1)
                if n == 8:
                    act.wait_ge(gla["b"], 1)
                    act.activation(g2[0:DK], g1[0:DK], ACT.Exp).then_inc(gla["eb"], 1)
                    act.activation(g3[0:DK], g1[0:DK], ACT.Exp, scale=-1.0).then_inc(gla["eb"], 1)
                    last = g1[0:DK].rearrange("p h (c t) -> p h c t", t=CH)[:, :, :, CH - 1]
                    act.activation(dec[0:DK, :].rearrange("p (h c) -> p h c", c=4), last, ACT.Exp).then_inc(gla["eb"], 1)
                    act.wait_ge(gla["d"], 1)
                    act.activation(g2[0:DK], g2[0:DK], ACT.Exp).then_inc(gla["ke"], 1)
                if n == 1:
                    act.wait_ge(gla["turn"], 2)
                    for r in range(RT):
                        act.activation(kend[:, r, :], X[2 + r][:, 0:4 * DK], ACT.Copy).then_inc(gla["kend"], 1)
                if n in (2, 3):
                    r = n - 2
                    act.wait_ge(gla["intra"], n - 1)
                    m = x[:, r, SWA_W:SWA_W + 768].rearrange("p (a b) -> p a b", a=2)
                    act.activation(m, ps[:, 4:6, 0:384], ACT.Copy).then_inc(gla["ic"], 1)

            def sb_a(part, c):
                if part == "sb_a":
                    act.wait_ge(sbs["z"], c + 1)
                    v = sb_l[:, :, :]
                    own.done(act.activation(v, ps[:, 4:6, 0:384], ACT.Abs, scale=0.125))
                    own.done(act.activation(v, v, ACT.Exp, scale=-1.0))
                    act.activation(v, v, ACT.Ln, bias=1.0).then_inc(sbs["l"], 1)
                elif part == "sb_b":
                    act.wait_ge(sbs["arg"], c + 1)
                    act.activation(sb_w[:, :, :], sb_w[:, :, :], ACT.Exp).then_inc(sbs["w"], 1)
                else:
                    act.wait_ge(sbs["o"], c + 1)
                    for r in range(RT):
                        act.activation(x[:, r, 1536 + P * c:1536 + P * c + P], X[2 + r][:, 384:512], ACT.Copy)\
                            .then_inc(sbs["out"], 1)

            def finish_a(part, n):
                if part == "norm_a":
                    a, b, w = ((0, 2, SWA_W), (10, 12, SB_W), (2, 10, DV))[n]
                    act.wait_ge(mix_v, n + 1)
                    own.done(act.activation(mrs[:, a:b], mss[:, a:b], ACT.Ln, scale=1.0 / w, bias=EPS))
                    act.activation(mrs[:, a:b], mrs[:, a:b], ACT.Exp, scale=-0.5).then_inc(mix_a, 1)
                if part == "gate":
                    v = sg[:, :, 384 * n:384 * n + 384]
                    if n == 0:
                        act.wait_ge(mix_v, 3)
                    act.wait_ge(drained[n], (D0_IN, D1_IN)[n])
                    own.done(act.activation(v, br[:, :, 384 * n:384 * n + 384], ACT.Abs))
                    own.done(act.activation(v, v, ACT.Exp, scale=-1.0))
                    act.activation(v, v, ACT.Ln, bias=1.0).then_inc(mix_a, 1)
                    act.wait_ge(mix_v, 4 + 2 * n)
                    act.activation(v, v, ACT.Exp).then_inc(mix_a, 1)
                if part == "turn":
                    at_ = (range(EARLY), range(EARLY, 8))[n]
                    turn(1, S, lambda k: cols[:, R_MIXG + k:R_MIXG + k + 1], order=ORDER_OUT, at_=at_)

            for m in range(8 * len(PANELS_IN)):
                n, j = divmod(m + 3, 8)
                if n < len(PANELS_IN):
                    name, _, w = PANELS_IN[n]
                    split(8 * n, j, w, (lr_ok[j % RING], 16 * (j // RING + 1)) if name == "BV0" else None)
                else:
                    split(8 * n, j)
                if m % 8 == 0 and m:
                    evac_in(m // 8 - 1)
                for part, s in PLAN.get(m, []):
                    if part == "gla":
                        gla_a(s)
                    else:
                        {"swa": swa, "sb_": sb_a}.get(part[:3], finish_a)(part, s)
            split(U_OUT, 3)
            evac_in(len(PANELS_IN) - 1)
            finish_a("gate", 1)
            finish_a("turn", 1)
            with act.Fori(0, 4) as n:
                for j in range(4, 12):
                    split(n * 8 + U_OUT, j)

            act.wait_ge(x_done, 1)
            rms_rows(1, x[:, 0, :], xs[:, 0, :])
            act.activation(xs[:, 0, :], x[:, 0, :], ACT.Copy, scale=rstd[:, 2:3]).then_inc(xs_ok, 1)
            turn(2, 0, lambda k: cols[:, 16 + k:17 + k])
            with own.loop(0, 4, 4) as g:
                with own.loop(0, 2, 2) as i:
                    for j in range(4, 20):
                        split(g * 64 + i * 16 + U_MLP, j)
                        if j % 8 == 3:
                            q = j // 8 - 1
                            act.wait_ge(unit_used, g * 64 + i * 16 + (U_MLP + 8 * q + 8))
                            act.activation(relu, Gf[q], ACT.Relu).then_inc(drained[q], 1)
                            act.wait_ge(drained[q], g * 4 + i + (D_OUT[q] + 1))
                            act.wait_ge(hid_v, g * 4 + i * 2 + (q + AHEAD))
                            own.done(act.activation(sqr, relu, ACT.Square))
                            act.activation(ahi[:, bass.ds(i * 8 + 4 * q, 4), S:2 * S],
                                           sqr.rearrange("p (c t) -> p c t", t=S), ACT.Copy).then_inc(hid_a, 1)
                with act.Fori(0, 2) as i:
                    for j in range(4, 20):
                        split(g * 64 + i * 16 + (U_MLP + 32), j)

            act.wait_ge(x_done, 2)
            rms_rows(2, x[:, 0, :], xs[:, 0, :])
            act.wait_ge(ctx_in, 16)
            act.wait_ge(ada_c, 16)
            for r in range(RT):
                own.done(act.activation(area(4096, D), ctxr[:, r, :], ACT.Square, accum_out=ssum[:, 10 + r:11 + r]))
            own.done(act.activation(rstd[:, 10:12], ssum[:, 10:12], ACT.Ln, scale=1.0 / D, bias=EPS))
            act.activation(rstd[:, 10:12], rstd[:, 10:12], ACT.Exp, scale=-0.5).then_inc(ctx_rs, 1)
            act.wait_ge(x_done, 3)
            rms_rows(3, x[:, 0, :], xs[:, 0, :])
            act.activation(xs[:, 0, :], x[:, 0, :], ACT.Copy, scale=rstd[:, 6:7]).then_inc(xs_ok, 1)
            act.wait_ge(ctx_rs, 1)
            act.activation(ctxr[:, 0, :], ctxr[:, 0, :], ACT.Copy, scale=rstd[:, 10:11]).then_inc(ctx_ok, 1)
            act.wait_ge(coef_ok, 2)
            turn(3, 0, lambda k: coefs[:, k:k + 1], lambda k: mods[:, k:k + 1])
            turn(4, S, lambda k: coefs[:, 16 + k:17 + k], lambda k: modc[:, k:k + 1])

            def attend_a(i, m):
                if m < 4:
                    a = i * 4 + (m - 4)
                    act.wait_ge(n_nm, a + 1)
                    act.activation(pr[:, m % 2, :], pr[:, m % 2, :], ACT.Exp, bias=nst[:, 4 + m:5 + m],
                                   accum_out=nst[:, 8 + m:9 + m]).then_inc(n_p, 1)
                if 1 <= m <= 4:
                    T = m - 1
                    a = i * 4 + (T - 4)
                    act.wait_ge(n_tr, a + (1 + AHEAD))
                    act.wait_ge(n_o, a + (AHEAD - 1))
                    act.activation(pT[:, T % 2, :], X[2], ACT.Copy).then_inc(n_pt, 1)

            def inv_rms(i, r):
                v = nrs[:, 512 * (r % 2):512 * (r % 2) + 512]
                act.wait_ge(n_nsum, i * 3 + (r + 1))
                act.wait_ge(n_norm, i * 3 + ((1 if r == 2 else 0) + AHEAD))
                act.activation(v, X[2], ACT.Ln, scale=1.0 / NHD, bias=EPS).then_inc(n_rs, 1)
                act.wait_ge(n_rs, i * 6 + (2 * r + 1 + AHEAD))
                act.activation(v, v, ACT.Exp, scale=-0.5).then_inc(n_rs, 1)

            def na_turn(i, first):
                u0 = i * 12 + U_NA
                for m in range(12):
                    if not (first and m == 0):
                        split(u0, m + 3)
                    if m == 0 and not first:
                        act.wait_ge(unit_used, u0)
                        act.activation(vv, Gf[1].rearrange("p (c t) -> p c t", t=S), ACT.Copy).then_inc(drained[1], 1)
                    if not first:
                        attend_a(i, m)
                    if m == 4:
                        act.wait_ge(unit_used, u0 + 4)
                        act.activation(nsq, Gf[0], ACT.Square).then_inc(n_sq, 1)
                    if m == 6:
                        inv_rms(i, 0)
                    if m == 7:
                        inv_rms(i, 1)
                    if m == 8:
                        act.wait_ge(unit_used, u0 + 8)
                        act.activation(nsq[:, 0:512], X[0], ACT.Square).then_inc(n_sq, 1)
                    if m == 10:
                        inv_rms(i, 2)

            na_turn(0, True)
            with act.Fori(1, 8) as i:
                na_turn(i, False)
            split(U_WO, 3)
            act.wait_ge(unit_used, U_WO)
            act.activation(vv, Gf[1].rearrange("p (c t) -> p c t", t=S), ACT.Copy).then_inc(drained[1], 1)
            for m in range(6):
                attend_a(8, m)
            act.wait_ge(n_oc, NH + AHEAD)
            for k in range(KC):
                act.activation(ahi[:, k, S:2 * S], oT[:, k, :], ACT.Copy).then_inc(a_hi, 1)
            with act.Fori(0, 4) as n:
                for j in range(4, 12):
                    split(n * 8 + U_WO, j)

            act.wait_ge(x_done, 4)
            rms_rows(4, x[:, 0, :], xs[:, 0, :])
            act.activation(xs[:, 0, :], x[:, 0, :], ACT.Copy, scale=rstd[:, 8:9]).then_inc(xs_ok, 1)
            act.wait_ge(coef_ok, 3)
            turn(5, 0, lambda k: coefs[:, 32 + k:33 + k], lambda k: mods[:, 48 + k:49 + k])
            act.preload_act_table_set("silu_and_others")

            def conv_a(pair, q, nc_, used):
                act.wait_ge(unit_used, used)
                dst = (held, cvt)[q]
                act.wait_ge(f_h, pair * 3 + AHEAD)
                for c in range(nc_):
                    at = C_CONV + q * FC + c
                    ins = act.activation(dst[:, S * c:S * c + S], Gf[q][:, S * c:S * c + S], ACT.Identity,
                                         scale=cols[:, bass.ds(pair * 4 + (at + 4 * FC), 1)],
                                         bias=cols[:, bass.ds(pair * 4 + at, 1)])
                ins.then_inc(f_a, 1)
                if q == 0:
                    act.wait_ge(f_v, pair * 2 + 1)
                    v = held[:, 0:S * nc_]
                    act.activation(v, v, ACT.Silu).then_inc(f_a, 1)

            def conv_pair(pair, u0, nc_):
                for j in range(4, 20):
                    split(u0, j)
                    if j == 11:
                        conv_a(pair, 0, nc_, u0 + 8)
                    if j == 19:
                        conv_a(pair, 1, nc_, u0 + 16)

            with act.Fori(0, 2) as g:
                with act.Fori(0, 4) as n:
                    conv_pair(g * 4 + n, g * 96 + n * 16 + U_FFN, 4)
                with act.Fori(0, 4) as n:
                    for j in range(4, 12):
                        split(g * 96 + n * 8 + (U_FFN + 64), j)
            with act.Fori(0, 2) as n:
                conv_pair(n + 8, n * 16 + U_LAST, 4)
            conv_pair(10, U_LAST + 32, 3)
            for j in range(4, 24):
                split(U_DOWN, j)

        @block.vector
        def _(dve):
            own = Steps(dve, dve_step)
            for s_ in (n_t, n_oc, n_norm, hid_v):
                dve.sem_inc(s_, AHEAD)

            def f(ap):
                return ap.bitcast(F32)

            def split(u0, j, w=1024):
                s = j % RING
                dve.wait_ge(hi_done, u0 + (j + 1))
                a, b, c = wlo[:, s, :], raw[:, s, :], f(whi[:, s, :])
                if w < 1024:
                    a, b, c = (v.rearrange("p (k n) -> p k n", n=512)[:, 0:2, 0:w] for v in (a, b, c))
                dve.tensor_tensor(a, b, c, ALU.subtract).then_inc(lo_done, 1)

            def ss_rows(n, rows, junk):
                dve.tensor_tensor_reduce(junk, rows, rows, 1.0, 0.0, ALU.mult, ALU.add,
                                         ssum[:, 2 * n + 1:2 * n + 2]).then_inc(ss_a, 1)

            def scale_rows(n, dst, rows):
                dve.wait_ge(rstd_ok, n + 1)
                dve.tensor_scalar(dst, rows, rstd[:, 2 * n + 1:2 * n + 2], None, ALU.mult).then_inc(xs_ok, 1)

            def turn(e, off, gain, shift=None, order=range(8), at_=range(8)):
                for at in at_:
                    dve.wait_ge(a_hi, TURN_AT[e] + 2 * at + 2)
                    if shift and (at >= 2 or e == 4):
                        dve.wait_ge(a_lo, TURN_AT[e] + 2 * at - 2)
                    for c in range(2):
                        k = 2 * order[at] + c
                        z = X[at % 4][:, c * S:c * S + S]
                        hi = f(ahi[:, k, off:off + S])
                        if shift:
                            dve.tensor_scalar(turned_f[:, at % 2, c, :], z, gain(k), shift(k), ALU.mult, ALU.add)\
                                .then_inc(a_f, 1)
                        else:
                            dve.scalar_tensor_tensor(out=alo[:, k, off:off + S], in0=z, scalar=gain(k), in1=hi,
                                                     op0=ALU.mult, op1=ALU.subtract).then_inc(a_lo, 1)

            dve.wait_ge(x_in, 16)
            ss_rows(0, x[:, 1, :], xs[:, 1, :])
            scale_rows(0, xs[:, 1, :], x[:, 1, :])
            dve.wait_ge(colT, 1)
            dve.tensor_copy(cols[:, 0:C_CONV], X01[:, 0:C_CONV]).then_inc(cols_ok, 1)
            dve.tensor_copy(cols[:, C_CONV:NCOLS], X01[:, 512:512 + NCOLS - C_CONV]).then_inc(cols_ok, 1)
            dve.wait_ge(ft_mm, 1)
            dve.tensor_copy(fT[0:12, :], X[2][0:12, 0:S]).then_inc(ft_ok, 1)
            for m in range(3):
                split(0, m, 384)
            dve.wait_ge(cols_ok, 2)
            turn(0, 0, lambda k: cols[:, k:k + 1])
            cc = cols[:, 64:96]
            dve.wait_ge(cond_ok, 1)
            dve.scalar_tensor_tensor(out=cond[:, :], in0=cc, scalar=0.0, in1=cond[:, :],
                                     op0=ALU.min, op1=ALU.subtract).then_inc(cond_ok, 1)
            dve.wait_ge(cond_ok, 3)
            own.done(dve.tensor_tensor(cond[:, :], cond[:, :], cc, ALU.mult))
            dve.sem_inc(cond_ok, 1)
            dve.wait_ge(small_in, 48)
            own.done(dve.tensor_scalar(negsink, sink, -1.0, None, ALU.mult))

            def evac_in(n):
                if PANELS_IN[n][0] == "KV":
                    dve.wait_ge(unit_used, 8 * n + 8)
                    dve.wait_ge(drained[0], 4)
                    kk = skd.rearrange("p (c a) t -> p c a t", a=2)
                    for a in range(2):
                        dve.tensor_copy(kk[HD:P, :, a, :],
                                        G[0][HD * a:HD * a + HD, 0, :].rearrange("p (c t) -> p c t", t=S))\
                            .then_inc(drained[0], 1)

            def swa(part, s):
                n, c = divmod(s, 6)
                w, lo = (P, P) if n == 0 else (S, 0)
                i = 12 * n + 2 * c
                if part == "swa_a":
                    dve.wait_ge(w_s, s + 1)
                    if s == 0:
                        dve.wait_ge(bm_ok, 1)
                    if s >= 2:
                        dve.wait_ge(w_tr, s - 1)
                    for a in range(2):
                        ins = dve.scalar_tensor_tensor(out=swt[:, s % 2, a, 0:w], in0=X[a][:, 0:w], scalar=0.125,
                                                       in1=bm[:, 2 * c + a, lo:S], op0=ALU.mult, op1=ALU.add)
                    ins.then_inc(w_t, 1)
                    dve.wait_ge(w_t, s + 1)
                    own.done(dve.tensor_reduce(smax[:, i:i + 2], swt[:, s % 2, :, 0:w], AXX, ALU.max))
                    own.done(dve.scalar_tensor_tensor(out=snm[:, i:i + 2], in0=smax[:, i:i + 2], scalar=-1.0,
                                                      in1=negsink[:, 2 * c:2 * c + 2], op0=ALU.mult, op1=ALU.min))
                    dve.tensor_tensor(ses[:, i:i + 2], snm[:, i:i + 2], sink[:, 2 * c:2 * c + 2], ALU.add)\
                        .then_inc(w_nm, 1)
                elif part == "swa_b":
                    dve.wait_ge(w_p, 3 * s + 3)
                    own.done(dve.tensor_tensor(sden[:, i:i + 2], sden[:, i:i + 2], ses[:, i:i + 2], ALU.add))
                    own.done(dve.reciprocal(sden[:, i:i + 2], sden[:, i:i + 2]))
                else:
                    dve.wait_ge(w_o, s + 1)
                    for a in range(2):
                        h = 2 * c + a
                        ins = dve.tensor_scalar(x[:, n, HD * h:HD * h + HD], X[3][:, HD * a:HD * a + HD],
                                                sden[:, i + a:i + a + 1], None, ALU.mult)
                    ins.then_inc(w_out_ok, 1)

            def gla_v(n):
                gd = gla
                if n == 0:
                    dve.wait_ge(gd["gate"], 1)
                    dve.wait_ge(gd["l"], 1)
                    for h in range(4):
                        own.mark(dve.tensor_scalar(g2[0:DK, h, :], X01[0:DK, S * h:S * h + S],
                                                   cols[0:DK, C_GATEB + h:C_GATEB + h + 1], 0.0, ALU.add, ALU.min))
                    own.wait()
                    own.done(dve.tensor_tensor(g2[0:DK], g2[0:DK], g1[0:DK], ALU.subtract))
                    own.done(dve.tensor_scalar(g2[0:DK], g2[0:DK], 1.0 / 16.0, -1.0, ALU.mult, ALU.max))
                    for h in range(4):
                        ins = dve.tensor_tensor_scan(g1[0:DK, h, :], C("reset")[0:DK, :], g2[0:DK, h, :], 0.0,
                                                     ALU.mult, ALU.add)
                    ins.then_inc(gd["b"], 1)
                    dve.wait_ge(gd["b"], 1)
                if n == 8:
                    dve.wait_ge(gd["eb"], 3)
                    own.done(dve.scalar_tensor_tensor(out=gq[0:DK], in0=gq[0:DK], scalar=float(DK) ** -0.5,
                                                      in1=g2[0:DK], op0=ALU.mult, op1=ALU.mult))
                    own.done(dve.tensor_tensor(g3[0:DK], g3[0:DK], gk[0:DK], ALU.mult))
                    b4 = g1[0:DK].rearrange("p h (c t) -> p (h c) t", t=CH)
                    o4 = g2[0:DK].rearrange("p h (c t) -> p (h c) t", t=CH)
                    last = b4[:, :, CH - 1:CH].to_broadcast([DK, 16, CH])
                    dve.tensor_tensor(o4, last, b4, ALU.subtract).then_inc(gd["d"], 1)
                    dve.wait_ge(gd["ke"], 1)
                    dve.tensor_tensor(g2[0:DK], g2[0:DK], gk[0:DK], ALU.mult).then_inc(gd["ki"], 1)
                if n == 1:
                    for r in range(RT):
                        dve.wait_ge(gd["sc"], r + 1)
                        dve.tensor_tensor(scT[:, r], X[r].rearrange("p (h t) -> p h t", t=P),
                                          C("glamask").unsqueeze(1).to_broadcast([P, 4, P]), ALU.mult)\
                            .then_inc(gd["scm"], 1)
                if n in (4, 5, 6):
                    c = n - 4
                    dve.wait_ge(gd["ds"], c + 1)
                    for h in range(4):
                        src = ps[0:DK, 6 + h // 2, DV * (h % 2):DV * (h % 2) + DV]
                        dst = state[0:DK, DV * h:DV * h + DV]
                        if c == 0:
                            ins = dve.tensor_copy(dst, src)
                        else:
                            ins = dve.scalar_tensor_tensor(out=dst, in0=dst, scalar=dec[0:DK, 4 * h + c:4 * h + c + 1],
                                                           in1=src, op0=ALU.mult, op1=ALU.add)
                    ins.then_inc(gd["st"], 1)
                    dve.wait_ge(gd["st"], c + 1)
                if n in (5, 6, 7):
                    c = n - 4
                    dve.wait_ge(gd["inter"], c)
                    dve.wait_ge(gd["ic"], 2)
                    p0 = CH * (c % 2)
                    m = x[p0:p0 + CH, c // 2, SWA_W:SWA_W + 768].rearrange("p (a b) -> p a b", a=2)
                    dve.tensor_tensor(m, m, ps[p0:p0 + CH, 4:6, 0:384], ALU.add).then_inc(gd["add"], 1)

            def sb_v(part, c):
                st = C("strict").unsqueeze(1).to_broadcast([P, 2, P])
                ng = C("negstrict").unsqueeze(1).to_broadcast([P, 2, P])
                if part == "sb_a":
                    dve.wait_ge(sbs["l"], c + 1)
                    own.done(dve.tensor_scalar(sb_z[:, :, :], ps[:, 4:6, 0:384], 0.125, None, ALU.mult))
                    own.done(dve.scalar_tensor_tensor(out=sb_sp[:, :, :], in0=sb_z[:, :, :], scalar=0.0,
                                                      in1=sb_l[:, :, :], op0=ALU.max, op1=ALU.add))
                    own.mark(dve.tensor_tensor(sb_sp[:, :, 0:P], sb_sp[:, :, 0:P], st, ALU.mult))
                    dve.tensor_tensor(sb_sp[:, :, S:384], sb_sp[:, :, S:384], st, ALU.mult).then_inc(sbs["p"], 1)
                elif part == "sb_b":
                    dve.wait_ge(sbs["c"], c + 1)
                    own.done(dve.tensor_tensor(sb_w[:, :, :], sb_z[:, :, :], ps[:, 6:8, 0:384], ALU.subtract))
                    own.mark(dve.tensor_tensor(sb_w[:, :, 0:P], sb_w[:, :, 0:P], ng, ALU.add))
                    dve.tensor_tensor(sb_w[:, :, S:384], sb_w[:, :, S:384], ng, ALU.add).then_inc(sbs["arg"], 1)

            jk = (area(13056, 768), area(13824, 768))

            def finish_v(part, n):
                a, b = ((0, SWA_W), (1536, D), (768, 1536))[n if part[:4] == "norm" else 2]
                if part == "norm_a":
                    if n == 0:
                        dve.wait_ge(w_out_ok, 12)
                    elif n == 1:
                        dve.wait_ge(sbs["out"], 8)
                    else:
                        dve.wait_ge(gla["add"], 3)
                    for r in range(RT):
                        v = x[:, r, a:b]
                        if n < 2:
                            i = (0, 10)[n] + r
                            ins = dve.tensor_tensor_reduce(jk[r][:, 0:b - a], v, v, 1.0, 0.0, ALU.mult, ALU.add,
                                                           mss[:, i:i + 1])
                        else:
                            own.done(dve.tensor_tensor(jk[r], v, v, ALU.mult))
                            ins = dve.tensor_reduce(mss[:, 2 + 4 * r:6 + 4 * r], jk[r].rearrange("p (h v) -> p h v", h=4),
                                                    AXX, ALU.add)
                        own.mark(ins)
                    own.wait()
                    dve.sem_inc(mix_v, 1)
                if part == "norm_b":
                    dve.wait_ge(mix_a, n + 1)
                    for r in range(RT):
                        i = (0, 10)[n] + r
                        own.mark(dve.tensor_scalar(x[:, r, a:b], x[:, r, a:b], mrs[:, i:i + 1], None, ALU.mult))
                if part == "gate":
                    half = slice(384 * n, 384 * n + 384)
                    v, bb = sg[:, :, half], br[:, :, half]
                    dve.wait_ge(mix_a, 4 + 2 * n)
                    dve.scalar_tensor_tensor(out=v, in0=bb, scalar=0.0, in1=v, op0=ALU.min, op1=ALU.subtract)\
                        .then_inc(mix_v, 1)
                    for r in range(RT):
                        for h in (2 * n, 2 * n + 1):
                            y = x[:, r, 768 + DV * h:768 + DV * h + DV]
                            i = 2 + 4 * r + h
                            own.mark(dve.scalar_tensor_tensor(out=y, in0=y, scalar=mrs[:, i:i + 1],
                                                              in1=br[:, r, DV * h:DV * h + DV], op0=ALU.mult, op1=ALU.mult))
                    own.wait()
                    dve.wait_ge(mix_a, 5 + 2 * n)
                    y = x[:, :, 768 + 384 * n:768 + 384 * n + 384]
                    dve.tensor_tensor(y, y, v, ALU.mult).then_inc(mix_v, 1)
                if part == "turn":
                    at_ = (range(EARLY), range(EARLY, 8))[n]
                    turn(1, S, lambda k: cols[:, R_MIXG + k:R_MIXG + k + 1], order=ORDER_OUT, at_=at_)

            for m in range(8 * len(PANELS_IN)):
                n, j = divmod(m + 3, 8)
                split(8 * n, j, PANELS_IN[n][2] if n < len(PANELS_IN) else 1024)
                if m % 8 == 0 and m:
                    evac_in(m // 8 - 1)
                for part, s in PLAN.get(m, []):
                    if part == "gla":
                        gla_v(s)
                    else:
                        {"swa": swa, "sb_": sb_v}.get(part[:3], finish_v)(part, s)
            split(U_OUT, 3)
            finish_v("gate", 1)
            finish_v("turn", 1)

            def add_panel(n, q, used, done):
                dve.wait_ge(unit_used, used)
                v = x[:, :, bass.ds(n * 512, 512)]
                dve.tensor_tensor(v, v, G[q], ALU.add).then_inc(done, 1)

            with dve.Fori(0, 2) as i:
                for j in range(4, 20):
                    split(i * 16 + U_OUT, j)
                    if j % 8 == 3:
                        q = j // 8 - 1
                        dve.wait_ge(x_again, 64)
                        add_panel(i * 2 + q, q, i * 16 + (U_OUT + 8 * q + 8), drained[q])
            for q in range(2):
                dve.wait_ge(drained[q], D_OUT[q])
            dve.sem_inc(x_done, 1)

            ss_rows(1, x[:, 1, :], xs[:, 1, :])
            scale_rows(1, xs[:, 1, :], x[:, 1, :])
            turn(2, 0, lambda k: cols[:, 16 + k:17 + k])

            def ada_term(s, k, piece, acc, c, first):
                sc = cond[:, c + k:c + k + 1]
                if first:
                    return dve.tensor_scalar(acc, piece, sc, None, ALU.mult)
                return dve.scalar_tensor_tensor(out=acc, in0=piece, scalar=sc, in1=acc, op0=ALU.mult, op1=ALU.add)

            def ada_slot(s, ks):
                for k in ks:
                    q = k // 4
                    if k % 4 == 0:
                        dve.wait_ge(ada_in[q], s * 16 + 16)
                    ins = ada_term(s, k, ada1[:, q, k % 4, :], accL, 0, k == 0)
                    if k % 4 == 3:
                        ins.then_inc(ada_done, 1)
                        dve.wait_ge(ada_done, s * 4 + (q + 1))
                    else:
                        own.done(ins)

            def mlp_pair(g, i, up):
                u0 = g * 64 + i * 16 + (U_MLP if up else U_MLP + 32)
                s = g * 4 + i + (0 if up else 2)
                for j in range(4, 20):
                    split(u0, j)
                    slot = j - 3
                    ada_slot(s, [2 * slot - 2, 2 * slot - 1] if slot < 4 else [slot + 2] if slot < 14 else [])
                    if j % 8 == 3:
                        q = j // 8 - 1
                        if up:
                            dve.wait_ge(hid_a, g * 4 + i * 2 + (q + 1))
                            dve.tensor_tensor(alo[:, bass.ds(i * 8 + 4 * q, 4), S:2 * S],
                                              sqr.rearrange("p (c t) -> p c t", t=S),
                                              f(ahi[:, bass.ds(i * 8 + 4 * q, 4), S:2 * S]), ALU.subtract).then_inc(hid_v, 1)
                        else:
                            add_panel(i * 2 + q, q, u0 + (8 * q + 8), drained[q])
                dve.wait_ge(ada_mm, s + 1)
                own.mark(dve.tensor_copy(mods[:, bass.ds(s * 3, 3)], X[0][:, 0:3]))
                dve.tensor_copy(modc[:, bass.ds(s * 3, 3)], X[0][:, 4:7]).then_inc(ada_col, 1)

            with own.loop(0, 4, 4 * 13) as g:
                with own.loop(0, 2, 13) as i:
                    mlp_pair(g, i, True)
                with own.loop(0, 2, 13) as i:
                    mlp_pair(g, i, False)
            for q in range(2):
                dve.wait_ge(drained[q], D_MLP[q])
            dve.sem_inc(x_done, 1)

            ss_rows(2, x[:, 1, :], xs[:, 1, :])
            dve.wait_ge(rstd_ok, 3)
            dve.wait_ge(nf_in, 16)
            for r in range(RT):
                own.mark(dve.scalar_tensor_tensor(out=x[:, r, :], in0=x[:, r, :], scalar=rstd[:, 4 + r:5 + r], in1=nfin,
                                                  op0=ALU.mult, op1=ALU.mult))
            own.wait()
            dve.sem_inc(x_done, 1)
            ss_rows(3, x[:, 1, :], xs[:, 1, :])
            dve.wait_ge(ada_col, 16)
            own.mark(dve.tensor_tensor(mods[:, 0:48], mods[:, 0:48], cols[:, C_ADAB:C_ADAB + 48], ALU.add))
            own.done(dve.tensor_tensor(modc[:, 0:48], modc[:, 0:48], cols[:, C_ADAB:C_ADAB + 48], ALU.add))
            for v, o in ((mods, 0), (modc, 16)):
                dve.scalar_tensor_tensor(out=coefs[:, o:o + 16], in0=v[:, 16:32], scalar=1.0, in1=cols[:, 32:48],
                                         op0=ALU.add, op1=ALU.mult).then_inc(coef_ok, 1)
            scale_rows(3, xs[:, 1, :], x[:, 1, :])
            dve.wait_ge(ctx_rs, 1)
            dve.tensor_scalar(ctxr[:, 1, :], ctxr[:, 1, :], rstd[:, 11:12], None, ALU.mult).then_inc(ctx_ok, 1)
            dve.wait_ge(coef_ok, 2)
            turn(3, 0, lambda k: coefs[:, k:k + 1], lambda k: mods[:, k:k + 1])
            turn(4, S, lambda k: coefs[:, 16 + k:17 + k], lambda k: modc[:, k:k + 1])

            def spread_early(m):
                if m == 0:
                    for c in range(KC):
                        own.mark(dve.tensor_scalar(gdiag[:, P * c:P * c + P], ident, mods[:, 32 + c:33 + c], None, ALU.mult))
                    own.wait()
                    dve.sem_inc(gb_ok, 1)
                if m == 4:
                    dve.wait_ge(gb_mm, 1)
                    dve.tensor_copy(gb[:, 0:1536].rearrange("p (a b) -> p a b", a=3), ps[:, 5:8, :]).then_inc(gb_rd, 1)
                if m == 8:
                    dve.wait_ge(gb_mm, 2)
                    dve.tensor_copy(gb[:, 1536:D], X[1]).then_inc(gb_rd, 1)

            KG, QG = cols[:, R_KG:R_KG + 1], cols[:, R_QG:R_QG + 1]

            def attend_v(i, m):
                if m < 4:
                    a = i * 4 + (m - 4)
                    hh, qb = m // 2, m % 2
                    if m == 0:
                        dve.wait_ge(n_eh, i * 16)
                    dve.wait_ge(n_s, a + 1)
                    dve.wait_ge(n_tr, a + (AHEAD - 1))
                    v = pr[:, m % 2, :]
                    e0 = GRID * (2 - 2 * qb)
                    own.mark(dve.scalar_tensor_tensor(out=v[:, 0:S], in0=X[1][:, 0:S], scalar=NA_SCALE,
                                                      in1=eh[:, hh, e0:e0 + S], op0=ALU.mult, op1=ALU.add))
                    dve.tensor_scalar(v[:, S:2 * S], X[1][:, S:2 * S], NA_SCALE, None, ALU.mult).then_inc(n_t, 1)
                    dve.wait_ge(n_t, a + (1 + AHEAD))
                    own.done(dve.tensor_reduce(nst[:, m:m + 1], v, AXX, ALU.max))
                    dve.tensor_scalar(nst[:, 4 + m:5 + m], nst[:, m:m + 1], -1.0, None, ALU.mult).then_inc(n_nm, 1)
                    dve.wait_ge(n_p, a + 1)
                    own.done(dve.reciprocal(nst[:, 12 + m:13 + m], nst[:, 8 + m:9 + m]))
                    dve.tensor_scalar(v, v, nst[:, 12 + m:13 + m], None, ALU.mult).then_inc(n_pn, 1)
                if m in (3, 5):
                    hh = (m - 3) // 2
                    dve.wait_ge(n_o, i * 4 + (m - 5 + AHEAD))
                    dve.tensor_copy(oT[:, bass.ds(i * 2 + (hh - 2), 1), :], X[3][:, 0:S].unsqueeze(1)).then_inc(n_oc, 1)

            def norm(i, r):
                dve.wait_ge(n_rs, i * 6 + (2 * r + 2 + AHEAD))
                if r < 2:
                    dve.scalar_tensor_tensor(out=kT[:, r, :], in0=Gf[0][:, 512 * r:512 * r + 512], scalar=KG,
                                             in1=nrs[:, 512 * r:512 * r + 512], op0=ALU.mult, op1=ALU.mult)\
                        .then_inc(n_norm, 1)
                else:
                    dve.scalar_tensor_tensor(out=qT.rearrange("p a b -> p (a b)"), in0=X[0], scalar=QG,
                                             in1=nrs[:, 0:512], op0=ALU.mult, op1=ALU.mult).then_inc(n_norm, 1)

            def ada_tail(i, slot):
                ks = ([3 * slot + c for c in range(3)] if slot < 4 else [8 + slot] if slot < 8 else
                      [16 + 4 * (slot - 8) + c for c in range(4)])
                for kk in ks:
                    s, k = divmod(kk, 16)
                    q = kk // 4
                    if k % 4 == 0:
                        dve.wait_ge(ada_in[q % 2], i * 64 + (16 * 16 + 16 * (q // 2) + 16))
                    ins = ada_term(s, k, ada2[:, q % 2, k % 4, :], (acc2, acc3[:, :])[s], 0, k == 0)
                    if k % 4 == 3:
                        ins.then_inc(ada_done, 1)
                        dve.wait_ge(ada_done, i * 8 + (64 + q + 1))
                    else:
                        own.done(ins)

            def ada_out(i, s):
                dve.wait_ge(ada_mm, i * 2 + (16 + s + 1))
                dve.tensor_copy(mods[:, bass.ds(i * 6 + (48 + 3 * s), 3)], X[1][:, 4 * s:4 * s + 3]).then_inc(ada_col, 1)

            def na_turn(i, first):
                u0 = i * 12 + U_NA
                for m in range(12):
                    if m == 0 and not first:
                        ada_out(i - 1, 1)
                    if not (first and m == 0):
                        split(u0, m + 3)
                    if first:
                        spread_early(m)
                    else:
                        attend_v(i, m)
                    ada_tail(i, m)
                    if m in (6, 7):
                        norm(i, m - 6)
                    if m == 10:
                        norm(i, 2)
                        ada_out(i, 0)

            na_turn(0, True)
            with own.loop(1, 8, NA_OWN) as i:
                na_turn(i, False)
            ada_out(7, 1)
            split(U_WO, 3)
            dve.wait_ge(ada_col, 32)
            own.done(dve.tensor_tensor(mods[:, 48:96], mods[:, 48:96], cols[:, C_ADAB + 48:C_ADAB + 96], ALU.add))
            dve.scalar_tensor_tensor(out=coefs[:, 32:48], in0=mods[:, 64:80], scalar=1.0, in1=cols[:, 48:64],
                                     op0=ALU.add, op1=ALU.mult).then_inc(coef_ok, 1)
            for m in range(6):
                attend_v(8, m)
                if m < 4:
                    for c in range(4 * m, 4 * m + 4):
                        own.mark(dve.tensor_scalar(gdiag2[:, P * c:P * c + P], ident, mods[:, 80 + c:81 + c], None, ALU.mult))
                    own.wait()
                    dve.sem_inc(gb_ok, 1)
                if m >= 2:
                    dve.wait_ge(gb_mm, m + 1)
                    dve.tensor_copy(gb2[:, 512 * (m - 2):512 * (m - 1)], X[0]).then_inc(gb_rd, 1)
            for k in range(KC):
                dve.wait_ge(a_hi, OT_AT + k + 1)
                dve.tensor_tensor(alo[:, k, S:2 * S], oT[:, k, :], f(ahi[:, k, S:2 * S]), ALU.subtract).then_inc(a_lo, 1)

            def add_gated(n, q, used, done, count, gate):
                dve.wait_ge(unit_used, used)
                gg = gate[:, bass.ds(n * 512, 512)].unsqueeze(1).to_broadcast([P, RT, 512])
                v = x[:, :, bass.ds(n * 512, 512)]
                tt = tmp.rearrange("p (r n) -> p r n", r=RT)
                dve.tensor_tensor(tt, G[q], gg, ALU.mult).then_inc(done, 1)
                dve.wait_ge(done, count)
                own.done(dve.tensor_tensor(v, v, tt, ALU.add))

            with own.loop(0, 2, 2) as i:
                for j in range(4, 20):
                    split(i * 16 + U_WO, j)
                    if j % 8 == 3:
                        q = j // 8 - 1
                        add_gated(i * 2 + q, q, i * 16 + (U_WO + 8 * q + 8), drained[q], i + (D_NA[q] + 1), gb)
            dve.sem_inc(x_done, 1)

            ss_rows(4, x[:, 1, :], xs[:, 1, :])
            scale_rows(4, xs[:, 1, :], x[:, 1, :])
            dve.wait_ge(coef_ok, 3)
            turn(5, 0, lambda k: coefs[:, 32 + k:33 + k], lambda k: mods[:, 48 + k:49 + k])

            def conv_v(pair, q, nc_, done):
                dst = (held, cvt)[q]
                dve.wait_ge(f_a, pair * 3 + (1 + 2 * q))
                for tap in (0, 2):
                    for c in range(nc_):
                        z = Gf[q][:, S * c:S * c + S]
                        v = dst[:, S * c:S * c + S]
                        w = cols[:, bass.ds(pair * 4 + (C_CONV + 2 * FC * (1 + tap) + q * FC + c), 1)]
                        a, b = (v[:, 1:S], z[:, 0:S - 1]) if tap == 0 else (v[:, 0:S - 1], z[:, 1:S])
                        ins = dve.scalar_tensor_tensor(out=a, in0=b, scalar=w, in1=a, op0=ALU.mult, op1=ALU.add)
                    if tap == 0:
                        own.done(ins)
                ins.then_inc(f_v, 1)
                dve.wait_ge(f_v, pair * 2 + (q + 1))
                dve.sem_inc(done, 1)

            def conv_pair(pair, u0, nc_):
                for j in range(4, 20):
                    split(u0, j)
                    if j == 11:
                        conv_v(pair, 0, nc_, drained[0])
                    if j == 19:
                        conv_v(pair, 1, nc_, drained[1])

            with own.loop(0, 2, 12) as g:
                with own.loop(0, 4, 2) as n:
                    conv_pair(g * 4 + n, g * 96 + n * 16 + U_FFN, 4)
                with own.loop(0, 2, 2) as n:
                    for j in range(4, 20):
                        split(g * 96 + n * 16 + (U_FFN + 64), j)
                        if j % 8 == 3:
                            q = j // 8 - 1
                            add_gated(n * 2 + q, q, g * 96 + n * 16 + (U_FFN + 64 + 8 * q + 8), drained[q],
                                      g * 6 + n + (D_WO[q] + 4 + 1), gb2)
            with own.loop(0, 2, 2) as n:
                conv_pair(n + 8, n * 16 + U_LAST, 4)
            conv_pair(10, U_LAST + 32, 3)
            for j in range(4, 24):
                split(U_DOWN, j)
                if j % 6 == 3:
                    n = j // 6 - 1
                    add_gated(n, n % 2, U_DOWN + 6 * n + 6, drained[n % 2], D_F1[n % 2] + 3 + n // 2 + 1, gb2)
                    dve.sem_inc(x_done, 1)
            add_gated(3, 1, U_DOWN + 24, drained[1], D_F1[1] + 3 + 2, gb2)
            dve.sem_inc(x_done, 1)

        @block.tensor
        def _(pe):
            pe.sem_inc(n_tr, AHEAD)
            pe.sem_inc(n_o, AHEAD)

            def kn(v, j):
                return v[:, j % RING, :].rearrange("p (k n) -> p k n", n=512)

            def terms(w_hi, w_lo, a_hi_, a_lo_, weights_left):
                for w, a in ((w_hi, a_hi_), (w_hi, a_lo_), (w_lo, a_hi_)):
                    yield (w, a) if weights_left else (a, w)

            def columns(o, j, kk, c0, k, t0, tn, start, last):
                n = o.shape[0]
                wh, wl = kn(whi, j)[:, kk, c0:c0 + n], kn(wlo, j)[:, kk, c0:c0 + n]
                for i, (a, b) in enumerate(terms(wh, wl, ahi[:, k, t0:t0 + tn], alo[:, k, t0:t0 + tn], True)):
                    ins = pe.matmul(o, a, b, start=start and i == 0, stop=last and i == 2, skip_group_check=True)
                return ins

            def rows(o, j, kk, c0, k, t0, start, last):
                n = o.shape[1]
                wh, wl = kn(whi, j)[:, kk, c0:c0 + n], kn(wlo, j)[:, kk, c0:c0 + n]
                for i, (a, b) in enumerate(terms(wh, wl, ahi[:, k, t0:t0 + P], alo[:, k, t0:t0 + P], False)):
                    ins = pe.matmul(o, a, b, start=start and i == 0, stop=last and i == 2, skip_group_check=True)
                return ins

            def unit_columns(u0, j, q, nc_, k0, t0, kc=KC, kper=2, width=P):
                pe.wait_ge(lo_done, u0 + (j + 1))
                for kk in range(kper):
                    k = k0 + kk
                    for c in range(nc_):
                        o = Gf[q][0:width, S * c:S * c + S]
                        ins = columns(o, j, kk, width * c, k, t0, S, k == 0 and c % 2 == 0, k == kc - 1)
                ins.then_inc(unit_used, 1)

            def unit_rows(u0, j, q, k0, t0, kc=KC, kper=2, w=512, final=None):
                final = kc - 1 if final is None else final
                pe.wait_ge(lo_done, u0 + (j + 1))
                for kk in range(kper):
                    k = k0 + kk
                    for r in range(RT):
                        ins = rows(G[q][:, r, 0:w], j, kk, 0, k, t0 + P * r, k == 0, k == final)
                ins.then_inc(unit_used, 1)

            def turn_rows(e, src, ready, order=range(8), at_=range(8)):
                for w in ready:
                    pe.wait_ge(*w)
                for at in at_:
                    if at >= 4 or e == 4:
                        pe.wait_ge(a_lo, TURN_AT[e] + 2 * (at - 4) + 2)
                    for c in range(2):
                        for r in range(RT):
                            k = 2 * order[at] + c
                            o = X[at % 4][:, c * S + P * r:c * S + P * r + P]
                            ins = pe.transpose(o, src[:, r, P * k:P * k + P], ident)
                    ins.then_inc(turned, 1)

            pe.wait_ge(cst_in, 16)
            pe.wait_ge(rows_in, 16 * NROWS_DMA)
            pe.wait_ge(pool_step, 1)
            pe.transpose(X01[:, 0:114], colrow[0:114, 0, :], ident[0:114, 0:114])
            pe.transpose(X01[:, C_ADAB:C_ADAB + 96], colrow[0:96, 1, :], ident[0:96, 0:96])
            pe.transpose(X01[:, C_GATEB:C_GATEB + 4], colrow[0:4, 2, :], ident[0:4, 0:4])
            for i in range(4):
                ins = pe.transpose(X01[:, 512 + 2 * FC * i:512 + 2 * FC * (i + 1)], colrow[0:2 * FC, 3 + i, :],
                                   ident[0:2 * FC, 0:2 * FC])
            ins.then_inc(colT, 1)
            pe.wait_ge(small_in, 48)
            pe.matmul(X[2][0:12, 0:S], relb[0:32, :], C("bucket")[0:32, :], start=True, stop=True).then_inc(ft_mm, 1)
            turn_rows(0, xs, [(xs_ok, 2), (cols_ok, 2), (ft_ok, 1)])

            def swa(part, s):
                n, c = divmod(s, 6)
                w = P if n == 0 else S
                if part == "swa_a":
                    if s == 0:
                        pe.wait_ge(drained[0], 6)
                        pe.wait_ge(drained[1], 1)
                        pe.wait_ge(a_lo, KC)
                    else:
                        pe.wait_ge(w_t, s)
                    for a in range(2):
                        p0 = HD * a
                        ins = pe.matmul(X[a][:, 0:w], sq_[p0:p0 + HD, c, P * n:P * n + P],
                                        skd[p0:p0 + HD, (2 * c + a) // 3, 0:w], start=True, stop=True)
                    ins.then_inc(w_s, 1)
                elif part == "swa_b":
                    pe.wait_ge(w_p, 3 * s + 3)
                    if s:
                        pe.wait_ge(w_pt, s)
                    for a in range(2):
                        for b in range(w // P):
                            ins = pe.transpose(X[2][:, a * w + P * b:a * w + P * b + P],
                                               swt[:, s % 2, a, P * b:P * b + P], ident)
                    ins.then_inc(w_tr, 1)
                else:
                    pe.wait_ge(w_pt, s + 1)
                    if s:
                        pe.wait_ge(w_out_ok, s)
                    for a in range(2):
                        kv = (2 * c + a) // 3
                        for b in range(w // P):
                            ins = pe.matmul(X[3][:, HD * a:HD * a + HD], swp[:, s % 2, a * w + P * b:a * w + P * b + P],
                                            sv[:, b, HD * kv:HD * kv + HD], start=(b == 0), stop=(b == w // P - 1))
                    ins.then_inc(w_o, 1)

            def gla_p(n):
                gd = gla
                if n == 0:
                    pe.wait_ge(in_ready, 1)
                    pe.wait_ge(sbs["p"], 4)
                    for h in range(4):
                        ins = pe.matmul(X01[0:DK, S * h:S * h + S], gw[0:LR, DK * h:DK * h + DK], lrT[0:LR, :],
                                        start=(h % 2 == 0), stop=True, skip_group_check=True)
                    ins.then_inc(gd["gate"], 1)
                if n == 1:
                    pe.wait_ge(gd["ki"], 1)
                    pe.wait_ge(sbs["out"], 8)
                    for r in range(RT):
                        for h in range(4):
                            ins = pe.transpose(X[2 + r][:, DK * h:DK * h + DK], g2[0:DK, h, P * r:P * r + P], ident[0:DK, 0:DK])
                        ins.then_inc(gd["turn"], 1)
                    for r in range(RT):
                        for h in range(4):
                            ins = pe.matmul(X[r][:, P * h:P * h + P], g3[0:DK, h, P * r:P * r + P],
                                            gq[0:DK, h, P * r:P * r + P], start=True, stop=True)
                        ins.then_inc(gd["sc"], 1)
                if n in (2, 3):
                    r = n - 2
                    if r == 0:
                        pe.wait_ge(drained[0], 9)
                        pe.wait_ge(drained[1], 5)
                        pe.wait_ge(gd["scm"], 2)
                    else:
                        pe.wait_ge(gd["ic"], 1)
                    for h in range(4):
                        ins = pe.matmul(ps[:, 4 + h // 2, DV * (h % 2):DV * (h % 2) + DV], scT[:, r, h, :],
                                        bv[:, r, DV * h:DV * h + DV], start=True, stop=True)
                    ins.then_inc(gd["intra"], 1)
                if n in (5, 6, 7):
                    c = n - 4
                    p0 = CH * (c % 2)
                    pe.wait_ge(gd["st"], c)
                    if c == 1:
                        pe.wait_ge(gd["ic"], 2)
                    else:
                        pe.wait_ge(gd["add"], c - 1)
                    for h in range(4):
                        ins = pe.matmul(ps[p0:p0 + CH, 4 + h // 2, DV * (h % 2):DV * (h % 2) + DV],
                                        gq[0:DK, h, CH * c:CH * c + CH], state[0:DK, DV * h:DV * h + DV],
                                        start=True, stop=True)
                    ins.then_inc(gd["inter"], 1)
                if n in (4, 5, 6):
                    c = n - 4
                    p0 = CH * (c % 2)
                    pe.wait_ge(gd["kend"], 2)
                    for h in range(4):
                        ins = pe.matmul(ps[0:DK, 6 + h // 2, DV * (h % 2):DV * (h % 2) + DV],
                                        kend[p0:p0 + CH, c // 2, DK * h:DK * h + DK], bv[p0:p0 + CH, c // 2, DV * h:DV * h + DV],
                                        start=True, stop=True)
                    ins.then_inc(gd["ds"], 1)

            def sb_p(part, c):
                if part == "sb_a":
                    if c == 0:
                        pe.wait_ge(drained[0], 7)
                        pe.wait_ge(drained[1], 3)
                        pe.wait_ge(w_out_ok, 12)
                    else:
                        pe.wait_ge(sbs["p"], c)
                    for a in range(2):
                        p0 = HD * a
                        pe.matmul(X[a][:, 0:S], ck[p0:p0 + HD, c, 0:P], cq[p0:p0 + HD, c, :], start=True, stop=True)
                        ins = pe.matmul(X[a][:, S:384], ck[p0:p0 + HD, c, P:S], cq[p0:p0 + HD, c, P:S], start=True, stop=True)
                    ins.then_inc(sbs["z"], 1)
                elif part == "sb_b":
                    pe.wait_ge(sbs["p"], c + 1)
                    if c:
                        pe.wait_ge(sbs["out"], 2 * c)
                    for a in range(2):
                        pe.matmul(X[2 + a][:, 0:384], C("tri"), sb_sp[:, a, :], start=True, stop=False, skip_group_check=True)
                        ins = pe.matmul(X[2 + a][:, P:S], ones, sb_sp[:, a, S:384], start=False, stop=True, skip_group_check=True)
                    ins.then_inc(sbs["c"], 1)
                else:
                    pe.wait_ge(sbs["w"], c + 1)
                    for a in range(2):
                        h = 2 * c + a
                        v0, v1 = (cv[:, 2 * r + h // 4, HD * (h % 4):HD * (h % 4) + HD] for r in range(RT))
                        pe.matmul(X[2][:, 384 + HD * a:448 + HD * a], sb_w[:, a, 0:P], v0, start=True, stop=True)
                        o = X[3][:, 384 + HD * a:448 + HD * a]
                        pe.matmul(o, sb_w[:, a, P:S], v0, start=True, stop=False)
                        ins = pe.matmul(o, sb_w[:, a, S:384], v1, start=False, stop=True)
                    ins.then_inc(sbs["o"], 1)

            def finish_p(part, n):
                if part == "turn":
                    at_ = (range(EARLY), range(EARLY, 8))[n]
                    turn_rows(1, x, [(mix_v, (5, 7)[n]), (gla["add"], 3)], order=ORDER_OUT, at_=at_)

            before = {0: 0, 1: 0}
            for m in range(8 * len(PANELS_IN)):
                n, j = divmod(m, 8)
                name, _, w = PANELS_IN[n]
                q = n % 2
                u0 = 8 * n
                if j == 0:
                    if n >= 2:
                        pe.wait_ge(drained[q], before[q])
                    before[q] += 5 if name == "KV" else 1
                if n == 0:
                    pe.wait_ge(a_lo, 2 * j + 2)
                if name in ("Q0", "Q1"):
                    unit_columns(u0, j, q, 3, 2 * j, 0)
                elif name == "KV":
                    pe.wait_ge(lo_done, u0 + j + 1)
                    for kk in range(2):
                        k = 2 * j + kk
                        for c in range(2):
                            columns(Gf[q][:, S * c:S * c + S], j, kk, P * c, k, 0, S, k == 0 and c == 0, k == KC - 1)
                        for r in range(RT):
                            ins = rows(G[q][:, 1, S * r:S * r + S], j, kk, S, k, P * r, k == 0 and r == 0, k == KC - 1)
                    ins.then_inc(unit_used, 1)
                elif name in ("GQ", "GK"):
                    unit_columns(u0, j, q, 4, 2 * j, 0, width=DK)
                elif name == "BV0":
                    pe.wait_ge(lo_done, u0 + j + 1)
                    for kk in range(2):
                        k = 2 * j + kk
                        for r in range(RT):
                            rows(G[q][:, r, 0:384], j, kk, LR, k, P * r, k == 0, k == KC - 1)
                            ins = columns(G[q][:, r, 384:512], j, kk, 0, k, P * r, P, False, k == KC - 1)
                    ins.then_inc(unit_used, 1)
                elif name in ("CQ", "CK"):
                    unit_columns(u0, j, q, 4, 2 * j, 0)
                else:
                    unit_rows(u0, j, q, 2 * j, 0, w=w)
                for part, s in PLAN.get(m, []):
                    if part == "gla":
                        gla_p(s)
                    else:
                        {"swa": swa, "sb_": sb_p}.get(part[:3], finish_p)(part, s)

            for n in range(4):
                q = n % 2
                pe.wait_ge(drained[q], (D0_IN, D1_IN)[q] + n // 2)
                for j in range(8):
                    if n == 0 and j == RING:
                        finish_p("turn", 1)
                    if n == 0:
                        pe.wait_ge(a_lo, TURN_AT[1] + 2 * j + 2)
                    unit_rows(U_OUT, 8 * n + j, q, 2 * ORDER_OUT[j], S, final=2 * ORDER_OUT[-1] + 1)

            turn_rows(2, xs, [(xs_ok, 4)])
            pe.wait_ge(a_lo, TURN_AT[3])

            def ada_sums(lat, cx, o, ready):
                for w in ready:
                    pe.wait_ge(*w)
                for c in range(3):
                    ins = pe.matmul(o[:, c:c + 1], lat[:, P * c:P * c + P], ones[:, 0:1], start=True, stop=True)
                if cx is not None:
                    for c in range(3):
                        ins = pe.matmul(o[:, 4 + c:5 + c], cx[:, P * c:P * c + P], ones[:, 0:1], start=True, stop=True)
                ins.then_inc(ada_mm, 1)

            with pe.Fori(0, 4) as g:
                with pe.Fori(0, 2) as i:
                    for q in range(2):
                        pe.wait_ge(drained[q], g * 4 + i + D_OUT[q])
                        for j in range(8):
                            if q == 1 and j == 7:
                                ada_sums(accL, accC, X[0], [(ada_done, g * 16 + i * 4 + 4), (ada_c, g * 4 + i + 1)])
                            unit_columns(g * 64 + i * 16 + U_MLP, 8 * q + j, q, 4, 2 * j, 0)
                with pe.Fori(0, 2) as i:
                    for q in range(2):
                        pe.wait_ge(drained[q], g * 4 + i + (D_OUT[q] + 2))
                        for j in range(8):
                            if q == 0 and j == 0:
                                pe.wait_ge(hid_v, g * 4 + (3 + AHEAD))
                            if q == 0 and j == 6:
                                pe.wait_ge(hid_v, g * 4 + (4 + AHEAD))
                            if q == 1 and j == 7:
                                ada_sums(accL, accC, X[0], [(ada_done, g * 16 + i * 4 + 12), (ada_c, g * 4 + i + 3)])
                            unit_rows(g * 64 + i * 16 + (U_MLP + 32), 8 * q + j, q, 2 * j, S)

            turn_rows(3, xs, [(xs_ok, 6), (ada_col, 16)])
            turn_rows(4, ctxr, [(ctx_ok, 2)])

            def attend_p(i, m):
                if m < 4:
                    a = i * 4 + (m - 4)
                    hh, qb = m // 2, m % 2
                    if m == 0:
                        pe.wait_ge(n_norm, i * 3 + AHEAD)
                    pe.wait_ge(n_t, a + AHEAD)
                    if m == 0:
                        pe.wait_ge(ada_col, i * 2 + 16)
                    pe.matmul(X[1], qT[:, hh, P * qb:P * qb + P], kT[:, hh, :], start=True, stop=True).then_inc(n_s, 1)
                if 1 <= m <= 4:
                    T = m - 1
                    a = i * 4 + (T - 4)
                    pe.wait_ge(n_pn, a + 1)
                    pe.wait_ge(n_pt, a + AHEAD)
                    if m == 1:
                        pe.wait_ge(n_rs, i * 6 + AHEAD)
                    for k in range(4):
                        ins = pe.transpose(X[2][:, P * k:P * k + P], pr[:, T % 2, P * k:P * k + P], ident)
                    ins.then_inc(n_tr, 1)
                if 2 <= m <= 5:
                    T = m - 2
                    hh, qb = T // 2, T % 2
                    a = i * 4 + (T - 4)
                    pe.wait_ge(n_pt, a + (1 + AHEAD))
                    if T == 0:
                        pe.wait_ge(drained[1], i + D_MLP[1])
                    if qb == 0:
                        pe.wait_ge(n_oc, i * 2 + (hh - 2 + AHEAD))
                    for k in range(4):
                        ins = pe.matmul(X[3][:, P * qb:P * qb + P], vv[:, k, NHD * hh:NHD * hh + NHD], pT[:, T % 2, P * k:P * k + P],
                                        start=(k == 0), stop=(k == 3))
                    ins.then_inc(n_o, 1)

            def norm_sums(i, r):
                pe.wait_ge(n_sq, i * 2 + (1 if r < 2 else 2))
                pe.wait_ge(n_pt, i * 4 + AHEAD)
                pe.wait_ge(n_rs, i * 6 + (2 * r + AHEAD))
                pe.matmul(X[2], ones, nsq[:, 512 * (r % 2):512 * (r % 2) + 512], start=True, stop=True).then_inc(n_nsum, 1)

            def na_turn(i, first):
                u0 = i * 12 + U_NA
                for m in range(12):
                    part = m // 4
                    j = m % 4
                    wh, wl = (v[:, m % RING, :].rearrange("p (k n) -> p k n", n=256) for v in (whi, wlo))
                    if m == 0 and first:
                        pe.wait_ge(drained[0], D_MLP[0])
                    elif m == 0:
                        pe.wait_ge(n_norm, i * 3 + (AHEAD - 1))
                    if m == 4:
                        pe.wait_ge(n_norm, i * 3 + AHEAD)
                    if m == 8:
                        pe.wait_ge(drained[1], i + D_MLP[1])
                    pe.wait_ge(lo_done, u0 + (m + 1))
                    for kk in range(4):
                        k = 4 * j + kk
                        st, sp_ = k == 0, k == KC - 1
                        if part == 0:
                            for c in range(2):
                                cs = slice(P * c, P * c + P)
                                for y, (a, b) in enumerate(terms(wh[:, kk, cs], wl[:, kk, cs], ahi[:, k, :], alo[:, k, :], True)):
                                    ins = pe.matmul(G[0][:, c, :], a, b, start=st and y == 0, stop=sp_ and y == 2)
                        elif part == 1:
                            for c in range(2):
                                cs = slice(P * c, P * c + P)
                                for y, (a, b) in enumerate(terms(wh[:, kk, cs], wl[:, kk, cs], ahi[:, k, 0:S], alo[:, k, 0:S], True)):
                                    ins = pe.matmul(X[0][:, S * c:S * c + S], a, b, start=st and y == 0 and c == 0,
                                                    stop=sp_ and y == 2, skip_group_check=True)
                        else:
                            for r in range(4):
                                rs = slice(P * r, P * r + P)
                                for y, (a, b) in enumerate(terms(wh[:, kk, :], wl[:, kk, :], ahi[:, k, rs], alo[:, k, rs], False)):
                                    ins = pe.matmul(Gf[1][:, S * r:S * r + S], a, b, start=st and y == 0 and r % 2 == 0,
                                                    stop=sp_ and y == 2, skip_group_check=True)
                    ins.then_inc(unit_used, 1)
                    if first and m == 0:
                        pe.wait_ge(gb_ok, 1)
                        pe.wait_ge(a_lo, OT_AT)
                        for b in range(3):
                            ins = pe.matmul(X[1 + b], ones, gdiag[:, 512 * b:512 * b + 512], start=True, stop=True)
                        ins.then_inc(gb_mm, 1)
                    if first and m == 5:
                        pe.wait_ge(gb_rd, 1)
                        pe.matmul(X[1], ones, gdiag[:, 1536:D], start=True, stop=True).then_inc(gb_mm, 1)
                    if not first:
                        attend_p(i, m)
                    if m in (6, 7):
                        norm_sums(i, m - 6)
                    if m == 9:
                        if first:
                            pe.wait_ge(gb_rd, 2)
                        ada_sums(acc2, None, X[1], [(ada_done, i * 8 + (64 + 4))])
                    if m == 10:
                        norm_sums(i, 2)
                    if m == 11:
                        ada_sums(acc3, None, X[1][:, 4:8], [(ada_done, i * 8 + (64 + 8))])

            na_turn(0, True)
            with pe.Fori(1, 8) as i:
                na_turn(i, False)
            for m in range(6):
                attend_p(8, m)
                if 1 <= m <= 4:
                    pe.wait_ge(gb_ok, m + 1)
                    pe.wait_ge(gb_rd, m + 1)
                    pe.matmul(X[0], ones, gdiag2[:, 512 * (m - 1):512 * m], start=True, stop=True).then_inc(gb_mm, 1)

            with pe.Fori(0, 2) as i:
                for q in range(2):
                    pe.wait_ge(drained[q], i + D_NA[q])
                    for j in range(8):
                        if q == 0:
                            pe.wait_ge(a_lo, OT_AT + 2 * j + 2)
                        unit_rows(i * 16 + U_WO, 8 * q + j, q, 2 * j, S)

            turn_rows(5, xs, [(xs_ok, 8), (gb_rd, 6)])
            pe.wait_ge(a_lo, 7 * KC)

            def pair_units(u0, nc_, count):
                for q in range(2):
                    pe.wait_ge(drained[q], count(q))
                    for j in range(8):
                        unit_columns(u0, 8 * q + j, q, nc_, 2 * j, 0)

            with pe.Fori(0, 2) as g:
                with pe.Fori(0, 4) as n:
                    pair_units(g * 96 + n * 16 + U_FFN, 4, lambda q: g * 6 + n + D_WO[q])
                with pe.Fori(0, 2) as n:
                    for q in range(2):
                        pe.wait_ge(drained[q], g * 6 + n + (D_WO[q] + 4))
                        for j in range(8):
                            if q == 0 and j == 0:
                                pe.wait_ge(f_h, g * 12 + (9 + AHEAD))
                            if q == 0 and j == 6:
                                pe.wait_ge(f_h, g * 12 + (12 + AHEAD))
                            unit_rows(g * 96 + n * 16 + (U_FFN + 64), 8 * q + j, q, 2 * j, S)
            with pe.Fori(0, 2) as n:
                pair_units(n * 16 + U_LAST, 4, lambda q: n + D_F1[q])
            pair_units(U_LAST + 32, 3, lambda q: 2 + D_F1[q])
            for n in range(4):
                pe.wait_ge(drained[n % 2], D_F1[n % 2] + 3 + n // 2)
                for j in range(6):
                    if n == 0 and j == 0:
                        pe.wait_ge(f_h, 30 + AHEAD)
                    if n == 0 and j == 4:
                        pe.wait_ge(f_h, 33 + AHEAD)
                    unit_rows(U_DOWN, 6 * n + j, n % 2, 2 * j, S, kc=11, kper=1 if j == 5 else 2)


_INS = ["x", "norm_mix", "w_in", "swa_sinks", "rel_bias", "gla_gate_w", "gla_gate_b", "gla_norm", "swa_out_norm",
        "sb_out_norm", "w_out", "norm_mlp", "w_mlp_in", "w_mlp_out", "norm_final", "c_2", "ctx_2", "c_ctx_2",
        "norm_mix_g_2", "norm_ffn_g_2", "w_ada_2", "b_ada_2", "na_w_qkv_2", "na_q_g_2", "na_k_g_2", "na_rpb_2",
        "na_w_o_2", "ffn_w_up_2", "ffn_conv_w_2", "ffn_conv_b_2", "ffn_w_down_2"]


def kernel(**inputs):
    import concourse.bacc as bacc
    from concourse.bass_utils import run_bass_kernel_spmd

    nc = bacc.Bacc("TRN2", target_bir_lowering=False, num_devices=1)
    arrays, tensors = {}, {}
    for name in _INS + ["consts"]:
        a = shape_constants() if name == "consts" else np.ascontiguousarray(inputs[name])
        arrays[f"in_{name}"] = a
        tensors[name] = nc.dram_tensor(f"in_{name}", a.shape, mybir.dt.from_np(a.dtype), kind="ExternalInput").ap()
    out = nc.dram_tensor("out_x", (1, S, D), F32, kind="ExternalOutput").ap()
    program(nc, tensors, out)
    return run_bass_kernel_spmd(nc, [arrays], core_ids=[0]).results[0]["out_x"]
```
